# Optimizing a Trainium2 kernel written in Bass

```python
import math
import jax
import jax.numpy as jnp
from jax import lax
import numpy as np
import jax, jax.numpy as jnp

D_MODEL = 1024
BATCH = 1
SEQ = 512
DEPTH = 1

HEAD_DIM = 64
SSD_HEADS = 16
SSD_GROUPS = 2
SSD_STATE = 128
SSD_CONV = 4
SSD_CHUNK = 128
SSD_WIDTH = SSD_HEADS * HEAD_DIM
SSD_BC_WIDTH = SSD_GROUPS * SSD_STATE
SSD_XBC_WIDTH = SSD_WIDTH + 2 * SSD_BC_WIDTH
FOX_HEADS = 16
FOX_WIDTH = FOX_HEADS * HEAD_DIM
Q_BLOCK = 128
MIX_WIDTH = SSD_WIDTH + FOX_WIDTH
D_FF = 2816
FFN_CONV = 3
NORM_EPS = 1e-6
Z_END = SSD_WIDTH
XBC_END = Z_END + SSD_XBC_WIDTH
DT_END = XBC_END + SSD_HEADS
Q_END = DT_END + FOX_WIDTH
K_END = Q_END + FOX_WIDTH
V_END = K_END + FOX_WIDTH
IN_COLS = V_END + FOX_HEADS


def rms_norm(x, w):
    xf = x.astype(jnp.float32)
    y = xf * lax.rsqrt(jnp.mean(xf * xf, axis=-1, keepdims=True) + NORM_EPS)
    return (y * w.astype(jnp.float32)).astype(x.dtype)

def causal_depthwise_conv(x, w, b):
    k = w.shape[0]
    y = lax.conv_general_dilated(
        x, w[:, None, :].astype(x.dtype), window_strides=(1,), padding=[(k - 1, 0)],
        dimension_numbers=('NWC', 'WIO', 'NWC'), feature_group_count=x.shape[-1])
    return y + b.astype(x.dtype)

def ssd_mixer(xbc_raw, z, dt_raw, conv_w, conv_b, dt_bias, a_log, d_skip, norm_w):
    b, s, _ = xbc_raw.shape
    nc = s // SSD_CHUNK
    e = SSD_HEADS // SSD_GROUPS
    xbc = jax.nn.silu(causal_depthwise_conv(xbc_raw, conv_w, conv_b))
    xs, bm, cm = jnp.split(xbc, [SSD_WIDTH, SSD_WIDTH + SSD_BC_WIDTH], axis=-1)
    x6 = xs.reshape(b, nc, SSD_CHUNK, SSD_GROUPS, e, HEAD_DIM)
    bm = bm.reshape(b, nc, SSD_CHUNK, SSD_GROUPS, SSD_STATE)
    cm = cm.reshape(b, nc, SSD_CHUNK, SSD_GROUPS, SSD_STATE)
    dt = jax.nn.softplus(dt_raw.astype(jnp.float32) + dt_bias.astype(jnp.float32))
    a = -jnp.exp(a_log.astype(jnp.float32))
    dt5 = dt.reshape(b, nc, SSD_CHUNK, SSD_GROUPS, e)
    a_cs = jnp.cumsum(dt5 * a.reshape(SSD_GROUPS, e), axis=2)
    xdt = x6 * dt5[..., None]
    at = jnp.moveaxis(a_cs, 2, -1)
    seg = at[..., :, None] - at[..., None, :]
    tri = jnp.tril(jnp.ones((SSD_CHUNK, SSD_CHUNK), dtype=bool))
    decay = jnp.exp(jnp.where(tri, seg, -jnp.inf))
    cb = jnp.einsum('bclgn,bcsgn->bcgls', cm, bm)
    scores = cb[:, :, :, None] * decay
    y_diag = jnp.einsum('bcgels,bcsgep->bclgep', scores, xdt)
    decay_to_end = jnp.exp(a_cs[:, :, -1:] - a_cs)
    chunk_states = jnp.einsum('bclgn,bclgep->bcgepn', bm, xdt * decay_to_end[..., None])
    chunk_decay = jnp.exp(a_cs[:, :, -1])

    def step(h, inp):
        dec, st = inp
        return h * dec[..., None, None] + st, h

    h0 = jnp.zeros((b, SSD_GROUPS, e, HEAD_DIM, SSD_STATE), jnp.float32)
    _, states_in = lax.scan(step, h0, (jnp.moveaxis(chunk_decay, 1, 0), jnp.moveaxis(chunk_states, 1, 0)))
    states_in = jnp.moveaxis(states_in, 0, 1)
    y_off = jnp.einsum('bclgn,bcgepn->bclgep', cm, states_in) * jnp.exp(a_cs)[..., None]
    y = y_diag + y_off + d_skip.astype(jnp.float32).reshape(SSD_GROUPS, e)[:, :, None] * x6
    y = y.reshape(b, s, SSD_WIDTH)
    yg = (y * jax.nn.silu(z.astype(jnp.float32))).reshape(b, s, SSD_GROUPS, SSD_WIDTH // SSD_GROUPS)
    yg = yg * lax.rsqrt(jnp.mean(yg * yg, axis=-1, keepdims=True) + NORM_EPS)
    return (yg.reshape(b, s, SSD_WIDTH) * norm_w.astype(jnp.float32)).astype(xbc_raw.dtype)

def fox_mixer(q, k, v, f_raw, f_bias, q_norm_w, k_norm_w):
    b, s, _ = q.shape

    def heads(t):
        return t.reshape(b, s, FOX_HEADS, HEAD_DIM).transpose(0, 2, 1, 3)

    qh = rms_norm(heads(q), q_norm_w)
    kh = rms_norm(heads(k), k_norm_w)
    vh = heads(v)
    log_f = jax.nn.log_sigmoid(f_raw.astype(jnp.float32) + f_bias.astype(jnp.float32))
    cum = jnp.cumsum(log_f, axis=1).transpose(0, 2, 1)
    scale = HEAD_DIM ** -0.5
    outs = []
    for start in range(0, s, Q_BLOCK):
        end = start + Q_BLOCK
        logits = jnp.einsum('bhqd,bhkd->bhqk', qh[:, :, start:end], kh[:, :, :end],
                            preferred_element_type=jnp.float32) * scale
        logits = logits + cum[:, :, start:end, None] - cum[:, :, None, :end]
        causal = (start + jnp.arange(Q_BLOCK))[:, None] >= jnp.arange(end)[None, :]
        p = jax.nn.softmax(jnp.where(causal, logits, -jnp.inf), axis=-1)
        outs.append(jnp.einsum('bhqk,bhkd->bhqd', p.astype(vh.dtype), vh[:, :, :end]))
    o = jnp.concatenate(outs, axis=2)
    return o.transpose(0, 2, 1, 3).reshape(b, s, FOX_WIDTH)

def conv_gated_mlp(x, w_up, conv_w, conv_b, w_down):
    h = x @ w_up.astype(x.dtype)
    h = causal_depthwise_conv(h, conv_w, conv_b)
    gate, val = jnp.split(h, 2, axis=-1)
    return (jax.nn.silu(gate) * val) @ w_down.astype(x.dtype)

def first_inputs(seed: int = 0) -> dict:
    key = jax.random.key(seed)
    ks = jax.random.split(key, 20)
    L = DEPTH

    def nrm(k, shape, scale):
        return jax.random.normal(k, shape, jnp.float32) * scale

    def gain(k, n):
        return 1.0 + 0.02 * jax.random.normal(k, (L, n), jnp.float32)

    dt = jnp.exp(jax.random.uniform(ks[5], (L, SSD_HEADS), jnp.float32, math.log(1e-3), math.log(1e-1)))
    dt_bias = dt + jnp.log(-jnp.expm1(-dt))
    return {
        'x': nrm(ks[0], (BATCH, SEQ, D_MODEL), 1.0),
        'norm_mix_w': gain(ks[1], D_MODEL),
        'w_in': nrm(ks[2], (L, D_MODEL, IN_COLS), D_MODEL ** -0.5),
        'ssd_conv_w': nrm(ks[3], (L, SSD_CONV, SSD_XBC_WIDTH), SSD_CONV ** -0.5),
        'ssd_conv_b': nrm(ks[4], (L, SSD_XBC_WIDTH), 0.02),
        'ssd_dt_bias': dt_bias,
        'ssd_a_log': jnp.log(jax.random.uniform(ks[6], (L, SSD_HEADS), jnp.float32, 1.0, 16.0)),
        'ssd_d': 1.0 + 0.1 * jax.random.normal(ks[7], (L, SSD_HEADS), jnp.float32),
        'ssd_norm_w': gain(ks[8], SSD_WIDTH),
        'fox_f_bias': jax.random.uniform(ks[9], (L, FOX_HEADS), jnp.float32, 2.0, 5.0),
        'fox_q_norm_w': gain(ks[10], HEAD_DIM),
        'fox_k_norm_w': gain(ks[11], HEAD_DIM),
        'w_out': nrm(ks[12], (L, MIX_WIDTH, D_MODEL), MIX_WIDTH ** -0.5),
        'norm_ffn_w': gain(ks[13], D_MODEL),
        'w_up': nrm(ks[14], (L, D_MODEL, 2 * D_FF), D_MODEL ** -0.5),
        'ffn_conv_w': nrm(ks[15], (L, FFN_CONV, 2 * D_FF), FFN_CONV ** -0.5),
        'ffn_conv_b': nrm(ks[16], (L, 2 * D_FF), 0.02),
        'w_down': nrm(ks[17], (L, D_FF, D_MODEL), D_FF ** -0.5),
    }

def first_block(x, norm_mix_w, w_in, ssd_conv_w, ssd_conv_b, ssd_dt_bias, ssd_a_log, ssd_d,
              ssd_norm_w, fox_f_bias, fox_q_norm_w, fox_k_norm_w, w_out, norm_ffn_w,
              w_up, ffn_conv_w, ffn_conv_b, w_down):
    for layer in range(DEPTH):
        h = rms_norm(x, norm_mix_w[layer])
        proj = h @ w_in[layer].astype(h.dtype)
        z, xbc, dt_raw, q, k, v, f_raw = jnp.split(
            proj, [Z_END, XBC_END, DT_END, Q_END, K_END, V_END], axis=-1)
        y_ssd = ssd_mixer(xbc, z, dt_raw, ssd_conv_w[layer], ssd_conv_b[layer], ssd_dt_bias[layer],
                          ssd_a_log[layer], ssd_d[layer], ssd_norm_w[layer])
        y_fox = fox_mixer(q, k, v, f_raw, fox_f_bias[layer], fox_q_norm_w[layer], fox_k_norm_w[layer])
        mixed = jnp.concatenate([y_ssd, y_fox.astype(y_ssd.dtype)], axis=-1)
        x = x + (mixed @ w_out[layer].astype(mixed.dtype)).astype(x.dtype)
        hf = rms_norm(x, norm_ffn_w[layer])
        x = x + conv_gated_mlp(hf, w_up[layer], ffn_conv_w[layer], ffn_conv_b[layer], w_down[layer]).astype(x.dtype)
    return x


PLE_DIM = 256
EPS = 1e-6
RET_HEADS = 4
RET_DK = 128
RET_DV = 128
RET_CHUNK = 128
SWA_HEADS = 8
SWA_KV_HEADS = 2
SWA_GROUP = SWA_HEADS // SWA_KV_HEADS
SWA_HD = 64
WINDOW = 128
N_GROUPS = 4
EXPERTS_PER_GROUP = 8
N_EXPERTS = N_GROUPS * EXPERTS_PER_GROUP
EXPERT_FF = 256
TOP_K = 2

RET_QK = RET_HEADS * RET_DK
RET_V = RET_HEADS * RET_DV
SWA_Q = SWA_HEADS * SWA_HD
SWA_KV = SWA_KV_HEADS * SWA_HD
IN_SPLITS = (RET_QK, RET_QK, RET_V, RET_V, SWA_Q, SWA_KV, SWA_KV, D_MODEL, D_MODEL)
IN_WIDTH = sum(IN_SPLITS)


def rms_norm_2(x, g):
    xf = x.astype(jnp.float32)
    y = xf * lax.rsqrt(jnp.mean(xf * xf, axis=-1, keepdims=True) + EPS)
    return (y * g.astype(jnp.float32)).astype(x.dtype)

def head_group_norm(y, g, b):
    yf = y.astype(jnp.float32)
    mu = jnp.mean(yf, axis=-1, keepdims=True)
    var = jnp.mean(jnp.square(yf - mu), axis=-1, keepdims=True)
    yn = ((yf - mu) * lax.rsqrt(var + EPS)).reshape(y.shape[0], y.shape[1], -1)
    return (yn * g.astype(jnp.float32) + b.astype(jnp.float32)).astype(y.dtype)

def retention_chunkwise(q, k, v):
    dtype = v.dtype
    q = q.astype(jnp.float32)
    k = k.astype(jnp.float32) * (RET_DK ** -0.5)
    v = v.astype(jnp.float32)
    b, s, h, dk = q.shape
    nc = s // RET_CHUNK
    q = q.reshape(b, nc, RET_CHUNK, h, dk)
    k = k.reshape(b, nc, RET_CHUNK, h, dk)
    v = v.reshape(b, nc, RET_CHUNK, h, RET_DV)
    log_gamma = jnp.log1p(-jnp.exp2(-5.0 - jnp.arange(h, dtype=jnp.float32)))
    pos = jnp.arange(RET_CHUNK, dtype=jnp.float32)
    diff = pos[:, None] - pos[None, :]
    decay_mask = jnp.where(diff[None] >= 0.0,
                           jnp.exp(jnp.maximum(diff, 0.0)[None] * log_gamma[:, None, None]), 0.0)
    scores = jnp.einsum('bnihd,bnjhd->bnhij', q, k) * decay_mask
    inner = jnp.einsum('bnhij,bnjhv->bnihv', scores, v)
    zeta = jnp.exp((RET_CHUNK - 1.0 - pos)[None, :] * log_gamma[:, None])
    chunk_kv = jnp.einsum('bnjhd,bnjhv,hj->nbhdv', k, v, zeta)
    chunk_decay = jnp.exp(RET_CHUNK * log_gamma)[None, :, None, None]

    def step(state, kv):
        return chunk_decay * state + kv, state

    _, prev_states = lax.scan(step, jnp.zeros_like(chunk_kv[0]), chunk_kv)
    xi = jnp.exp((pos + 1.0)[None, :] * log_gamma[:, None])
    cross = jnp.einsum('bnihd,nbhdv,hi->bnihv', q, prev_states, xi)
    return (inner + cross).reshape(b, s, h, RET_DV).astype(dtype)

def sliding_window_gqa(q, k, v, sinks):
    b, s = q.shape[:2]
    nb = s // WINDOW
    qb = q.reshape(b, nb, WINDOW, SWA_KV_HEADS, SWA_GROUP, SWA_HD)
    kb = k.reshape(b, nb, WINDOW, SWA_KV_HEADS, SWA_HD)
    vb = v.reshape(b, nb, WINDOW, SWA_KV_HEADS, SWA_HD)
    k_band = jnp.concatenate([jnp.concatenate([jnp.zeros_like(kb[:, :1]), kb[:, :-1]], axis=1), kb], axis=2)
    v_band = jnp.concatenate([jnp.concatenate([jnp.zeros_like(vb[:, :1]), vb[:, :-1]], axis=1), vb], axis=2)
    scores = jnp.einsum('bnqkgd,bnskd->bnkgqs', qb, k_band).astype(jnp.float32) * (SWA_HD ** -0.5)
    qi = jnp.arange(WINDOW)
    sj = jnp.arange(2 * WINDOW)
    rel = qi[:, None] + WINDOW - sj[None, :]
    in_window = (rel >= 0) & (rel < WINDOW)
    key_exists = (jnp.arange(nb)[:, None] * WINDOW - WINDOW + sj[None, :]) >= 0
    mask = in_window[None] & key_exists[:, None, :]
    slopes = jnp.exp2(-8.0 * jnp.arange(1, SWA_HEADS + 1, dtype=jnp.float32) / SWA_HEADS)
    slopes = slopes.reshape(SWA_KV_HEADS, SWA_GROUP)
    alibi = -slopes[:, :, None, None] * rel.astype(jnp.float32)[None, None]
    scores = jnp.where(mask[None, :, None, None], scores + alibi[None, None], -1e30)
    sink = jnp.broadcast_to(sinks.astype(jnp.float32).reshape(1, 1, SWA_KV_HEADS, SWA_GROUP, 1, 1),
                            scores.shape[:-1] + (1,))
    probs = jax.nn.softmax(jnp.concatenate([scores, sink], axis=-1), axis=-1)[..., :-1]
    out = jnp.einsum('bnkgqs,bnskd->bnqkgd', probs.astype(v.dtype), v_band)
    return out.reshape(b, s, SWA_Q)

def hierarchical_moe(h, w_rg, b_rg, w_re, b_re, w_gate, w_up, w_down):
    b, s, d = h.shape
    hf = h.reshape(-1, d)
    g_prob = jax.nn.softmax((hf @ w_rg + b_rg).astype(jnp.float32), axis=-1)
    g_sel = jnp.argmax(g_prob, axis=-1)
    g_w = jnp.take_along_axis(g_prob, g_sel[:, None], axis=-1)
    e_logits = (hf @ w_re + b_re).astype(jnp.float32).reshape(-1, N_GROUPS, EXPERTS_PER_GROUP)
    e_in_group = jnp.take_along_axis(e_logits, g_sel[:, None, None], axis=1)[:, 0]
    top_p, top_i = lax.top_k(jax.nn.softmax(e_in_group, axis=-1), TOP_K)
    top_p = top_p / jnp.sum(top_p, axis=-1, keepdims=True)
    expert_id = g_sel[:, None] * EXPERTS_PER_GROUP + top_i
    combine = jnp.sum(jax.nn.one_hot(expert_id, N_EXPERTS, dtype=jnp.float32)
                      * (g_w * top_p)[..., None], axis=1)
    y = jnp.zeros_like(hf)
    for grp in range(N_GROUPS):
        sl = slice(grp * EXPERTS_PER_GROUP, (grp + 1) * EXPERTS_PER_GROUP)
        hid = jax.nn.silu(jnp.einsum('td,edf->tef', hf, w_gate[sl])) * jnp.einsum('td,edf->tef', hf, w_up[sl])
        y = y + jnp.einsum('tef,efd->td', hid * combine[:, sl, None].astype(hid.dtype), w_down[sl])
    return y.reshape(b, s, d)

def second_inputs(seed: int = 0) -> dict:
    key = jax.random.key(seed)
    ks = jax.random.split(key, 26)
    f32 = jnp.float32
    L = DEPTH

    def nrm(k, shape, scale):
        return jax.random.normal(k, shape, f32) * scale

    def gain(k, shape):
        return 1.0 + 0.02 * jax.random.normal(k, shape, f32)

    return dict(
        x=nrm(ks[0], (BATCH, SEQ, D_MODEL), 1.0),
        p=nrm(ks[1], (L, BATCH, SEQ, PLE_DIM), 1.0),
        mix_norm_g=gain(ks[2], (L, D_MODEL)),
        w_in=nrm(ks[3], (L, D_MODEL, IN_WIDTH), D_MODEL ** -0.5),
        ret_gn_g=gain(ks[4], (L, RET_V)),
        ret_gn_b=nrm(ks[5], (L, RET_V), 0.02),
        w_ret_o=nrm(ks[6], (L, RET_V, D_MODEL), RET_V ** -0.5),
        q_norm_g=gain(ks[7], (L, SWA_HD)),
        k_norm_g=gain(ks[8], (L, SWA_HD)),
        attn_sinks=nrm(ks[9], (L, SWA_HEADS), 0.5),
        w_swa_o=nrm(ks[10], (L, SWA_Q, D_MODEL), SWA_Q ** -0.5),
        w_out=nrm(ks[11], (L, D_MODEL, D_MODEL), D_MODEL ** -0.5),
        ffn_norm_g=gain(ks[12], (L, D_MODEL)),
        w_router_group=nrm(ks[13], (L, D_MODEL, N_GROUPS), D_MODEL ** -0.5),
        b_router_group=nrm(ks[14], (L, N_GROUPS), 0.01),
        w_router_expert=nrm(ks[15], (L, D_MODEL, N_EXPERTS), D_MODEL ** -0.5),
        b_router_expert=nrm(ks[16], (L, N_EXPERTS), 0.01),
        w_exp_gate=nrm(ks[17], (L, N_EXPERTS, D_MODEL, EXPERT_FF), D_MODEL ** -0.5),
        w_exp_up=nrm(ks[18], (L, N_EXPERTS, D_MODEL, EXPERT_FF), D_MODEL ** -0.5),
        w_exp_down=nrm(ks[19], (L, N_EXPERTS, EXPERT_FF, D_MODEL), EXPERT_FF ** -0.5),
        ple_gate_norm_g=gain(ks[20], (L, D_MODEL)),
        w_ple_gate=nrm(ks[21], (L, D_MODEL, D_MODEL), D_MODEL ** -0.5),
        w_ple=nrm(ks[22], (L, PLE_DIM, D_MODEL), PLE_DIM ** -0.5),
        ple_norm_g=gain(ks[23], (L, D_MODEL)),
    )

def second_block(x, p, mix_norm_g, w_in, ret_gn_g, ret_gn_b, w_ret_o, q_norm_g, k_norm_g, attn_sinks,
              w_swa_o, w_out, ffn_norm_g, w_router_group, b_router_group, w_router_expert,
              b_router_expert, w_exp_gate, w_exp_up, w_exp_down, ple_gate_norm_g, w_ple_gate,
              w_ple, ple_norm_g):
    b, s, _ = x.shape
    split_at = [int(c) for c in np.cumsum(IN_SPLITS)[:-1]]
    for i in range(DEPTH):
        h = rms_norm_2(x, mix_norm_g[i])
        z = h @ w_in[i]
        rq, rk, rv, rg, sq, sk, sv, gate_r, gate_s = jnp.split(z, split_at, axis=-1)
        y_r = retention_chunkwise(rq.reshape(b, s, RET_HEADS, RET_DK),
                                  rk.reshape(b, s, RET_HEADS, RET_DK),
                                  rv.reshape(b, s, RET_HEADS, RET_DV))
        y_r = (jax.nn.silu(rg) * head_group_norm(y_r, ret_gn_g[i], ret_gn_b[i])) @ w_ret_o[i]
        q = rms_norm_2(sq.reshape(b, s, SWA_HEADS, SWA_HD), q_norm_g[i])
        k = rms_norm_2(sk.reshape(b, s, SWA_KV_HEADS, SWA_HD), k_norm_g[i])
        v = sv.reshape(b, s, SWA_KV_HEADS, SWA_HD)
        y_s = sliding_window_gqa(q, k, v, attn_sinks[i]) @ w_swa_o[i]
        merged = jax.nn.sigmoid(gate_r) * y_r + jax.nn.sigmoid(gate_s) * y_s
        x = x + merged @ w_out[i]
        x = x + hierarchical_moe(rms_norm_2(x, ffn_norm_g[i]), w_router_group[i], b_router_group[i],
                                 w_router_expert[i], b_router_expert[i], w_exp_gate[i],
                                 w_exp_up[i], w_exp_down[i])
        ple = rms_norm_2(p[i] @ w_ple[i], ple_norm_g[i])
        x = x + jax.nn.sigmoid(rms_norm_2(x, ple_gate_norm_g[i]) @ w_ple_gate[i]) * ple
    return x


def setup_inputs(seed=0):
    out = dict(first_inputs(seed))
    for name, value in second_inputs(seed + 1).items():
        if name != "x":
            out[name + "_2"] = value
    return out


def reference(
    x, norm_mix_w, w_in, ssd_conv_w, ssd_conv_b, ssd_dt_bias, ssd_a_log, ssd_d, ssd_norm_w,
    fox_f_bias, fox_q_norm_w, fox_k_norm_w, w_out, norm_ffn_w, w_up, ffn_conv_w, ffn_conv_b,
    w_down, p_2, mix_norm_g_2, w_in_2, ret_gn_g_2, ret_gn_b_2, w_ret_o_2, q_norm_g_2,
    k_norm_g_2, attn_sinks_2, w_swa_o_2, w_out_2, ffn_norm_g_2, w_router_group_2,
    b_router_group_2, w_router_expert_2, b_router_expert_2, w_exp_gate_2, w_exp_up_2,
    w_exp_down_2, ple_gate_norm_g_2, w_ple_gate_2, w_ple_2, ple_norm_g_2,
):
    x = first_block(
        x, norm_mix_w, w_in, ssd_conv_w, ssd_conv_b, ssd_dt_bias, ssd_a_log, ssd_d, ssd_norm_w,
        fox_f_bias, fox_q_norm_w, fox_k_norm_w, w_out, norm_ffn_w, w_up, ffn_conv_w, ffn_conv_b,
        w_down,
    )
    return second_block(
        x, p_2, mix_norm_g_2, w_in_2, ret_gn_g_2, ret_gn_b_2, w_ret_o_2, q_norm_g_2, k_norm_g_2,
        attn_sinks_2, w_swa_o_2, w_out_2, ffn_norm_g_2, w_router_group_2, b_router_group_2,
        w_router_expert_2, b_router_expert_2, w_exp_gate_2, w_exp_up_2, w_exp_down_2,
        ple_gate_norm_g_2, w_ple_gate_2, w_ple_2, ple_norm_g_2,
    )


_drawn_inputs = setup_inputs


def setup_inputs(seed=0):
    import zlib

    import numpy as np

    out = dict(_drawn_inputs(seed))
    spreads = {}
    factors = {'fox_q_norm_w': 6.348,
     'fox_k_norm_w': 5.681,
     'ffn_conv_b': 2.714,
     'mix_norm_g_2': 3.065,
     'ret_gn_g_2': 5.331,
     'ret_gn_b_2': 5.211,
     'q_norm_g_2': 8.0,
     'k_norm_g_2': 6.74,
     'attn_sinks_2': 115.165,
     'ffn_norm_g_2': 2.806,
     'b_router_group_2': 18.085,
     'b_router_expert_2': 6.475,
     'ple_gate_norm_g_2': 38.424,
     'ple_norm_g_2': 125.081}
    for name, (base, spread) in spreads.items():
        noise = np.random.default_rng([zlib.crc32(name.encode()), seed]).standard_normal(out[name].shape)
        drawn = base * np.exp(spread * noise) if base else spread * noise
        out[name] = jnp.asarray(drawn.astype(out[name].dtype))
    for name, factor in factors.items():
        out[name] = (out[name] * factor).astype(out[name].dtype)
    return out
```

```python
from contextlib import ExitStack

import numpy as np

import concourse.bass as bass
from concourse import mybir

F32 = mybir.dt.float32
F32R = mybir.dt.float32r
BF16 = mybir.dt.bfloat16
I32 = mybir.dt.int32
ALU = mybir.AluOpType
ACT = mybir.ActivationFunctionType
AX = mybir.AxisListType

P = 128
S = 512
T = S // P
D = 1024
DC = D // P
EPS = 1e-6
NEG = -1e30

HD = 64
H1 = 16
NS = 128
XBC = D + 4 * NS
FF = 2816
RH = 4
SH, SKV = 8, 2
NG, EG = 4, 8
NE = NG * EG
EF = 256
TILES = NE + 2 * S // P - 1
RING = 8

PLAN = (
    [(f"xbc{b}", 8) for b in range(3)] + [(f"z{b}", 8) for b in range(2)]
    + [("dtf", 2)] + [(f"{n}{b}", 8) for n in "qkv" for b in range(2)]
    + [(f"out{b}", 16) for b in range(2)]
    + [(f"up{b}", 8) for b in range(FF // 256)] + [(f"down{b}", FF // P) for b in range(2)]
    + [(n, 8) for n in ("rq", "rk", "rv", "rg", "sq")] + [("skv", 4)]
    + [(f"g{n}{b}", 8) for n in "rs" for b in range(2)]
    + [(f"{n}{b}", 4) for b in range(2) for n in ("ro", "so")]
    + [(f"mo{b}", 8) for b in range(2)] + [("wr", 1), ("moe", TILES * 8)]
    + [(f"ple{b}", 2) for b in range(2)] + [(f"pg{b}", 8) for b in range(2)]
)
FIRST, UNITS = {}, {}
_at = 0
for _name, _n in PLAN:
    FIRST[_name], UNITS[_name] = _at, _n
    _at += _n
NU = _at
MOE_AT = FIRST["moe"]
XU = TILES * 8

COLS = {}
_at = 0
for _name, _n in (("nmix", DC), ("nffn", DC), ("nmix2", DC), ("nffn2", DC), ("nple", DC), ("nssd", DC),
                  ("cw", 12 * 4), ("cb", 12), ("fw", 44 * 3), ("fb", 44), ("qw", 1), ("kw", 1),
                  ("sqw", 1), ("skw", 1), ("dtb", 1), ("sgn", 1), ("alog", 1), ("asg", 1),
                  ("dskip", H1), ("gng", RH), ("gnb", RH), ("sink", SH), ("zeta", RH)):
    COLS[_name] = (_at, _n)
    _at += _n
NCST = _at

LOG_GAMMA = np.log1p(-np.exp2(-5.0 - np.arange(RH)))


class Chain:

    def __init__(self, eng, sem):
        self.eng, self.sem, self.n = eng, sem, 0

    def mark(self, ins):
        self.n += 1
        ins.then_inc(self.sem, 1)
        return self.n

    def wait(self, n=None):
        self.eng.wait_ge(self.sem, self.n if n is None else n)

    def link(self, ins):
        self.mark(ins)
        self.wait()


def bass_two_blocks(nc, x, cst_d, rows_d, mats_d, bias_d, ident_d, identb_d, maskT_d, maskL_d, sel_d, rb_d, tri_d,
                    pT_d, wstream, wexp, out):
    ctx = ExitStack()
    with ctx:
        def sem(name):
            return ctx.enter_context(nc.semaphore(name))

        base = 16512

        def at(name, shape, dt, off):
            return nc.alloc_sbuf_tensor_at(name, shape, dt, offset=base + int(off * 1024))

        ctx.enter_context(nc.sbuf_tensor("slab", [P, (229344 - 16512) // 4 - 32], F32))

        X = at("X", [P, T, D], F32, 0)
        raw = at("raw", [P, RING, 512], F32, 16)
        hi = at("hi", [P, RING, 512], F32R, 32)
        lo = at("lo", [P, RING, 512], F32R, 48)
        cst = at("cst", [P, NCST], F32, 64)
        ident = at("ident", [P, P], F32, 65.375)
        identb = at("identb", [P, P], BF16, 65.875)
        maskT = at("maskT", [P, P], BF16, 66.125)
        maskL = at("maskL", [P, P], BF16, 66.375)
        small = at("small", [P, 128], F32, 66.625)
        assert NCST * 4 <= 1.375 * 1024
        A = 67.25
        HTh = at("HTh", [P, DC, S], F32R, A)
        HTl = at("HTl", [P, DC, S], F32R, A + 16)
        zs = at("zs", [P, T, D], F32, A + 32)
        xs = at("xs", [P, T, D], F32, A + 48)
        MIXh0 = at("MIXh0", [P, DC, S], F32R, A + 32)
        MIXl0 = at("MIXl0", [P, DC, S], F32R, A + 48)
        xbcT = at("xbcT", [P, 12, S], F32, A + 64)
        Y1 = at("Y1", [P, T, D], F32, A + 64)
        Btok = at("Btok", [P, T, 2 * NS], F32, A + 88)
        xn = at("xn", [P, T, D], F32, A + 92)
        rows = at("rows", [P, 7, S], F32, A + 92)
        xd = at("xd", [P, T, 512], F32, A + 92)
        xw = at("xw", [P, T, 512], F32, A + 100)
        st = at("st", [P, 3, 512], F32, A + 108)
        cbS = at("cbS", [P, 2, S], F32, A + 114)
        acc = at("acc", [P, 4, S], F32, A + 118)
        SC = at("SC", [P, 4, S], F32, A + 118)
        yt = at("yt", [P, 512], F32, A + 126)
        BR = at("BR", [P, S], F32R, A + 128)
        tok = at("tok", [P, 4, T, 32], F32, A + 130)
        decB = small[:, 64:128]
        sel = at("sel", [P, H1, P], F32R, A + 132)
        selF = at("selF", [P, H1, P], F32, A + 108)
        q = at("q", [P, T, D], F32, A + 64)
        k = at("k", [P, T, D], F32, A + 80)
        v = at("v", [P, T, D], F32, A + 96)
        qT = at("qT", [P, DC, S], F32, A)
        kT = at("kT", [P, DC, S], F32, A + 16)
        MIXh1 = at("MIXh1", [P, DC, S], F32R, A + 64)
        MIXl1 = at("MIXl1", [P, DC, S], F32R, A + 80)
        Pb = at("Pb", [P, 2, 1280], F32, A + 112)
        PT = at("PT", [P, 1280], F32, A + 122)
        sqr = at("sqr", [P, 2, 512], F32, A + 112)
        qst = at("qst", [P, 2, T, H1], F32, A + 130)
        qst2 = at("qst2", [P, 2, T, H1], F32, A + 130.5)
        fst = at("fst", [P, 3, 2, 4], F32, A + 131)
        qst3 = at("qst3", [P, 2, T, H1], F32, A + 131.25)
        gh = at("gh", [P, FF // P, S], F32R, A + 32)
        gl = at("gl", [P, FF // P, S], F32R, A + 76)
        xnF = at("xnF", [P, T, D], F32, A + 120)
        facc = at("facc", [P, 4, S], F32, A + 120)
        fsg = at("fsg", [P, 2, S], F32, A + 128)
        fg = at("fg", [P, 2, S], F32, A + 132)
        rqT = at("rqT", [P, RH, S], F32, A + 32)
        rqx = at("rqx", [P, RH, S], F32, A + 40)
        rkT = at("rkT", [P, RH, S], F32, A + 48)
        rv = at("rv", [P, T, 512], F32, A + 56)
        kz = at("kz", [P, T, 512], F32, A + 64)
        rg = at("rg", [P, RH, S], F32, A + 72)
        DM = at("DM", [P, 2, RH, P], F32, A + 80)
        sT = at("sT", [P, RH, S], F32, A + 84)
        xn2 = at("xn2", [P, T, D], F32, A + 84)
        yR = at("yR", [P, T, 512], F32, A + 92)
        yrh = at("yrh", [P, RH, S], F32R, A + 100)
        yrl = at("yrl", [P, RH, S], F32R, A + 108)
        rS = at("rS", [P, 3, 512], F32, A + 116)
        rbn = at("rbn", [P, T * RH, 6], F32, A + 122)
        rmv = at("rmv", [P, T * RH, 2], F32, A + 122.5)
        rrs = at("rrs", [P, T * RH], F32, A + 122.75)
        ryt = at("ryt", [P, RH, S], F32, A + 124)
        sq = at("sq", [P, T, 512], F32, A + 32)
        skv = at("skv", [P, T, 256], F32, A + 40)
        kd = at("kd", [P, T, 2, 128], F32, A + 44)
        sqT = at("sqT", [P, 4, S], F32, A + 48)
        skT = at("skT", [P, 2, S], F32, A + 56)
        sbias = at("sbias", [P, SH, 256], F32, A + 60)
        sPb = at("sPb", [P, 2, 896], F32, A + 68)
        sPT = at("sPT", [P, 896], F32, A + 76)
        ysh = at("ysh", [P, 4, S], F32R, A + 80)
        ysl = at("ysl", [P, 4, S], F32R, A + 88)
        sst = at("sst", [P, 3, T, 10], F32, A + 96)
        sfst = at("sfst", [P, 5, 2, 4], F32, A + 97)
        ssqr = at("ssqr", [P, 512], F32, A + 98)
        gr = at("gr", [P, DC, S], F32, A + 32)
        gs = at("gs", [P, DC, S], F32, A + 48)
        t1 = at("t1", [P, 4, S], F32, A + 64)
        t2 = at("t2", [P, 4, S], F32, A + 72)
        MTh = at("MTh", [P, DC, S], F32R, A)
        MTl = at("MTl", [P, DC, S], F32R, A + 16)
        xn3 = at("xn3", [P, T, D], F32, A + 32)
        XNh = at("XNh", [P, T, D], F32R, A + 48)
        XNl = at("XNl", [P, T, D], F32R, A + 64)
        rawd = at("rawd", [P, 2, 4, 512], F32, A + 80)
        grow = at("grow", [P, D], F32, A + 96)
        XTh = [at(f"XTh{i}", [P, DC, 2 * P], F32R, A + o) for i, o in ((0, 8), (1, 24))]
        XTl = [at(f"XTl{i}", [P, DC, 2 * P], F32R, A + o) for i, o in ((0, 16), (1, 100))]
        Sel = at("Sel", [P, T, 2 * P], F32R, A + 108)
        Se1 = at("Se1", [P, T, 2 * P], F32, A + 133.1875)
        Se2 = at("Se2", [P, T, 2 * P], F32, A + 112)
        esg = at("esg", [P, EF], F32, A + 137.1875)
        hid = at("hid", [P, EF], F32, A + 138.1875)
        hidT = at("hidT", [P, EF], F32, A + 139.1875)
        R = at("R", [P, 24, T, 36], F32, A + 116)
        rb = at("rb", [P, 76 + 2 * P], F32, A + 129.5)
        ovw = at("ovw", [P, 5, NE], F32, A + 130.8125)
        eow = at("eow", [P, 8, NE], F32, A + 131.4375)
        Mb = at("Mb", [P, T, NE], BF16, A + 132.4375)
        tri = at("tri", [P, 2, P], BF16, A + 132.6875)
        yrow = at("yrow", [P, 2, T], F32, 66.875)
        yrel = at("yrel", [P, 2, T], F32, 66.90625)
        rq_w = at("rq_w", [P, 8, T], F32, 66.9375)
        yidx = at("yidx", [P, 2, T], I32, 67.0625)
        eov = at("eov", [P, 8], I32, 67.09375)
        Ye = at("Ye", [P, 2, D], F32, A)
        YG = at("YG", [P, 8, D], F32, A)
        pTf = at("pTf", [P, 2, S], F32, A + 52)
        pTh = at("pTh", [P, 2, S], F32R, A + 56)
        pTl = at("pTl", [P, 2, S], F32R, A + 60)
        ple = at("ple", [P, T, D], F32, A + 64)
        prow = at("prow", [P, D], F32, A + 80)
        psg = at("psg", [P, T, 512], F32, A + 84)
        psq = at("psq", [P, T, 512], F32, A + 92)
        xn4 = at("xn4", [P, T, D], F32, A + 32)

        ye_d = nc.dram_tensor("ye_d", [TILES * P, D], F32, kind="Internal").ap()

        ps = ctx.enter_context(nc.psum_tensor("ps", [P, 8, 512], F32))

        def bset(s):
            return ps[:, 4 * s:4 * s + 4, :]

        x_loaded, misc_loaded = sem("x_loaded"), sem("misc_loaded")
        raw_full = [sem(f"raw_full{i}") for i in range(RING)]
        hi_ready, lo_ready, unit_used = sem("hi_ready"), sem("lo_ready"), sem("unit_used")
        act_c, dve_c, pool_c = sem("act_c"), sem("dve_c"), sem("pool_c")
        n_ss, n_ms, n_rstd, n_xn, n_tr, n_hi, ht_lo = [sem(s) for s in "n_ss n_ms n_rstd n_xn n_tr n_hi ht_lo".split()]
        cvA, cvD, xbc_ready, z_done = [sem(s) for s in "cvA cvD xbc_ready z_done".split()]
        dtf_v, dtf_e, dtf_s, dtf_l, dtf_cs, br_hi, br_lo, dte_a, dte_d, tok_mm, tok_ready, ddg, dec_mm = [
            sem(s) for s in ("dtf_v dtf_e dtf_s dtf_l dtf_cs br_hi br_lo dte_a dte_d tok_mm tok_ready "
                             "ddg dec_mm").split()]
        xs_tr, xs_ready, cb_mm, cb_ready, xdw, st_mm, st_ready, bc_mm, seg, dcy, sc_ready, yd_mm, yo_mm, y_done = [
            sem(s) for s in ("xs_tr xs_ready cb_mm cb_ready xdw st_mm st_ready bc_mm seg dcy sc_ready yd_mm yo_mm "
                             "y_done").split()]
        mix_tr, mix_hi, mix_lo = [sem(s) for s in "mix_tr mix_hi mix_lo".split()]
        qkv_copied, qk_ss, qk_ln, qk_n, qk_tr = [
            sem(s) for s in "qkv_copied qk_ss qk_ln qk_n qk_tr".split()]
        fx_qk, fx_nm, fx_exp, fx_pn, fx_t, fx_pA, fx_pD, fx_pv, fx_hi, fx_lo = [
            sem(s) for s in "fx_qk fx_nm fx_exp fx_pn fx_t fx_pA fx_pD fx_pv fx_hi fx_lo".split()]
        x_res = sem("x_res")
        ys_ss, ys_ms, ys_rs, ys_n = [sem(s) for s in "ys_ss ys_ms ys_rs ys_n".split()]
        yo_done, dec_cp, qT_done, kT_done, etok, sel_loaded, sel_ready, sel_z, ff_c = [
            sem(s) for s in "yo_done dec_cp qT_done kT_done etok sel_loaded sel_ready sel_z ff_c".split()]
        ffA, ffD, ff_sg, ff_g, ff_hi, ff_lo = [sem(s) for s in "ffA ffD ff_sg ff_g ff_hi ff_lo".split()]
        b2c, mats_loaded, rq_x, rk_tr, kz_ready, ry_mm, yR_norm, yr_t, yr_hi, yr_lo = [
            sem(s) for s in ("b2c mats_loaded rq_x rk_tr kz_ready ry_mm yR_norm yr_t "
                             "yr_hi yr_lo").split()]
        rvar, rpow, s_ss, s_pow, s_n, s_tr, sT_ready = [
            sem(s) for s in "rvar rpow s_ss s_pow s_n s_tr sT_ready".split()]
        sx_l = sem("sx_l")
        m_t, m_r, m_s, skT_ready, sbias_loaded = [
            sem(s) for s in "m_t m_r m_s skT_ready sbias_loaded".split()]
        xg_f, xg_hi, xg_lo, mb_ready, rk_mm, yidx_ready, eov_ready, xsel, xt_h, xt_l, xg_mh, xg_ml, yg0, yg1 = [
            sem(s) for s in ("xg_f xg_hi xg_lo mb_ready rk_mm yidx_ready eov_ready xsel xt_h xt_l xg_mh xg_ml "
                             "yg0 yg1").split()]
        e_h, e_tr, e_hT, dn_mm, ye_a, ye_b = [sem(s) for s in "e_h e_tr e_hT dn_mm ye_a ye_b".split()]
        sel_c = sem("sel_c")
        ye_st = [sem("ye_st0"), sem("ye_st1")]
        dn_full = [sem("dn_full0"), sem("dn_full1")]
        r_d, r_e, route_loaded, e_sg, p_loaded, p_hi, p_lo, ple_done, p_sg = [
            sem(s) for s in "r_d r_e route_loaded e_sg p_loaded p_hi p_lo ple_done p_sg".split()]
        prow_loaded, out_ready, out_stored = [sem(s) for s in "prow_loaded out_ready out_stored".split()]

        block_cm = nc.Block()
        block = block_cm.__enter__()

        def col(name, i=0, n=1):
            c0 = COLS[name][0] + i
            return cst[:, c0:c0 + n]

        def act_split(act, u, n=1):
            for i in range(u, u + n):
                act.wait_ge(raw_full[i % RING], 16 * (i // RING + 1))
                if i >= RING:
                    act.wait_ge(unit_used, i - RING + 1)
                act.activation(hi[:, i % RING, :], raw[:, i % RING, :], ACT.Copy).then_inc(hi_ready, 1)

        def dve_split(dve, u, n=1):
            for i in range(u, u + n):
                dve.wait_ge(hi_ready, i + 1)
                dve.tensor_tensor(lo[:, i % RING, :], raw[:, i % RING, :], hi[:, i % RING, :].bitcast(F32),
                                  ALU.subtract).then_inc(lo_ready, 1)

        def mm3(pe, o, ah, al, bh, bl, start, stop):
            pe.matmul(o, al, bh, start=start, stop=False)
            pe.matmul(o, ah, bl, start=False, stop=False)
            return pe.matmul(o, ah, bh, start=False, stop=stop)

        def pe_tokens(pe, u, nk, s, Lh, Ll, k0=0, ready=None, first=True, last=True):
            for c in range(nk):
                if ready is not None:
                    pe.wait_ge(ready[0], ready[1] + c + 1)
                pe.wait_ge(lo_ready, u + c + 1)
                w = (u + c) % RING
                for t in range(T):
                    mm = mm3(pe, ps[:, 4 * s + t, :], Lh[:, k0 + c, t * P:(t + 1) * P], Ll[:, k0 + c, t * P:(t + 1) * P],
                             hi[:, w, :], lo[:, w, :], first and c == 0, last and c == nk - 1)
                mm.then_inc(unit_used, 1)

        def pe_features(pe, u, nk, s, Rh, Rl, ready=None, slot=None):
            for c in range(nk):
                if ready is not None:
                    pe.wait_ge(ready[0], ready[1] + c + 1)
                pe.wait_ge(lo_ready, u + (c + 1))
                w = ((u if slot is None else slot) + c) % RING
                for j in range(4):
                    mm = mm3(pe, ps[:, 4 * s + j, :], hi[:, w, j * P:(j + 1) * P], lo[:, w, j * P:(j + 1) * P],
                             Rh[:, c, :], Rl[:, c, :], c == 0, c == nk - 1)
                mm.then_inc(unit_used, 1)

        def act_norm(act, n, xnb, wname):
            if n == 0:
                act.wait_ge(x_loaded, 16)
            else:
                act.wait_ge(x_res, 8 * n)
            for t in range(T):
                ins = act.activation(xnb[:, t, :], X[:, t, :], ACT.Square, accum_out=small[:, t:t + 1])
            ins.then_inc(n_ss, 1)
            for c in range(DC):
                act.wait_ge(n_tr, DC * n + c + 1)
                act.activation(HTh[:, c, :], ps[:, c, :], ACT.Identity,
                               scale=col(wname, c)).then_inc(n_hi, 1)

        def dve_norm(dve, n, xnb, wname):
            dve.wait_ge(n_ss, n + 1)
            dve.tensor_scalar(small[:, 4:8], small[:, 0:4], 1.0 / D, EPS, ALU.mult, ALU.add).then_inc(n_ms, 1)
            dve.wait_ge(n_rstd, n + 1)
            for t in range(T):
                dve.tensor_scalar(xnb[:, t, :], X[:, t, :], small[:, 8 + t:9 + t], None, ALU.mult).then_inc(n_xn, 1)
            for c in range(DC):
                dve.wait_ge(n_hi, DC * n + c + 1)
                dve.scalar_tensor_tensor(HTl[:, c, :], ps[:, c, :], col(wname, c), HTh[:, c, :].bitcast(F32),
                                         ALU.mult, ALU.subtract).then_inc(ht_lo, 1)

        def pool_norm(pool, n):
            pool.wait_ge(n_ms, n + 1)
            pool.tensor_tensor(small[:, 8:12], small[:, 4:8], small[:, 12:16], ALU.pow).then_inc(n_rstd, 1)

        def pe_norm(pe, n, xnb, free):
            for s_, v_ in free:
                pe.wait_ge(s_, v_)
            pe.wait_ge(n_xn, T * (n + 1))
            for c in range(DC):
                for t in range(T):
                    tr = pe.transpose(ps[:, c, t * P:(t + 1) * P], xnb[:, t, c * P:(c + 1) * P], ident[:, :])
                tr.then_inc(n_tr, 1)

        FG = ((1, ((3, 0),)), (0, ((2, 0), (0, 384))), (2, ((1, 0),)))
        NG_ = len(FG)
        FOFF = (0, 128, 384, 768)
        PTB = ((3, 0), (4, 0), (5, 0), (4, 384))
        PTO = (0, 512, 1024, 896)
        SB = ((0, 256, P), (0, 0, 2 * P), (1, 0, 2 * P), (1, 256, 2 * P))
        SO = (0, 128, 384, 640)

        def PE_B2(pe):
            U = FIRST
            pe_norm(pe, 2, xn2, [(x_res, 16)])
            pe.wait_ge(ht_lo, 20)
            pe_features(pe, U["rq"], 8, 0, HTh, HTl, ready=(ht_lo, 16))
            pe_features(pe, U["rk"], 8, 1, HTh, HTl)
            pe.wait_ge(b2c, 4)
            pe_tokens(pe, U["rv"], 8, 0, HTh, HTl)
            pe.wait_ge(b2c, 8)
            pe_features(pe, U["rg"], 8, 1, HTh, HTl)
            pe.wait_ge(b2c, 12)
            for c in range(T - 1):
                for h in range(RH):
                    tr = pe.transpose(ps[:, c, h * P:(h + 1) * P], rkT[:, h, c * P:(c + 1) * P], ident[:, :])
                tr.then_inc(rk_tr, 1)
            pe.wait_ge(b2c, 16)
            for h in range(RH):
                for c in range(T):
                    mm = pe.matmul(ps[:, 4 + h, c * P:(c + 1) * P], rkT[:, h, c * P:(c + 1) * P],
                                   rqT[:, h, c * P:(c + 1) * P], start=True, stop=True)
                mm.then_inc(cb_mm, 1)
            for c in range(T - 1):
                pe.wait_ge(kz_ready, c + 1)
                for h in range(RH):
                    mm = pe.matmul(ps[:, c, h * P:(h + 1) * P], kz[:, c, h * P:(h + 1) * P], rv[:, c, h * P:(h + 1) * P],
                                   start=True, stop=True)
                mm.then_inc(st_mm, 1)
            pe.wait_ge(cb_ready, 2 + RH)
            pe.wait_ge(rq_x, RH)
            for c in range(T):
                if c:
                    pe.wait_ge(st_ready, 6 + c)
                for h in range(RH):
                    hc = slice(h * P, (h + 1) * P)
                    mm = pe.matmul(ps[:, 4 + c, hc], sT[:, h, c * P:(c + 1) * P], rv[:, c, hc], start=True, stop=c == 0)
                    if c:
                        mm = pe.matmul(ps[:, 4 + c, hc], rqx[:, h, c * P:(c + 1) * P], rS[:, c - 1, hc],
                                       start=False, stop=True)
                mm.then_inc(ry_mm, 1)
            pe_tokens(pe, U["sq"], 8, 0, HTh, HTl)
            pe.wait_ge(yR_norm, T)
            for h in range(RH):
                for t in range(T):
                    tr = pe.transpose(ps[:, 4 + h, t * P:(t + 1) * P], yR[:, t, h * P:(h + 1) * P], ident[:, :])
                tr.then_inc(mix_tr, 1)
            pe.wait_ge(b2c, 20)
            for i in range(4):
                pe.wait_ge(lo_ready, U["skv"] + i + 1)
                w = (U["skv"] + i) % RING
                for t in range(T):
                    for k_ in range(2):
                        c = 2 * i + k_
                        cc = slice(256 * k_, 256 * k_ + 256)
                        mm = mm3(pe, ps[:, t, 0:256], HTh[:, c, t * P:(t + 1) * P], HTl[:, c, t * P:(t + 1) * P],
                                 hi[:, w, cc], lo[:, w, cc], c == 0, c == DC - 1)
                mm.then_inc(unit_used, 1)
            pe.wait_ge(s_n, 1)
            pe.wait_ge(yr_t, RH)
            for c in range(4):
                for t in range(T):
                    tr = pe.transpose(ps[:, 4 + c, t * P:(t + 1) * P], sq[:, t, c * P:(c + 1) * P], ident[:, :])
                tr.then_inc(s_tr, 1)
            pe.wait_ge(b2c, 24)
            for g in range(SKV):
                for t in range(T):
                    tr = pe.transpose(ps[:, g, t * P:(t + 1) * P], kd[:, t, g, :], ident[:, :])
                tr.then_inc(s_tr, 1)
            pe.wait_ge(sT_ready, 4)
            pe.wait_ge(skT_ready, SKV)

            def scores(h):
                r = slice(HD * (h % 2), HD * (h % 2) + HD)
                if h:
                    pe.wait_ge(sx_l, h)
                for i, (bank, o, n) in enumerate(SB):
                    mm = pe.matmul(ps[:, bank, o:o + n], sqT[r, h // 2, i * P:(i + 1) * P],
                                   skT[r, h // 4, (i + 1) * P - n:(i + 1) * P], start=True, stop=True)
                mm.then_inc(fx_qk, 1)

            def values(h):
                pe.wait_ge(fx_pA, H1 + h + 1)
                pe.wait_ge(fx_pD, H1 + h + 1)
                pr = h // 2
                if pr >= 2:
                    pe.wait_ge(fx_lo, H1 // 2 + pr - 1)
                vc = slice(128 + HD * (h // 4), 128 + HD * (h // 4) + HD)
                for i in range(T):
                    o = ps[HD * (h % 2):HD * (h % 2) + HD, 4 + pr % 2, i * P:(i + 1) * P]
                    if i:
                        pe.matmul(o, skv[:, i - 1, vc], sPT[:, SO[i]:SO[i] + P], start=True, stop=False)
                    c0 = SO[i] + (P if i else 0)
                    mm = pe.matmul(o, skv[:, i, vc], sPT[:, c0:c0 + P], start=i == 0, stop=True)
                mm.then_inc(fx_pv, 1)

            scores(0)
            for h in range(SH):
                if h + 1 < SH:
                    scores(h + 1)
                if h:
                    values(h - 1)
                pe.wait_ge(fx_pn, NG_ * H1 + h + 1)
                if h:
                    pe.wait_ge(fx_pA, H1 + h)
                    pe.wait_ge(fx_pD, H1 + h)
                for k_ in range(7):
                    tr = pe.transpose(ps[:, 2 + k_ // 4, (k_ % 4) * P:(k_ % 4 + 1) * P],
                                      sPb[:, h % 2, k_ * P:(k_ + 1) * P], ident[:, :])
                tr.then_inc(fx_t, 1)
            values(SH - 1)
            for b, n in enumerate(("gr0", "gr1", "gs0", "gs1")):
                if b == 1:
                    pe.wait_ge(fx_lo, H1 // 2 + 4)
                if b >= 2:
                    pe.wait_ge(b2c, 24 + 4 * (b - 1))
                pe_features(pe, U[n], 8, b % 2, HTh, HTl)
            pe.wait_ge(yr_lo, RH)
            for b in range(2):
                if b:
                    pe.wait_ge(m_r, 4)
                else:
                    pe.wait_ge(b2c, 36)
                pe_features(pe, U[f"ro{b}"], 4, 0, yrh, yrl)
                if b:
                    pe.wait_ge(m_s, 4)
                else:
                    pe.wait_ge(b2c, 40)
                pe_features(pe, U[f"so{b}"], 4, 1, ysh, ysl)
            for b in range(2):
                pe.wait_ge((m_r, m_s)[b], 8)
                pe_tokens(pe, U[f"mo{b}"], 8, b, MTh, MTl, ready=(mix_lo, DC) if b == 0 else None)
            PE_MOE(pe)

        def ACT_B2(act, w, ch):
            U = FIRST
            act_norm(act, 2, xn2, "nmix2")

            def copy(dst, src, name, func=ACT.Copy, after=()):
                def piece():
                    act.wait_ge(unit_used, FIRST[name] + UNITS[name])
                    for s_, v_ in after:
                        act.wait_ge(s_, v_)
                    act.activation(dst, src, func).then_inc(b2c, 1)
                return piece

            w.upto(U["rk"] + 8)
            w.beside(U["rv"] + 8, [copy(rqT[:, j, :], ps[:, j, :], "rq") for j in range(4)])
            w.beside(U["rg"] + 8, [copy(rkT[:, j, :], ps[:, 4 + j, :], "rk") for j in range(4)])
            w.beside(U["sq"] + 8, [copy(rv[:, j, :], ps[:, j, :], "rv") for j in range(4)])
            for j in range(4):
                copy(rg[:, j, :], ps[:, 4 + j, :], "rg", ACT.Silu)()
            w.beside(U["skv"] + 4, [copy(sq[:, j, :], ps[:, j, :], "sq", after=((ry_mm, 4),)) for j in range(4)])
            for h in range(RH):
                act.wait_ge(yr_t, h + 1)
                act.activation(yrh[:, h, :], ryt[:, h, :], ACT.Copy).then_inc(yr_hi, 1)
            w.beside(U["gr0"] + 8, [copy(skv[:, j, :], ps[:, j, 0:256], "skv") for j in range(4)])
            for c in range(4):
                act.wait_ge(s_tr, c + 1)
                act.activation(sqT[:, c, :], ps[:, 4 + c, :], ACT.Identity, scale=small[:, 19:20]).then_inc(sT_ready, 1)

            def weights(h):
                act.wait_ge(fx_nm, NG_ * H1 + h + 1)
                for i in range(T):
                    n = P if i == 0 else 2 * P
                    act.activation(sPb[:, h % 2, SO[i]:SO[i] + n], sPb[:, h % 2, SO[i]:SO[i] + n], ACT.Exp,
                                   bias=sfst[:, 1, h % 2, i:i + 1], accum_out=sfst[:, 2, h % 2, i:i + 1])
                act.activation(sfst[:, 3, h % 2, :], sfst[:, 1, h % 2, :], ACT.Exp, bias=col("sink", h)).then_inc(fx_exp, 1)

            def transposed(h):
                act.wait_ge(fx_t, H1 + h + 1)
                if h:
                    act.wait_ge(fx_pv, H1 + h)
                act.activation(sPT[:, 0:512], ps[:, 2, :], ACT.Copy).then_inc(fx_pA, 1)

            def output(h):
                act.wait_ge(fx_pv, H1 + h + 1)
                act.activation(ysh[:, h // 2, :], ps[:, 4 + h // 2 % 2, :], ACT.Copy).then_inc(fx_hi, 1)

            weights(0)
            for h in range(SH):
                if h:
                    transposed(h - 1)
                if h + 1 < SH:
                    weights(h + 1)
                if h and h % 2 == 0:
                    output(h - 1)
            transposed(SH - 1)
            output(SH - 1)
            w.upto(U["gr1"] + 8)
            w.beside(U["gs0"] + 8, [copy(gr[:, j, :], ps[:, j, :], "gr0", ACT.Sigmoid) for j in range(4)])
            w.beside(U["gs1"] + 8, [copy(gr[:, 4 + j, :], ps[:, 4 + j, :], "gr1", ACT.Sigmoid) for j in range(4)])
            w.beside(U["ro0"] + 8, [copy(gs[:, j, :], ps[:, j, :], "gs0", ACT.Sigmoid) for j in range(4)])
            w.beside(U["ro1"] + 4, [copy(gs[:, 4 + j, :], ps[:, 4 + j, :], "gs1", ACT.Sigmoid) for j in range(4)])
            w.upto(U["ro1"] + 8)
            for b in range(2):
                for j in range(4):
                    act.wait_ge(m_t, 4 * b + j + 1)
                    act.activation(MTh[:, 4 * b + j, :], t1[:, j, :], ACT.Copy).then_inc(mix_hi, 1)
            w.upto(U["mo1"] + 8)
            w.upto(U["wr"] + 1)
            ACT_MOE(act, w, ch)

        def DVE_B2(dve, w, ch):
            U = FIRST
            dve_norm(dve, 2, xn2, "nmix2")

            def heads(a):
                return a.rearrange("p (h e) -> p h e", e=HD)

            def per_chunk(a):
                return a.rearrange("p (c i) -> p c i", c=T)

            w.upto(U["rk"] + 8)
            w.upto(U["rv"] + 8)

            def rqx_h(h):
                def piece():
                    dve.wait_ge(b2c, h + 1)
                    dve.wait_ge(mats_loaded, 16)
                    dve.tensor_tensor(per_chunk(rqx[:, h, :]), per_chunk(rqT[:, h, :]),
                                      DM[:, 1, h:h + 1, :].broadcast_to([P, T, P]), ALU.mult).then_inc(rq_x, 1)
                return piece

            w.beside(U["rg"] + 8, [rqx_h(h) for h in range(RH)])
            w.upto(U["sq"] + 8)
            for c in range(T - 1):
                dve.wait_ge(rk_tr, c + 1)
                dve.tensor_tensor(per_chunk(kz[:, c, :]), per_chunk(ps[:, c, :]),
                                  col("zeta", 0, RH).unsqueeze(2).broadcast_to([P, RH, P]), ALU.mult).then_inc(kz_ready, 1)
            for h in range(RH):
                dve.wait_ge(cb_mm, 2 + h + 1)
                dve.tensor_tensor(per_chunk(sT[:, h, :]), per_chunk(ps[:, 4 + h, :]),
                                  DM[:, 0, h:h + 1, :].broadcast_to([P, T, P]), ALU.mult).then_inc(cb_ready, 1)
            for c in range(T - 1):
                dve.wait_ge(st_mm, 6 + c + 1)
                if c == 0:
                    dve.tensor_copy(rS[:, 0, :], ps[:, 0, :]).then_inc(st_ready, 1)
                    continue
                dve.wait_ge(st_ready, 6 + c)
                for h in range(RH):
                    hc = slice(h * P, (h + 1) * P)
                    ins = dve.scalar_tensor_tensor(rS[:, c, hc], rS[:, c - 1, hc], float(np.exp(P * LOG_GAMMA[h])),
                                                   ps[:, c, hc], ALU.mult, ALU.add)
                ins.then_inc(st_ready, 1)
            for c in range(T):
                dve.wait_ge(ry_mm, c + 1)
                for h in range(RH):
                    ins = dve.bn_stats(rbn[:, c * RH + h, :], ps[:, 4 + c, h * P:(h + 1) * P])
                ch.link(ins)
                for h in range(RH):
                    ins = dve.bn_aggr(rmv[:, c * RH + h, :], rbn[:, c * RH + h, :])
            ch.link(ins)
            dve.tensor_scalar(rrs[:, :].unsqueeze(2), rmv[:, :, 1:2], EPS, None, ALU.add).then_inc(rvar, 1)
            dve.wait_ge(rpow, 1)
            for c in range(T):
                for h in range(RH):
                    i = c * RH + h
                    ins = dve.tensor_scalar(yR[:, c, h * P:(h + 1) * P], ps[:, 4 + c, h * P:(h + 1) * P],
                                            rmv[:, i, 0:1], rrs[:, i:i + 1], ALU.subtract, ALU.mult)
                ins.then_inc(yR_norm, 1)
            w.upto(U["skv"] + 4)
            for h in range(RH):
                dve.wait_ge(mix_tr, DC + h + 1)
                ch.link(dve.tensor_scalar(ryt[:, h, :], ps[:, 4 + h, :], col("gng", h), col("gnb", h), ALU.mult, ALU.add))
                dve.wait_ge(b2c, 13 + h)
                dve.tensor_tensor(ryt[:, h, :], ryt[:, h, :], rg[:, h, :], ALU.mult).then_inc(yr_t, 1)
            for h in range(RH):
                dve.wait_ge(yr_hi, h + 1)
                dve.tensor_tensor(yrl[:, h, :], ryt[:, h, :], yrh[:, h, :].bitcast(F32), ALU.subtract).then_inc(yr_lo, 1)
            for t in range(T):
                dve.wait_ge(b2c, 17 + t)
                ch.wait()
                ch.link(dve.tensor_tensor(ssqr[:, :], sq[:, t, :], sq[:, t, :], ALU.mult))
                ch.mark(dve.tensor_reduce(sst[:, 0, t, 0:8], heads(ssqr[:, :]), AX.X, ALU.add))
            w.upto(U["gr0"] + 4)
            for t in range(T):
                dve.wait_ge(b2c, 21 + t)
                ch.wait()
                ch.link(dve.tensor_tensor(ssqr[:, 0:128], skv[:, t, 0:128], skv[:, t, 0:128], ALU.mult))
                ch.mark(dve.tensor_reduce(sst[:, 0, t, 8:10], heads(ssqr[:, 0:128]), AX.X, ALU.add))
            ch.wait()
            dve.tensor_scalar(sst[:, 1, :, :], sst[:, 0, :, :], 1.0 / HD, EPS, ALU.mult, ALU.add).then_inc(s_ss, 1)
            w.upto(U["gr0"] + 8)
            dve.wait_ge(s_pow, 1)
            for t in range(T):
                dve.tensor_tensor(heads(sq[:, t, :]), heads(sq[:, t, :]),
                                  sst[:, 2, t, 0:8].unsqueeze(2).broadcast_to([P, 8, HD]), ALU.mult)
                for r in range(2):
                    ins = dve.tensor_tensor(kd[:, t, :, r * HD:(r + 1) * HD], heads(skv[:, t, 0:128]),
                                            sst[:, 2, t, 8:10].unsqueeze(2).broadcast_to([P, SKV, HD]), ALU.mult)
            ins.then_inc(s_n, 1)
            for g in range(SKV):
                dve.wait_ge(s_tr, 5 + g)
                dve.tensor_scalar(skT[:, g, :], ps[:, g, :], col("skw"), None, ALU.mult).then_inc(skT_ready, 1)

            def logits(h):
                dve.wait_ge(fx_qk, NG_ * H1 + h + 1)
                dve.wait_ge(sbias_loaded, 16)
                if h >= 2:
                    dve.wait_ge(fx_t, H1 + h - 1)
                b_ = h % 2
                i1 = dve.tensor_tensor(sPb[:, b_, 0:128], ps[:, 0, 256:384], sbias[:, h, 128:256], ALU.add)
                i1 = dve.tensor_tensor(sPb[:, b_, 128:384], ps[:, 0, 0:256], sbias[:, h, :], ALU.add)
                i1 = dve.tensor_tensor(sPb[:, b_, 384:896].rearrange("p (i n) -> p i n", i=2),
                                       ps[:, 1, :].rearrange("p (i n) -> p i n", i=2),
                                       sbias[:, h:h + 1, :].broadcast_to([P, 2, 256]), ALU.add)
                i1.then_inc(sx_l, 1)
                dve.wait_ge(sx_l, h + 1)
                dve.tensor_reduce(sfst[:, 0, b_, 0:1], sPb[:, b_, 0:128], AX.X, ALU.max)
                ch.link(dve.tensor_reduce(sfst[:, 0, b_, 1:4], sPb[:, b_, 128:896].rearrange("p (i n) -> p i n", i=3),
                                          AX.X, ALU.max))
                dve.tensor_scalar(sfst[:, 1, b_, :], sfst[:, 0, b_, :], col("sink", h), -1.0, ALU.max, ALU.mult
                                  ).then_inc(fx_nm, 1)

            def transposed(h):
                dve.wait_ge(fx_t, H1 + h + 1)
                if h:
                    dve.wait_ge(fx_pv, H1 + h)
                dve.tensor_copy(sPT[:, 512:896], ps[:, 3, 0:384]).then_inc(fx_pD, 1)

            def normalize(h):
                b_ = h % 2
                dve.wait_ge(fx_exp, NG_ * H1 + h + 1)
                ch.link(dve.tensor_tensor(sfst[:, 2, b_, :], sfst[:, 2, b_, :], sfst[:, 3, b_, :], ALU.add))
                ch.link(dve.reciprocal(sfst[:, 4, b_, :], sfst[:, 2, b_, :]))
                dve.tensor_scalar(sPb[:, b_, 0:128], sPb[:, b_, 0:128], sfst[:, 4, b_, 0:1], None, ALU.mult)
                v3 = sPb[:, b_, 128:896].rearrange("p (i n) -> p i n", i=3)
                dve.tensor_tensor(v3, v3, sfst[:, 4, b_, 1:4].unsqueeze(2).broadcast_to([P, 3, 256]), ALU.mult
                                  ).then_inc(fx_pn, 1)

            def output(h):
                pr = h // 2
                dve.wait_ge(fx_hi, H1 // 2 + pr + 1)
                dve.tensor_tensor(ysl[:, pr, :], ps[:, 4 + pr % 2, :], ysh[:, pr, :].bitcast(F32),
                                  ALU.subtract).then_inc(fx_lo, 1)

            logits(0)
            for h in range(SH):
                if h:
                    transposed(h - 1)
                normalize(h)
                if h + 1 < SH:
                    logits(h + 1)
                if h and h % 2 == 0:
                    output(h - 1)
            transposed(SH - 1)
            output(SH - 1)
            w.upto(U["ro1"] + 8)

            def merge(b):
                for j in range(4):
                    dve.wait_ge(unit_used, U[f"ro{b}"] + 4)
                    if b:
                        dve.wait_ge(mix_lo, DC + 4)
                    dve.wait_ge(b2c, 36)
                    dve.tensor_tensor(t1[:, j, :], ps[:, j, :], gr[:, 4 * b + j, :], ALU.mult).then_inc(m_r, 1)
                for j in range(4):
                    dve.wait_ge(unit_used, U[f"so{b}"] + 4)
                    dve.wait_ge(b2c, 40)
                    if b:
                        dve.wait_ge(m_t, 4)
                    dve.tensor_tensor(t2[:, j, :], ps[:, 4 + j, :], gs[:, 4 * b + j, :], ALU.mult).then_inc(m_s, 1)
                    dve.wait_ge(m_r, 4 * b + j + 1)
                    dve.wait_ge(m_s, 4 * b + j + 1)
                    dve.tensor_tensor(t1[:, j, :], t1[:, j, :], t2[:, j, :], ALU.add).then_inc(m_t, 1)
                for j in range(4):
                    dve.wait_ge(mix_hi, DC + 4 * b + j + 1)
                    dve.tensor_tensor(MTl[:, 4 * b + j, :], t1[:, j, :], MTh[:, 4 * b + j, :].bitcast(F32),
                                      ALU.subtract).then_inc(mix_lo, 1)

            def residual2(name, s_, b):
                def make(t):
                    def piece():
                        dve.wait_ge(unit_used, FIRST[name] + UNITS[name])
                        dve.tensor_tensor(X[:, t, b * 512:(b + 1) * 512], X[:, t, b * 512:(b + 1) * 512],
                                          ps[:, 4 * s_ + t, :], ALU.add).then_inc(x_res, 1)
                    return piece
                return [make(t) for t in range(T)]

            merge(0)
            merge(1)
            w.upto(U["mo1"] + 8)
            w.upto(U["wr"] + 1)
            for p in residual2("mo0", 0, 0) + residual2("mo1", 1, 1):
                p()
            DVE_MOE(dve, w, ch)

        def POOL_B2(pool):
            pool.wait_ge(x_res, 16)
            pool.dma_start(DM[:, :, :, :], mats_d).then_inc(mats_loaded, 16)
            pool_norm(pool, 2)
            pool.wait_ge(rvar, 1)
            pool.tensor_tensor(rrs[:, :], rrs[:, :], small[:, 48:49].broadcast_to([P, T * RH]), ALU.pow).then_inc(rpow, 1)
            pool.wait_ge(ry_mm, T)
            pool.dma_start(sbias[:, :, :], bias_d).then_inc(sbias_loaded, 16)
            pool.wait_ge(s_ss, 1)
            pool.tensor_tensor(sst[:, 2, :, :], sst[:, 1, :, :], small[:, 48:49].unsqueeze(2).broadcast_to([P, T, 10]),
                               ALU.pow).then_inc(s_pow, 1)
            POOL_MOE(pool)

        def PE_MOE(pe):
            U = FIRST
            pe_norm(pe, 3, xn3, [(x_res, 24)])
            pe.wait_ge(ht_lo, 32)
            pe.wait_ge(lo_ready, U["wr"] + 1)
            w = U["wr"] % RING
            for t in range(T):
                for c in range(DC):
                    mm = mm3(pe, ps[:, 0, t * 36:(t + 1) * 36], HTh[:, c, t * P:(t + 1) * P], HTl[:, c, t * P:(t + 1) * P],
                             hi[:, w, c * 36:(c + 1) * 36], lo[:, w, c * 36:(c + 1) * 36], c == 0, c == DC - 1)
            mm.then_inc(unit_used, 1)
            pe.wait_ge(mb_ready, 1)
            pe.wait_ge(route_loaded, 48)
            for t in range(T + 1):
                for t_ in range(min(t, T - 1) + 1):
                    mm = pe.matmul(ps[:, 1, t * NE:(t + 1) * NE], tri[:, 0 if t_ == t else 1, :], Mb[:, t_, :],
                                   start=t_ == 0, stop=t_ == min(t, T - 1))
            mm.then_inc(rk_mm, 1)

            def gather(g, src, bank0, done):
                for b in range(2):
                    for j in range(2):
                        c = 4 * g + 2 * b + j
                        for t in range(T):
                            mm = pe.matmul(ps[:, bank0 + b, j * 2 * P:(j + 1) * 2 * P], src[:, t, c * P:(c + 1) * P],
                                           Sel[:, t, :], start=t == 0, stop=t == T - 1)
                    mm.then_inc(done, 1)

            pe.wait_ge(xg_lo, T)
            pe.wait_ge(xsel, 1)
            for g in range(2):
                if g:
                    pe.wait_ge(xt_h, 2)
                    pe.wait_ge(xt_l, 2)
                gather(g, XNh, 0, xg_mh)
                gather(g, XNl, 2, xg_ml)

            def body(n, par, h, h1, pp):
                pe.wait_ge(xt_h, h * 4 + 4)
                pe.wait_ge(xt_l, h * 4 + 4)
                if not (isinstance(n, int) and n == 0):
                    pe.wait_ge(e_h, n)
                for c in range(DC):
                    pe.wait_ge(lo_ready, n * 8 + (MOE_AT + c + 1))
                    w = (MOE_AT + c) % RING
                    rows_ = slice(par * P, (par + 1) * P)
                    mm3(pe, ps[:, 4, :], XTh[pp][:, c, rows_], XTl[pp][:, c, rows_], hi[:, w, :], lo[:, w, :], c == 0, c == DC - 1
                        ).then_inc(unit_used, 1)
                last = isinstance(n, int) and n == TILES - 1
                if not last:
                    pe.wait_ge(xsel, h + 2)
                    pe.wait_ge(xt_h, n * 2 + 4)
                    pe.wait_ge(xt_l, n * 2 + 4)
                    gather(par, XNh, 0, xg_mh)
                pe.wait_ge(e_h, n + 1)
                if not (isinstance(n, int) and n == 0):
                    pe.wait_ge(e_hT, n)
                for j in range(2):
                    tr = pe.transpose(ps[:, 5, j * P:(j + 1) * P], hid[:, j * P:(j + 1) * P], ident[:, :])
                tr.then_inc(e_tr, 1)
                if not last:
                    gather(par, XNl, 2, xg_ml)
                pe.wait_ge(e_hT, n + 1)
                pe.wait_ge(dn_full[par], h * 16 + 16)
                if not (isinstance(n, int) and n == 0):
                    pe.wait_ge(ye_a, n)
                    pe.wait_ge(ye_b, n)
                for hf in range(2):
                    for c in range(2):
                        mm = pe.matmul(ps[:, 6 + hf, :], hidT[:, c * P:(c + 1) * P], rawd[:, par, 2 * hf + c, :],
                                       start=c == 0, stop=c == 1)
                    mm.then_inc(dn_mm, 1)

            tiles(pe, body)
            PE_PLE(pe)

        def tiles(eng, body):
            for n in range(3):
                body(n, n % 2, n // 2, (n - 1) // 2, n // 2 % 2)
            with eng.Fori(0, (TILES - 7) // 4) as i:
                body(i * 4 + 3, 1, i * 2 + 1, i * 2 + 1, 1)
                body(i * 4 + 4, 0, i * 2 + 2, i * 2 + 1, 0)
                body(i * 4 + 5, 1, i * 2 + 2, i * 2 + 2, 0)
                body(i * 4 + 6, 0, i * 2 + 3, i * 2 + 2, 1)
            for n in range(TILES - 4, TILES):
                body(n, n % 2, n // 2, (n - 1) // 2, n // 2 % 2)

        def PE_PLE(pe):
            U = FIRST
            pe.wait_ge(p_lo, 1)
            pe.wait_ge(ye_a, TILES)
            pe.wait_ge(ye_b, TILES)
            for b in range(2):
                pe_tokens(pe, U[f"ple{b}"], 2, b, pTh, pTl)
            pe_norm(pe, 4, xn4, [(ple_done, 8)])
            pe.wait_ge(ht_lo, 36)
            pe_tokens(pe, U["pg0"], 8, 0, HTh, HTl, ready=(ht_lo, 32))
            pe_tokens(pe, U["pg1"], 8, 1, HTh, HTl)

        def ACT_MOE(act, w, ch):
            act_norm(act, 3, xn3, "nffn2")
            w.upto(MOE_AT + 8)
            for t in range(T):
                act.wait_ge(xg_f, t + 1)
                act.activation(XNh[:, t, :], xn3[:, t, :], ACT.Copy).then_inc(xg_hi, 1)
            act.wait_ge(r_d, 1)
            act.activation(R[:, 2, :, 0:4], R[:, 1, :, 0:4], ACT.Exp).then_inc(r_e, 1)
            act.wait_ge(r_d, 2)
            act.activation(R[:, 10, :, 0:1], R[:, 9, :, 0:1], ACT.Exp).then_inc(r_e, 1)

            def xt(k_, g, pp):
                for b in range(2):
                    act.wait_ge(xg_mh, k_ * 2 + (b + 1))
                    c = 4 * g + 2 * b
                    act.activation(XTh[pp][:, c:c + 2, :], ps[:, b, :].rearrange("p (c r) -> p c r", c=2), ACT.Copy
                                   ).then_inc(xt_h, 1)

            xt(0, 0, 0)
            xt(1, 1, 0)

            def body(n, par, h, h1, pp):
                last = isinstance(n, int) and n == TILES - 1
                if not (isinstance(n, int) and n == 0):
                    store(n, par, h1)
                if not last:
                    for c in range(6):
                        split1(act, n, c)
                act.wait_ge(unit_used, n * 8 + (MOE_AT + 8))
                if not (isinstance(n, int) and n == 0):
                    act.wait_ge(e_h, n)
                act.activation(esg[:, :], ps[:, 4, 0:EF], ACT.Silu).then_inc(e_sg, 1)
                if not last:
                    for c in range(6, 8):
                        split1(act, n, c)
                    xt(n + 2, par, 1 - pp)
                act.wait_ge(e_tr, n + 1)
                if not (isinstance(n, int) and n == 0):
                    act.wait_ge(dn_mm, n * 2)
                act.activation(hidT[:, :], ps[:, 5, 0:EF], ACT.Copy).then_inc(e_hT, 1)

            def store(n, par, h1):
                act.wait_ge(dn_mm, n * 2 - 1)
                if not isinstance(n, int) or n >= 3:
                    act.wait_ge(ye_st[1 - par], h1 * 16)
                act.activation(Ye[:, 1 - par, 0:512], ps[:, 6, :], ACT.Copy).then_inc(ye_a, 1)

            tiles(act, body)
            store(TILES, TILES % 2, TILES // 2)
            ACT_PLE(act, w)

        def split1(act, n, c):
            sl = (MOE_AT + c) % RING
            act.wait_ge(raw_full[sl], n * 16 + 16 * ((MOE_AT + c) // RING + 2))
            act.wait_ge(unit_used, n * 8 + (MOE_AT + c + 1))
            act.activation(hi[:, sl, :], raw[:, sl, :], ACT.Copy).then_inc(hi_ready, 1)

        def split2(dve, n, c):
            sl = (MOE_AT + c) % RING
            dve.wait_ge(hi_ready, n * 8 + (MOE_AT + 8 + c + 1))
            dve.tensor_tensor(lo[:, sl, :], raw[:, sl, :], hi[:, sl, :].bitcast(F32), ALU.subtract).then_inc(lo_ready, 1)

        def ACT_PLE(act, w):
            U = FIRST
            w.n = U["ple0"]
            act.wait_ge(p_loaded, 16)
            act.activation(pTh[:, :, :], pTf[:, :, :], ACT.Copy).then_inc(p_hi, 1)
            w.upto(U["ple1"] + 2)
            for b in range(2):
                act.wait_ge(unit_used, U[f"ple{b}"] + 2)
                for t in range(T):
                    ins = act.activation((psg, psq)[b][:, t, :], ps[:, 4 * b + t, :], ACT.Square,
                                         accum_out=small[:, 24 + 2 * t + b:25 + 2 * t + b])
            ins.then_inc(ys_ss, 1)
            act_norm(act, 4, xn4, "nple")
            w.upto(U["pg1"] + 8)
            for b in range(2):
                act.wait_ge(unit_used, U[f"pg{b}"] + 8)
                for t in range(T):
                    if b:
                        act.wait_ge(out_ready, t + 1)
                    act.activation(psg[:, t, :], ps[:, 4 * b + t, :], ACT.Sigmoid).then_inc(p_sg, 1)

        def DVE_MOE(dve, w, ch):
            U = FIRST
            dve_norm(dve, 3, xn3, "nffn2")
            w.upto(MOE_AT + 8)
            dve.wait_ge(unit_used, U["wr"] + 1)
            dve.wait_ge(route_loaded, 48)
            L = R[:, 0, :, :]
            ch.link(dve.tensor_tensor(L, ps[:, 0, 0:4 * 36].rearrange("p (t n) -> p t n", t=T),
                                      rb[:, 0:36].unsqueeze(1).broadcast_to([P, T, 36]), ALU.add))

            def first_of(v, n, k0, idx0=36):
                m = R[:, k0, :, 0:1]
                oh = R[:, k0 + 1, :, 0:n]
                ch.link(dve.tensor_reduce(m, v, AX.X, ALU.max))
                ch.link(dve.tensor_tensor(oh, v, m.broadcast_to([P, T, n]), ALU.is_ge))
                ch.link(dve.tensor_tensor(oh, oh, rb[:, 36:36 + n].unsqueeze(1).broadcast_to([P, T, n]), ALU.mult))
                ch.link(dve.tensor_reduce(R[:, k0 + 2, :, 0:1], oh, AX.X, ALU.max))
                ch.link(dve.tensor_tensor(oh, oh, R[:, k0 + 2, :, 0:1].broadcast_to([P, T, n]), ALU.is_equal))
                return m, oh

            gmax, g1 = first_of(L[:, :, 0:4], 4, 11)
            dve.tensor_tensor(R[:, 1, :, 0:4], L[:, :, 0:4], gmax.broadcast_to([P, T, 4]), ALU.subtract).then_inc(r_d, 1)
            dve.wait_ge(route_loaded, 48)
            dve.wait_ge(n_tr, 32)
            for t in range(T):
                dve.tensor_tensor(xn3[:, t, :], xn3[:, t, :], grow[:, :], ALU.mult).then_inc(xg_f, 1)
            for t in range(T):
                dve.wait_ge(xg_hi, t + 1)
                dve.tensor_tensor(XNl[:, t, :], xn3[:, t, :], XNh[:, t, :].bitcast(F32), ALU.subtract).then_inc(xg_lo, 1)
            pg = R[:, 3, :, 0:32].rearrange("p t (g e) -> p t g e", g=NG)
            ch.link(dve.tensor_tensor(pg, L[:, :, 4:36].rearrange("p t (g e) -> p t g e", g=NG),
                                      g1.unsqueeze(3).broadcast_to([P, T, NG, EG]), ALU.mult))
            E = R[:, 4, :, 0:8]
            ch.link(dve.tensor_reduce(E, R[:, 3, :, 0:32].rearrange("p t (g e) -> p t e g", g=NG), AX.X, ALU.add))
            m1, o1 = first_of(E, 8, 14)
            E2 = R[:, 5, :, 0:8]
            ch.link(dve.scalar_tensor_tensor(E2, o1, NEG, E, ALU.mult, ALU.add))
            m2, o2 = first_of(E2, 8, 17)
            dve.tensor_tensor(R[:, 9, :, 0:1], m2, m1, ALU.subtract).then_inc(r_d, 1)
            dve.wait_ge(r_e, 1)
            ch.link(dve.tensor_reduce(R[:, 6, :, 0:1], R[:, 2, :, 0:4], AX.X, ALU.add))
            dve.wait_ge(r_e, 2)
            ch.link(dve.scalar_tensor_tensor(R[:, 6, :, 1:2], R[:, 10, :, 0:1], 1.0, R[:, 6, :, 0:1], ALU.add, ALU.mult))
            W1, W2 = R[:, 6, :, 2:3], R[:, 6, :, 3:4]
            ch.link(dve.reciprocal(W1, R[:, 6, :, 1:2]))
            ch.link(dve.tensor_tensor(W2, W1, R[:, 10, :, 0:1], ALU.mult))
            O = (R[:, 20, :, 0:NE], R[:, 21, :, 0:NE])
            for k_, o in enumerate((o1, o2)):
                for g in range(NG):
                    ins = dve.tensor_tensor(R[:, 20 + k_, :, 8 * g:8 * g + 8], o, g1[:, :, g:g + 1].broadcast_to([P, T, 8]),
                                            ALU.mult)
            ch.link(ins)
            dve.tensor_tensor(Mb[:, :, :], O[0], O[1], ALU.add).then_inc(mb_ready, 1)
            dve.wait_ge(rk_mm, 1)
            rank = R[:, 23, :, 0:NE]
            ch.mark(dve.tensor_copy(rank, ps[:, 1, 0:T * NE].rearrange("p (t e) -> p t e", t=T)))
            cnt, ov, inc, base, one = [ovw[:, i, :] for i in range(5)]
            ch.link(dve.tensor_copy(cnt, ps[:, 1, T * NE:(T + 1) * NE]))
            ch.mark(dve.memset(one, 1.0))
            ch.link(dve.tensor_scalar(ov, cnt, float(P + 1), None, ALU.is_ge))
            for q_ in (2, 3):
                ch.link(dve.scalar_tensor_tensor(ov, cnt, float(P * q_ + 1), ov, ALU.is_ge, ALU.add))
            ch.link(dve.tensor_tensor_scan(inc, one, ov, 0.0, ALU.mult, ALU.add))
            ch.link(dve.tensor_tensor(base, inc, ov, ALU.subtract))
            for k_ in range(2):
                rk, bs, ex, qq, fl = [rq_w[:, i, :].unsqueeze(2) for i in range(5)]
                for dst, v in ((rk, rank), (bs, base.unsqueeze(1).broadcast_to([P, T, NE])),
                               (ex, rb[:, 44:76].unsqueeze(1).broadcast_to([P, T, NE]))):
                    ch.link(dve.tensor_tensor(R[:, 22, :, 0:NE], O[k_], v, ALU.mult))
                    ch.link(dve.tensor_reduce(dst, R[:, 22, :, 0:NE], AX.X, ALU.add))
                ch.link(dve.tensor_scalar(fl, rk, float(P), None, ALU.is_ge))
                ch.link(dve.scalar_tensor_tensor(qq, rk, float(2 * P), fl, ALU.is_ge, ALU.add))
                ch.link(dve.scalar_tensor_tensor(qq, rk, float(3 * P), qq, ALU.is_ge, ALU.add))
                ch.link(dve.scalar_tensor_tensor(bs, bs, NE - 1.0, qq, ALU.add, ALU.add))
                ch.link(dve.tensor_tensor(bs, bs, ex, ALU.subtract))
                ch.link(dve.tensor_tensor(bs, bs, fl, ALU.mult))
                ch.link(dve.tensor_tensor(bs, bs, ex, ALU.add))
                ch.link(dve.tensor_tensor(bs, bs, qq, ALU.subtract))
                ch.link(dve.scalar_tensor_tensor(yrow[:, k_, :].unsqueeze(2), bs, float(P), rk, ALU.mult, ALU.add))
            dve.tensor_copy(yidx[:, :, :], yrow[:, :, :]).then_inc(yidx_ready, 1)

            def select(p):
                k_ = [0]

                def link(ins):
                    k_[0] += 1
                    ins.then_inc(sel_c, 1)
                    dve.wait_ge(sel_c, p * 3 + k_[0])

                if isinstance(p, int) and p == 0:
                    link(dve.tensor_copy(yrel[:, :, :], yrow[:, :, :]))
                else:
                    dve.wait_ge(xg_ml, p * 4)
                    link(dve.tensor_scalar(yrel[:, :, :], yrel[:, :, :], -2.0 * P, None, ALU.add))
                io = rb[:, 76:76 + 2 * P].unsqueeze(1).broadcast_to([P, T, 2 * P])
                link(dve.tensor_tensor(Se1[:, :, :], io, yrel[:, 0, :].unsqueeze(2).broadcast_to([P, T, 2 * P]), ALU.is_equal))
                link(dve.tensor_tensor(Se2[:, :, :], io, yrel[:, 1, :].unsqueeze(2).broadcast_to([P, T, 2 * P]), ALU.is_equal))
                dve.tensor_tensor(Sel[:, :, :], Se1[:, :, :], Se2[:, :, :], ALU.add).then_inc(xsel, 1)

            select(0)
            ch.link(dve.tensor_tensor(eow[:, 0:7, :], rb[:, 44:51].unsqueeze(2).broadcast_to([P, 7, NE]),
                                      inc.unsqueeze(1).broadcast_to([P, 7, NE]), ALU.is_ge))
            ch.link(dve.tensor_reduce(eow[:, 7, 0:7].unsqueeze(2), eow[:, 0:7, :], AX.X, ALU.add))
            dve.tensor_scalar(eov[:, 0:7], eow[:, 7, 0:7], NE - 1.0, None, ALU.min).then_inc(eov_ready, 1)

            def xt(k_, g, pp):
                for b in range(2):
                    dve.wait_ge(xg_ml, k_ * 2 + (b + 1))
                    c = 4 * g + 2 * b
                    dve.tensor_copy(XTl[pp][:, c:c + 2, :], ps[:, 2 + b, :].rearrange("p (c r) -> p c r", c=2)
                                    ).then_inc(xt_l, 1)

            xt(0, 0, 0)
            xt(1, 1, 0)

            def store(n, par, h1):
                dve.wait_ge(dn_mm, n * 2)
                if not isinstance(n, int) or n >= 3:
                    dve.wait_ge(ye_st[1 - par], h1 * 16)
                dve.tensor_copy(Ye[:, 1 - par, 512:1024], ps[:, 7, :]).then_inc(ye_b, 1)

            def body(n, par, h, h1, pp):
                last = isinstance(n, int) and n == TILES - 1
                if not (isinstance(n, int) and n == 0):
                    store(n, par, h1)
                early = 6 if par else 2
                if not last:
                    if par == 0:
                        select(h + 1)
                    for c in range(early):
                        split2(dve, n, c)
                dve.wait_ge(e_sg, n + 1)
                if not (isinstance(n, int) and n == 0):
                    dve.wait_ge(e_tr, n)
                dve.tensor_tensor(hid[:, :], esg[:, :], ps[:, 4, EF:2 * EF], ALU.mult).then_inc(e_h, 1)
                if not last:
                    for c in range(early, 8):
                        split2(dve, n, c)
                    xt(n + 2, par, 1 - pp)

            tiles(dve, body)
            store(TILES, TILES % 2, TILES // 2)
            for k_ in range(2):
                dve.wait_ge((yg0, yg1)[k_], 16 * T)
                if k_:
                    dve.wait_ge(x_res, 28)
                for t in range(T):
                    dve.scalar_tensor_tensor(X[:, t, :], YG[:, k_ * T + t, :], R[:, 6, t, 2 + k_:3 + k_], X[:, t, :],
                                             ALU.mult, ALU.add).then_inc(x_res, 1)
            DVE_PLE(dve, w, ch)

        def DVE_PLE(dve, w, ch):
            U = FIRST
            w.n = U["ple0"]
            dve.wait_ge(p_hi, 1)
            dve.tensor_tensor(pTl[:, :, :], pTf[:, :, :], pTh[:, :, :].bitcast(F32), ALU.subtract).then_inc(p_lo, 1)
            w.upto(U["ple1"] + 2)
            dve.wait_ge(ys_ss, 1 + 1)
            ch.link(dve.tensor_tensor(small[:, 32:36], small[:, 24:32:2], small[:, 25:32:2], ALU.add))
            dve.tensor_scalar(small[:, 36:40], small[:, 32:36], 1.0 / D, EPS, ALU.mult, ALU.add).then_inc(ys_ms, 1)
            dve.wait_ge(ys_rs, 1 + 1)
            dve.wait_ge(prow_loaded, 16)
            for b in range(2):
                for t in range(T):
                    dve.scalar_tensor_tensor(ple[:, t, b * 512:(b + 1) * 512], ps[:, 4 * b + t, :], small[:, 40 + t:41 + t],
                                             prow[:, b * 512:(b + 1) * 512], ALU.mult, ALU.mult).then_inc(ple_done, 1)
            dve_norm(dve, 4, xn4, "nple")
            w.upto(U["pg1"] + 8)
            for b in range(2):
                for t in range(T):
                    cc = slice(b * 512, (b + 1) * 512)
                    dve.wait_ge(p_sg, 4 * b + t + 1)
                    dve.wait_ge(ple_done, 8)
                    ch.link(dve.tensor_tensor(ple[:, t, cc], ple[:, t, cc], psg[:, t, :], ALU.mult))
                    dve.tensor_tensor(X[:, t, cc], X[:, t, cc], ple[:, t, cc], ALU.add).then_inc(out_ready, 1)

        def POOL_MOE(pool):
            pool.wait_ge(x_res, 24)
            pool.dma_start(rb[:, :], rb_d).then_inc(route_loaded, 16)
            pool.dma_start(grow[:, :], rows_d[0]).then_inc(route_loaded, 16)
            pool.dma_start(tri[:, :, :], tri_d).then_inc(route_loaded, 16)
            pool_norm(pool, 3)

            def store(n, par, dst):
                pool.wait_ge(ye_a, n + 1)
                pool.wait_ge(ye_b, n + 1)
                pool.dma_start(dst, Ye[:, par, :]).then_inc(ye_st[par], 16)

            with pool.Fori(0, TILES // 2) as i:
                for par in range(2):
                    store(i * 2 + par, par, ye_d[bass.ds(i * (2 * P) + par * P, P), :])
            store(TILES - 1, 0, ye_d[(TILES - 1) * P:TILES * P, :])
            pool.wait_ge(yidx_ready, 1)
            pool.wait_ge(ye_st[0], 16 * (TILES // 2 + 1))
            pool.wait_ge(ye_st[1], 16 * (TILES // 2))
            for k_ in range(2):
                for t in range(T):
                    pool.indirect_dma_start(YG[:, k_ * T + t, :], None, ye_d,
                                            bass.IndirectOffsetOnAxis(ap=yidx[:, k_, t:t + 1], axis=0)
                                            ).then_inc((yg0, yg1)[k_], 16)
            pool.dma_start(pTf[:, :, :], pT_d).then_inc(p_loaded, 16)
            pool.wait_ge(ys_ms, 1 + 1)
            pool.tensor_tensor(small[:, 40:44], small[:, 36:40], small[:, 48:52], ALU.pow).then_inc(ys_rs, 1)
            pool_norm(pool, 4)

        @block.sync
        def _(sp):
            sp.dma_start(X[:, :, :], x.rearrange("(t p) d -> p t d", p=P)).then_inc(x_loaded, 16)
            for c in range(RING):
                sp.dma_start(raw[:, c, :], wstream[c]).then_inc(raw_full[c], 16)

            def reload(u0, n=RING):
                for u in range(u0, u0 + n):
                    sp.wait_ge(lo_ready, u + 1 - RING)
                    sp.dma_start(raw[:, u % RING, :], wstream[u if u < MOE_AT else u - XU]).then_inc(raw_full[u % RING], 16)

            rounds = MOE_AT // RING
            with sp.Fori(1, rounds) as i:
                for c in range(RING):
                    sp.wait_ge(lo_ready, i * RING + (c + 1 - RING))
                    sp.dma_start(raw[:, c, :], wstream[bass.ds(i * RING + c, 1)].rearrange("a p n -> (a p) n")
                                 ).then_inc(raw_full[c], 16)
            reload(rounds * RING, MOE_AT - rounds * RING)
            def gate_up(n, src):
                for c in range(8):
                    u = MOE_AT + c
                    sp.wait_ge(lo_ready, n * 8 + (u + 1 - RING))
                    sp.dma_start(raw[:, u % RING, :], src[c]).then_inc(raw_full[u % RING], 16)

            def down(n, par, src):
                if not isinstance(n, int) or n >= 2:
                    sp.wait_ge(dn_mm, n * 2 - 2)
                sp.dma_start(rawd[:, par, :, :], src).then_inc(dn_full[par], 16)

            def expert(n, par, e):
                w_e = wexp[bass.ds(e, 1)].rearrange("a c p n -> (a c) p n")
                gate_up(n, w_e)
                down(n, par, w_e[8:12].rearrange("c p n -> p c n"))

            gate_up(0, wexp[0])
            sp.wait_ge(x_res, 24)
            down(0, 0, wexp[0, 8:12].rearrange("c p n -> p c n"))
            gate_up(1, wexp[1])
            down(1, 1, wexp[1, 8:12].rearrange("c p n -> p c n"))
            with sp.Fori(0, NE // 2 - 1) as i:
                for k_ in range(2):
                    expert(i * 2 + (2 + k_), k_, i * 2 + (2 + k_))
            sp.wait_ge(eov_ready, 1)
            for j in range(TILES - NE):
                e = sp.value_load(eov[0:1, j:j + 1], min_val=0, max_val=NE - 1)
                expert(NE + j, j % 2, e)
            sp.wait_ge(dn_mm, 2 * TILES)
            sp.dma_start(prow[:, :], rows_d[1]).then_inc(prow_loaded, 16)
            reload(FIRST["ple0"], NU - FIRST["ple0"])
            for t in range(T):
                sp.wait_ge(out_ready, 4 + t + 1)
                sp.dma_start(out[t * P:(t + 1) * P, :], X[:, t, :]).then_inc(out_stored, 16)
            sp.wait_ge(out_stored, 16 * T)

        @block.tensor
        def _(pe):
            U = FIRST
            pe.wait_ge(misc_loaded, 80)
            pe_norm(pe, 0, xn, [])
            for b in range(3):
                if b == 0:
                    pe.wait_ge(ht_lo, 4)
                elif b == 1:
                    pe.wait_ge(ht_lo, 8)
                else:
                    pe.wait_ge(cvD, 4)
                pe_features(pe, U[f"xbc{b}"], 8, b % 2, HTh, HTl, ready=(ht_lo, 0) if b == 0 else None)
            for b in range(2):
                pe.wait_ge(cvD, 8 + 4 * b)
                pe_tokens(pe, U[f"z{b}"], 8, (b + 1) % 2, HTh, HTl)
            pe.wait_ge(z_done, 4)
            for u in range(2):
                pe.wait_ge(lo_ready, U["dtf"] + u + 1)
                w = (U["dtf"] + u) % RING
                for j in range(4):
                    c = 4 * u + j
                    mm = mm3(pe, ps[:, 4, :], hi[:, w, j * P:(j + 1) * P], lo[:, w, j * P:(j + 1) * P],
                             HTh[:, c, :], HTl[:, c, :], c == 0, c == DC - 1)
                mm.then_inc(unit_used, 1)
            pe.wait_ge(z_done, 8)
            pe.wait_ge(xbc_ready, 12)
            for m in range(10):
                if m >= 4:
                    pe.wait_ge(xs_ready, m - 3)
                for i in range(4):
                    if m < 8:
                        t, kk = m // 2, 4 * (m % 2) + i
                    else:
                        t, kk = 2 * (m - 8) + i // 2, 8 + i % 2
                    tr = pe.transpose(ps[:, m % 4, i * P:(i + 1) * P], xbcT[:, kk, t * P:(t + 1) * P], ident[:, :])
                tr.then_inc(xs_tr, 1)
            for g in range(2):
                for c in range(T):
                    mm = pe.matmul(ps[:, 5 + g, c * P:(c + 1) * P], xbcT[:, 8 + g, c * P:(c + 1) * P],
                                   xbcT[:, 10 + g, c * P:(c + 1) * P], start=True, stop=True)
                mm.then_inc(cb_mm, 1)
            pe.wait_ge(dte_d, 1)
            for i, r in enumerate((3, 2, 5)):
                for t in range(T):
                    tr = pe.transpose(ps[:, 7, (i * T + t) * 32:(i * T + t + 1) * 32], rows[0:32, r, t * P:(t + 1) * P],
                                      ident[0:32, 0:32])
            tr.then_inc(tok_mm, 1)
            pe.wait_ge(ddg, 1)
            pe.wait_ge(dtf_v, 1)
            pe.matmul(ps[:, 4, 0:4 * H1], rows[0:H1, 6, 0:P], rows[0:H1, 4, 0:4 * H1],
                      start=True, stop=True).then_inc(dec_mm, 1)

            pe.wait_ge(br_lo, 2)
            pe.wait_ge(sel_ready, 1)
            for g in range(2):
                pe.wait_ge(xdw, 2 * (g + 1))
                pe.wait_ge(xs_ready, 10)
                if g == 1:
                    pe.wait_ge(y_done, 4)
                    pe.wait_ge(seg, 8)
                    pe.wait_ge(yo_done, 3)
                for c in range(3):
                    pe.matmul(ps[:, c, :], Btok[:, c, g * P:(g + 1) * P], xw[:, c, :],
                              start=True, stop=True).then_inc(st_mm, 1)
                for c in range(1, 4):
                    pe.wait_ge(st_ready, 3 * (g + 1))
                    pe.matmul(ps[:, c, :], xbcT[:, 10 + g, c * P:(c + 1) * P], st[:, c - 1, :],
                              start=True, stop=True).then_inc(yo_mm, 1)

                def bcast(i):
                    h = 8 * g + i
                    if i == 0:
                        pe.wait_ge(st_ready, 3 * (g + 1))
                    if i == 1:
                        pe.wait_ge(yo_done, 3 * g + 1)
                    if i >= 2:
                        pe.wait_ge(seg, h - 1)
                    b = i % 2
                    pe.matmul(ps[:, b, :], sel[0:64, h, :], BR[0:64, :], start=True, stop=False)
                    for c in range(T):
                        mm = pe.matmul(ps[:, b, c * P:(c + 1) * P], identb[:, :], maskT[:, :],
                                       start=False, stop=(c == T - 1))
                    mm.then_inc(bc_mm, 1)

                bcast(0)
                bcast(1)
                for i in range(8):
                    h = 8 * g + i
                    if i + 2 < 8:
                        bcast(i + 2)
                    pe.wait_ge(sc_ready, h + 1)
                    if i == 0:
                        pe.wait_ge(dec_cp, 1)
                        pe.wait_ge(tok_ready, 1)
                        pe.wait_ge(cb_ready, 2)
                    for c in range(T):
                        mm = pe.matmul(ps[:, 4 + c, i * HD:(i + 1) * HD], SC[:, h % 4, c * P:(c + 1) * P],
                                       xd[:, c, i * HD:(i + 1) * HD], start=True, stop=True)
                    mm.then_inc(yd_mm, 1)
            pe.wait_ge(ys_n, 1)
            pe.wait_ge(yo_done, 6)
            for c in range(DC):
                for t in range(T):
                    tr = pe.transpose(ps[:, c, t * P:(t + 1) * P], Y1[:, t, c * P:(c + 1) * P], ident[:, :])
                tr.then_inc(mix_tr, 1)

            for b in range(6):
                if b < 2:
                    pe.wait_ge(mix_lo, 4 + 4 * b)
                else:
                    pe.wait_ge(qkv_copied, 4 * (b - 1))
                pe_tokens(pe, U["qqkkvv"[b] + str(b % 2)], 8, b % 2, HTh, HTl)
            for c in range(DC):
                for i, src in enumerate((q, k)):
                    if c >= 4:
                        pe.wait_ge((qT_done, kT_done)[i], c - 3)
                    elif c == 0:
                        pe.wait_ge(qk_n, 1)
                        pe.wait_ge(qkv_copied, 24)
                    for t in range(T):
                        tr = pe.transpose(ps[:, 4 * i + c % 4, t * P:(t + 1) * P], src[:, t, c * P:(c + 1) * P],
                                          ident[:, :])
                    tr.then_inc(qk_tr, 1)

            def scores(h, g):
                r = slice(HD * (h % 2), HD * (h % 2) + HD)
                if h == 0:
                    pe.wait_ge(sel_z, 1)
                    pe.wait_ge(qT_done, 8)
                    pe.wait_ge(kT_done, 8)
                else:
                    pe.wait_ge(fx_exp, NG_ * (h - 1) + g + 1)
                bank, parts = FG[g]
                for i, o in parts:
                    n = (i + 1) * P
                    pe.matmul(ps[:, bank, o:o + n], qT[r, h // 2, i * P:(i + 1) * P], kT[r, h // 2, 0:n],
                              start=True, stop=False)
                    pe.matmul(ps[:, bank, o:o + n], sel[:, h, :], BR[:, 0:n], start=False, stop=False)
                    mm = pe.matmul(ps[:, bank, o + n - P:o + n], identb[:, :], maskL[:, :], start=False, stop=True)
                mm.then_inc(fx_qk, 1)

            def values(h):
                pe.wait_ge(fx_pA, h + 1)
                pe.wait_ge(fx_pD, h + 1)
                pr = h // 2
                if pr >= 2:
                    pe.wait_ge(fx_lo, pr - 1)
                for j in range(T):
                    mm = pe.matmul(ps[HD * (h % 2):HD * (h % 2) + HD, 6 + pr % 2, j * P:S], v[:, j, h * HD:(h + 1) * HD],
                                   PT[:, PTO[j]:PTO[j] + S - j * P], start=(j == 0), stop=(j == T - 1))
                mm.then_inc(fx_pv, 1)

            for g in range(NG_):
                scores(0, g)
            for h in range(H1):
                if h + 1 < H1:
                    scores(h + 1, 0)
                    scores(h + 1, 1)
                if h:
                    values(h - 1)
                if h + 1 < H1:
                    scores(h + 1, 2)
                for g in range(NG_):
                    pe.wait_ge(fx_pn, NG_ * h + g + 1)
                    if g == 0 and h:
                        pe.wait_ge(fx_pA, h)
                        pe.wait_ge(fx_pD, h)
                    for i, _o in FG[g][1]:
                        for j in range(i + 1):
                            bank, o = PTB[j]
                            tr = pe.transpose(ps[:, bank, o + (i - j) * P:o + (i - j + 1) * P],
                                              Pb[:, h % 2, FOFF[i] + j * P:FOFF[i] + (j + 1) * P], ident[:, :])
                tr.then_inc(fx_t, 1)
            values(H1 - 1)

            pe.wait_ge(fx_lo, 8)
            for b in range(2):
                pe_tokens(pe, U[f"out{b}"], 8, b, MIXh0, MIXl0, last=False)
                pe_tokens(pe, U[f"out{b}"] + 8, 8, b, MIXh1, MIXl1, first=False)
            pe_norm(pe, 1, xnF, [(x_res, 8)])
            u = U["up0"]
            pe.wait_ge(ht_lo, 12)
            pe_features(pe, u, 8, 0, HTh, HTl, ready=(ht_lo, 8))
            with pe.Fori(0, 5) as i:
                for s_ in range(2):
                    st_ = (1 + s_) % 2
                    pe.wait_ge(ffD, i * 8 + (4 * s_ + 1))
                    pe_features(pe, i * 16 + (u + 8 + 8 * s_), 8, st_, HTh, HTl, slot=u + 8 + 8 * s_)
            for b in range(2):
                pe.wait_ge(ffD, 1 + 4 * (10 + b))
                pe_tokens(pe, U[f"down{b}"], FF // P, (1 + b) % 2, gh, gl, ready=(ff_lo, 1) if b == 0 else None)
            PE_B2(pe)

        class Splits:

            def __init__(self, eng, one):
                self.eng, self.one, self.n = eng, one, 0

            def upto(self, n):
                if n > self.n:
                    self.one(self.eng, self.n, n - self.n)
                    self.n = n

            def beside(self, n, pieces):
                pieces = list(pieces)
                total = max(1, n - self.n)
                for i in range(total):
                    self.upto(self.n + 1)
                    while pieces and len(pieces) * total > (total - 1 - i) * (len(pieces) + 4):
                        pieces.pop(0)()
                for p in pieces:
                    p()

        @block.scalar
        def _(act):
            U = FIRST
            ch = Chain(act, act_c)
            w = Splits(act, act_split)
            for dst, src in ((ident, ident_d), (cst, cst_d), (identb, identb_d), (maskT, maskT_d), (maskL, maskL_d)):
                act.dma_start(dst[:, :], src).then_inc(misc_loaded, 16)
            act.wait_ge(misc_loaded, 80)
            act_norm(act, 0, xn, "nmix")
            w.upto(U["xbc0"] + 16)
            ch.mark(act.activation(small[:, 18:19], col("qw"), ACT.Copy, scale=HD ** -0.5))
            ch.mark(act.activation(small[:, 19:20], col("sqw"), ACT.Copy, scale=HD ** -0.5))

            def silu_x(kk):
                act.wait_ge(cvD, kk + 1)
                act.activation(xbcT[:, kk, :], acc[:, kk % 4, :], ACT.Silu).then_inc(xbc_ready, 1)

            def conv_x(b, m):
                def piece():
                    kk = 4 * b + m
                    act.wait_ge(unit_used, U[f"xbc{b}"] + 8)
                    if kk >= 4:
                        act.wait_ge(xbc_ready, kk - 3)
                    act.activation(acc[:, m, :], ps[:, 4 * (b % 2) + m, :], ACT.Identity,
                                   scale=col("cw", 4 * kk + 3), bias=col("cb", kk)).then_inc(cvA, 1)
                    if kk:
                        silu_x(kk - 1)
                return piece

            def silu_z(b, t):
                def piece():
                    act.wait_ge(unit_used, U[f"z{b}"] + 8)
                    act.activation(zs[:, t, b * 512:(b + 1) * 512], ps[:, 4 * ((b + 1) % 2) + t, :],
                                   ACT.Silu).then_inc(z_done, 1)
                return piece

            w.beside(U["z0"], [conv_x(0, m) for m in range(4)])
            w.beside(U["z1"], [conv_x(1, m) for m in range(4)])
            w.beside(U["dtf"], [conv_x(2, m) for m in range(4)] + [lambda: silu_x(11)])
            w.beside(U["q0"], [silu_z(0, t) for t in range(4)])
            for t in range(T):
                silu_z(1, t)()

            act.wait_ge(sel_loaded, 16)
            act.activation(sel[:, :, :], selF[:, :, :], ACT.Copy).then_inc(sel_ready, 1)
            act.wait_ge(dtf_v, 2)
            act.activation(rows[:, 2, :], rows[:, 1, :], ACT.Exp).then_inc(dtf_e, 1)
            act.activation(small[:, 16:17], col("alog"), ACT.Exp).then_inc(dtf_e, 1)
            act.wait_ge(dtf_s, 1)
            act.activation(rows[:, 1, :], rows[:, 3, :], ACT.Ln).then_inc(dtf_l, 1)
            for m in range(10):
                act.wait_ge(xs_tr, m + 1)
                if m < 8:
                    dst = xs[:, m // 2, (m % 2) * 512:(m % 2 + 1) * 512]
                    src = ps[:, m % 4, :]
                else:
                    dst = Btok[:, 2 * (m - 8):2 * (m - 8) + 2, :]
                    src = ps[:, m % 4, :].rearrange("p (t n) -> p t n", t=2)
                act.activation(dst, src, ACT.Copy).then_inc(xs_ready, 1)
            act.wait_ge(dtf_cs, 5)
            act.activation(BR[:, :], rows[:, 2, :], ACT.Copy).then_inc(br_hi, 1)
            for c in range(T):
                end = rows[0:32, 2, c * P + P - 1:c * P + P]
                act.activation(rows[0:32, 5, c * P:(c + 1) * P], rows[0:32, 2, c * P:(c + 1) * P], ACT.Exp,
                               bias=end, scale=-1.0).then_inc(dte_a, 1)
            act.activation(small[0:H1, 20:24], rows[0:H1, 2, P - 1:S:P], ACT.Exp).then_inc(dte_a, 1)
            act.wait_ge(tok_ready, 1)
            act.activation(tok[:, 3, :, :], tok[:, 1, :, :], ACT.Exp).then_inc(etok, 1)
            w.upto(U["q0"] + 8)
            for h in range(H1):
                act.wait_ge(seg, h + 1)
                act.activation(SC[:, h % 4, :], SC[:, h % 4, :], ACT.Exp).then_inc(dcy, 1)
            act.wait_ge(y_done, 8)
            for g in range(2):
                for t in range(T):
                    ins = act.activation((xw, xd)[g][:, t, :], Y1[:, t, g * 512:(g + 1) * 512], ACT.Square,
                                         accum_out=small[:, 24 + 2 * t + g:25 + 2 * t + g])
            ins.then_inc(ys_ss, 1)
            for c in range(DC):
                act.wait_ge(mix_tr, c + 1)
                act.activation(MIXh0[:, c, :], ps[:, c, :], ACT.Identity, scale=col("nssd", c)).then_inc(mix_hi, 1)

            def copy_qkv(b, t):
                def piece():
                    act.wait_ge(unit_used, U["qqkkvv"[b] + str(b % 2)] + 8)
                    if b == 0 and t == 0:
                        act.wait_ge(mix_tr, 8)
                    act.activation((q, k, v)[b // 2][:, t, (b % 2) * 512:(b % 2 + 1) * 512], ps[:, 4 * (b % 2) + t, :],
                                   ACT.Copy).then_inc(qkv_copied, 1)
                return piece

            w.upto(U["q1"] + 8)
            for b in range(4):
                w.beside(U["qqkkvv"[b + 2] + str(b % 2)] + 8, [copy_qkv(b, t) for t in range(T)])
            act.wait_ge(qk_ss, 1)
            act.activation(qst3[:, :, :, :], qst2[:, :, :, :], ACT.Ln).then_inc(qk_ln, 1)
            act.wait_ge(qk_ln, 1)
            act.activation(qst[:, :, :, :], qst3[:, :, :, :], ACT.Exp, scale=-0.5).then_inc(qk_ln, 1)
            w.beside(U["out0"], [copy_qkv(4, t) for t in range(T)])
            for t in range(T):
                copy_qkv(5, t)()
            w.upto(U["out0"] + 8)
            for c in range(DC):
                act.wait_ge(qk_tr, 2 * c + 1)
                act.activation(qT[:, c, :], ps[:, c % 4, :], ACT.Identity, scale=small[:, 18:19]).then_inc(qT_done, 1)

            def weights(h, g):
                act.wait_ge(fx_nm, NG_ * h + g + 1)
                if h >= 2:
                    act.wait_ge(fx_t, h - 1)
                bank, parts = FG[g]
                for i, o in parts:
                    n = (i + 1) * P
                    ins = act.activation(Pb[:, h % 2, FOFF[i]:FOFF[i] + n], ps[:, bank, o:o + n], ACT.Exp,
                                         bias=fst[:, 0, h % 2, i:i + 1], accum_out=fst[:, 1, h % 2, i:i + 1])
                ins.then_inc(fx_exp, 1)

            def transposed(h):
                act.wait_ge(fx_t, h + 1)
                if h:
                    act.wait_ge(fx_pv, h)
                act.activation(PT[:, 0:512], ps[:, 3, :], ACT.Copy).then_inc(fx_pA, 1)

            def output(h):
                act.wait_ge(fx_pv, h + 1)
                act.activation(MIXh1[:, h // 2, :], ps[:, 6 + h // 2 % 2, :], ACT.Copy).then_inc(fx_hi, 1)

            for g in range(NG_):
                weights(0, g)
            for h in range(H1):
                if h:
                    transposed(h - 1)
                if h + 1 < H1:
                    weights(h + 1, 0)
                    weights(h + 1, 1)
                if h and h % 2 == 0:
                    output(h - 1)
                if h + 1 < H1:
                    weights(h + 1, 2)
            transposed(H1 - 1)
            output(H1 - 1)
            w.upto(U["out0"] + 16)
            w.upto(U["out1"] + 16)
            w.upto(U["up0"] + 8)
            act_norm(act, 1, xnF, "nffn")
            w.upto(U["up1"] + 8)

            def split8(u0):
                for c in range(RING):
                    sl = (U["up0"] + c) % RING
                    act.wait_ge(raw_full[sl], (u0 + c - sl) * 2 + 16)
                    act.wait_ge(unit_used, u0 + (c - RING + 1))
                    act.activation(hi[:, sl, :], raw[:, sl, :], ACT.Copy).then_inc(hi_ready, 1)
                    yield

            def conv_f(b, s_, m):
                f = b * 2 + (m if m < 2 else FF // P + m - 2)
                act.activation(facc[:, m, :], ps[:, 4 * s_ + m, :], ACT.Identity,
                               scale=cst[:, bass.ds(COLS["fw"][0] + f * 3 + 2, 1)] if not isinstance(f, int) else col("fw", 3 * f + 2),
                               bias=cst[:, bass.ds(COLS["fb"][0] + f, 1)] if not isinstance(f, int) else col("fb", f)
                               ).then_inc(ffA, 1)

            def post_f(b, s_, pump):
                act.wait_ge(unit_used, b * 8 + (U["up0"] + 8))
                act.wait_ge(ff_g, b * 2 + 1)
                for m in range(4):
                    conv_f(b, s_, m)
                    pump()
                for m in range(2):
                    act.wait_ge(ffD, b * 4 + (m + 2))
                    act.activation(fsg[:, m, :], facc[:, m, :], ACT.Silu).then_inc(ff_sg, 1)
                    pump()
                for m in range(2):
                    act.wait_ge(ff_g, b * 2 + (m + 2))
                    if isinstance(b, int):
                        dst = gh[:, 2 * b + m, :]
                    else:
                        dst = gh[:, bass.ds(b * 2 + m, 1), :]
                    act.activation(dst, fg[:, m, :] if isinstance(b, int) else fg[:, m:m + 1, :], ACT.Copy).then_inc(ff_hi, 1)
                    pump()

            def steps(gen):
                def pump():
                    next(gen, None)
                return pump

            def drain(gen):
                for _ in gen:
                    pass

            with act.Fori(0, 5) as i:
                for s_ in range(2):
                    b = i * 2 + s_
                    gen = split8(i * 16 + (U["up2"] + 8 * s_))
                    post_f(b, s_, steps(gen))
                    drain(gen)
            w.n = U["up2"] + 80
            assert w.n == U["down0"] + 8
            post_f(10, 0, lambda: None)
            w.upto(U["rq"] + 8)
            ACT_B2(act, w, ch)

        @block.vector
        def _(dve):
            U = FIRST
            ch = Chain(dve, dve_c)
            w = Splits(dve, dve_split)
            dve.wait_ge(misc_loaded, 80)
            dve.memset(small[:, 56:57], 0.0).then_inc(ffD, 1)
            dve.memset(small[:, 57:58], 0.0).then_inc(ff_g, 1)
            dve_norm(dve, 0, xn, "nmix")
            w.upto(U["xbc0"] + 16)

            def conv_x(b, m):
                def piece():
                    kk = 4 * b + m
                    dve.wait_ge(cvA, kk + 1)
                    for j in (2, 1, 0):
                        sh = 3 - j
                        ins = dve.scalar_tensor_tensor(acc[:, m, sh:], ps[:, 4 * (b % 2) + m, 0:S - sh],
                                                       col("cw", 4 * kk + j), acc[:, m, sh:], ALU.mult, ALU.add)
                        if j:
                            ch.link(ins)
                    ins.then_inc(cvD, 1)
                return piece

            w.beside(U["z0"], [conv_x(0, m) for m in range(4)])
            w.beside(U["z1"], [conv_x(1, m) for m in range(4)])
            w.beside(U["dtf"], [conv_x(2, m) for m in range(4)])
            w.upto(U["q0"])
            V, E0, E, S1, Q, RC, ONE = range(7)
            dve.wait_ge(n_tr, 8)
            ch.link(dve.memset(rows[:, ONE, :], 1.0))
            dve.wait_ge(unit_used, U["q0"])
            dve.tensor_scalar(rows[:, V, :], ps[:, 4, :], col("dtb"), col("sgn"), ALU.add, ALU.mult).then_inc(dtf_v, 1)
            dve.wait_ge(dtf_v, 1)
            dve.scalar_tensor_tensor(rows[:, E0, :], rows[:, V, :], -1.0, rows[:, V, :], ALU.mult, ALU.min
                                     ).then_inc(dtf_v, 1)
            dve.wait_ge(dtf_e, 2)
            dve.tensor_scalar(rows[:, S1, :], rows[:, E, :], 1.0, None, ALU.add).then_inc(dtf_s, 1)
            dve.wait_ge(dtf_s, 1)
            ch.mark(dve.scalar_tensor_tensor(rows[:, Q, :], rows[:, S1, :], 1.0, rows[:, E, :], ALU.subtract, ALU.subtract))
            ch.link(dve.reciprocal(rows[:, RC, :], rows[:, S1, :]))
            ch.link(dve.tensor_tensor(rows[:, Q, :], rows[:, Q, :], rows[:, RC, :], ALU.mult))
            dve.wait_ge(dtf_l, 1)
            ch.link(dve.tensor_tensor(rows[:, E0, :], rows[:, E0, :], rows[:, Q, :], ALU.subtract))
            ch.link(dve.scalar_tensor_tensor(rows[:, S1, :], rows[:, V, :], 0.0, rows[:, E0, :], ALU.max, ALU.add))
            ch.link(dve.tensor_scalar(small[:, 17:18], small[:, 16:17], col("asg"), None, ALU.mult))
            ch.link(dve.tensor_scalar(rows[:, Q, :], rows[:, S1, :], small[:, 17:18], None, ALU.mult))
            for c in range(T):
                cc = slice(c * P, (c + 1) * P)
                dve.tensor_tensor_scan(rows[0:64, 2, cc], rows[0:64, ONE, cc], rows[0:64, Q, cc], 0.0,
                                       ALU.mult, ALU.add).then_inc(dtf_cs, 1)
            dve.tensor_tensor_scan(rows[64:128, 2, :], rows[64:128, ONE, :], rows[64:128, Q, :], 0.0,
                                   ALU.mult, ALU.add).then_inc(dtf_cs, 1)
            dve.wait_ge(dtf_cs, 5)
            dve.wait_ge(br_hi, 1)
            for r in (slice(32, 64), slice(96, 128)):
                dve.tensor_tensor(BR[r, :], rows[r, 2, :], BR[r, :].bitcast(F32), ALU.subtract).then_inc(br_lo, 1)
            dve.wait_ge(dte_a, 5)
            dve.tensor_tensor(rows[0:32, 5, :], rows[0:32, 5, :], rows[0:32, S1, :], ALU.mult).then_inc(dte_d, 1)
            for c in range(T):
                ins = dve.tensor_scalar(rows[0:H1, Q, c * H1:(c + 1) * H1], ident[0:H1, 0:H1],
                                        small[0:H1, 20 + c:21 + c], None, ALU.mult)
            ins.then_inc(ddg, 1)
            for g in range(2):
                dve.wait_ge(cb_mm, g + 1)
                dve.wait_ge(sel_ready, 1)
                dve.tensor_copy(cbS[:, g, :], ps[:, 5 + g, :]).then_inc(cb_ready, 1)
            dve.wait_ge(tok_mm, 1)
            dve.tensor_copy(tok[:, 0:3, :, :].rearrange("p a t h -> p (a t h)"), ps[:, 7, 0:384]).then_inc(tok_ready, 1)
            dve.wait_ge(dec_mm, 1)
            dve.tensor_copy(decB, ps[:, 4, 0:4 * H1]).then_inc(dec_cp, 1)
            w.upto(U["q0"] + 8)
            dve.wait_ge(xs_ready, 10)
            dve.wait_ge(etok, 1)
            dve.wait_ge(tok_ready, 1)
            dve.wait_ge(dec_cp, 1)

            def heads(a):
                return a.rearrange("p (h e) -> p h e", h=8)

            def per_head(a):
                return a.unsqueeze(2).broadcast_to([P, 8, HD])

            for g in range(2):
                G = slice(g * 512, (g + 1) * 512)
                hs = slice(8 * g, 8 * g + 8)
                if g:
                    dve.wait_ge(yd_mm, 8)
                    dve.wait_ge(yo_mm, 3)
                for t in range(T):
                    i1 = dve.tensor_tensor(heads(xw[:, t, :]), heads(xs[:, t, G]), per_head(tok[:, 2, t, hs]), ALU.mult)
                i1.then_inc(xdw, 1)
                for t in range(T):
                    i1 = dve.tensor_tensor(heads(xd[:, t, :]), heads(xs[:, t, G]), per_head(tok[:, 0, t, hs]), ALU.mult)
                i1.then_inc(xdw, 1)
                if g:
                    dve.wait_ge(yo_mm, 3)
                dve.wait_ge(st_mm, 3 * g + 1)
                dve.tensor_copy(st[:, 0, :], ps[:, 0, :]).then_inc(st_ready, 1)
                for c in (1, 2):
                    dve.wait_ge(st_ready, 3 * g + c)
                    ch.link(dve.tensor_tensor(heads(st[:, c, :]), heads(st[:, c - 1, :]),
                                              per_head(decB[:, c * H1 + 8 * g:c * H1 + 8 * g + 8]), ALU.mult))
                    dve.wait_ge(st_mm, 3 * g + c + 1)
                    dve.tensor_tensor(st[:, c, :], st[:, c, :], ps[:, c, :], ALU.add).then_inc(st_ready, 1)
                dve.wait_ge(xs_tr, 8)
                for t in range(T):
                    n = ch.mark(dve.tensor_tensor(heads(Y1[:, t, G]), heads(xs[:, t, G]),
                                                  per_head(col("dskip", 8 * g, 8)), ALU.mult))
                for c in range(1, T):
                    dve.wait_ge(yo_mm, 3 * g + c)
                    if c > 1:
                        ch.wait()
                    dve.tensor_tensor(heads(yt[:, :]), heads(ps[:, c, :]), per_head(tok[:, 3, c, hs]),
                                      ALU.mult).then_inc(yo_done, 1)
                    dve.wait_ge(yo_done, 3 * g + c)
                    ch.wait(n)
                    ch.mark(dve.tensor_tensor(Y1[:, c, G], Y1[:, c, G], yt[:, :], ALU.add))
                def seg_h(h):
                    dve.wait_ge(bc_mm, h + 1)
                    if h >= 4:
                        dve.wait_ge(yd_mm, h - 3)
                    dve.tensor_tensor(SC[:, h % 4, :].rearrange("p (c l) -> p c l", c=T),
                                      ps[:, h % 2, :].rearrange("p (c l) -> p c l", c=T),
                                      tok[:, 1, :, h:h + 1].broadcast_to([P, T, P]), ALU.subtract).then_inc(seg, 1)

                def sc_h(h):
                    dve.wait_ge(dcy, h + 1)
                    dve.wait_ge(cb_ready, 2)
                    dve.tensor_tensor(SC[:, h % 4, :], SC[:, h % 4, :], cbS[:, g, :], ALU.mult).then_inc(sc_ready, 1)

                seg_h(8 * g)
                for h in range(8 * g, 8 * g + 8):
                    if h + 1 < 8 * g + 8:
                        seg_h(h + 1)
                    sc_h(h)
                dve.wait_ge(yd_mm, 8 * g + 8)
                for t in range(T):
                    ch.wait()
                    ch.link(dve.tensor_tensor(Y1[:, t, G], Y1[:, t, G], ps[:, 4 + t, :], ALU.add))
                    dve.tensor_tensor(Y1[:, t, G], Y1[:, t, G], zs[:, t, G], ALU.mult).then_inc(y_done, 1)
            dve.wait_ge(ys_ss, 1)
            dve.tensor_scalar(small[:, 32:40], small[:, 24:32], 1.0 / 512, EPS, ALU.mult, ALU.add).then_inc(ys_ms, 1)
            dve.wait_ge(ys_rs, 1)
            for t in range(T):
                for g in range(2):
                    ins = dve.tensor_scalar(Y1[:, t, g * 512:(g + 1) * 512], Y1[:, t, g * 512:(g + 1) * 512],
                                            small[:, 40 + 2 * t + g:41 + 2 * t + g], None, ALU.mult)
            ins.then_inc(ys_n, 1)
            for c in range(DC):
                dve.wait_ge(mix_hi, c + 1)
                dve.scalar_tensor_tensor(MIXl0[:, c, :], ps[:, c, :], col("nssd", c), MIXh0[:, c, :].bitcast(F32),
                                         ALU.mult, ALU.subtract).then_inc(mix_lo, 1)

            def squares(b, t):
                def piece():
                    src = (q, k)[b // 2][:, t, (b % 2) * 512:(b % 2 + 1) * 512]
                    dve.wait_ge(qkv_copied, 4 * b + t + 1)
                    ch.wait()
                    ch.link(dve.tensor_tensor(sqr[:, t % 2, :], src, src, ALU.mult))
                    ch.mark(dve.tensor_reduce(qst[:, b // 2, t, 8 * (b % 2):8 * (b % 2) + 8],
                                              heads(sqr[:, t % 2, :]), AX.X, ALU.add))
                return piece

            w.upto(U["q1"] + 8)
            for b in range(4):
                w.beside(U["qqkkvv"[b + 2] + str(b % 2)] + 8, [squares(b, t) for t in range(T)])
            ch.wait()
            dve.tensor_scalar(qst2[:, :, :, :], qst[:, :, :, :], 1.0 / HD, EPS, ALU.mult, ALU.add).then_inc(qk_ss, 1)
            dve.wait_ge(qk_ln, 2)
            dve.wait_ge(qk_ss, 1)
            ch.link(dve.tensor_tensor(qst3[:, :, :, :], qst[:, :, :, :], qst[:, :, :, :], ALU.mult))
            ch.link(dve.tensor_tensor(qst3[:, :, :, :], qst3[:, :, :, :], qst2[:, :, :, :], ALU.mult))
            ch.link(dve.tensor_scalar(qst3[:, :, :, :], qst3[:, :, :, :], -0.5, 1.5, ALU.mult, ALU.add))
            ch.link(dve.tensor_tensor(qst3[:, :, :, :], qst3[:, :, :, :], qst[:, :, :, :], ALU.mult))

            def scale_qk(i, t):
                def piece():
                    src = (q, k)[i][:, t, :].rearrange("p (h e) -> p h e", h=H1)
                    ins = dve.tensor_tensor(src, src, qst3[:, i, t, :].unsqueeze(2).broadcast_to([P, H1, HD]), ALU.mult)
                    if (i, t) == (1, T - 1):
                        ins.then_inc(qk_n, 1)
                return piece

            w.beside(U["out0"], [scale_qk(i, t) for i in range(2) for t in range(T)])
            w.upto(U["out0"] + 8)
            for c in range(DC):
                dve.wait_ge(qk_tr, 2 * c + 2)
                dve.tensor_scalar(kT[:, c, :], ps[:, 4 + c % 4, :], col("kw"), None, ALU.mult).then_inc(kT_done, 1)

            def maxima(h, g):
                dve.wait_ge(fx_qk, NG_ * h + g + 1)
                if h >= 2:
                    dve.wait_ge(fx_exp, NG_ * (h - 1))
                bank, parts = FG[g]
                for i, o in parts:
                    ins = dve.tensor_reduce(fst[:, 0, h % 2, i:i + 1], ps[:, bank, o:o + (i + 1) * P], AX.X, ALU.max,
                                            negate=True)
                ins.then_inc(fx_nm, 1)

            def normalize(h, g):
                dve.wait_ge(fx_exp, NG_ * h + g + 1)
                parts = FG[g][1]
                for i, _o in parts:
                    ins = dve.reciprocal(fst[:, 2, h % 2, i:i + 1], fst[:, 1, h % 2, i:i + 1])
                ch.link(ins)
                for i, _o in parts:
                    ins = dve.tensor_scalar(Pb[:, h % 2, FOFF[i]:FOFF[i] + (i + 1) * P], Pb[:, h % 2, FOFF[i]:FOFF[i] + (i + 1) * P],
                                            fst[:, 2, h % 2, i:i + 1], None, ALU.mult)
                ins.then_inc(fx_pn, 1)

            def head(h):
                maxima(h, 0)
                maxima(h, 1)
                normalize(h, 0)
                normalize(h, 1)
                maxima(h, 2)
                normalize(h, 2)

            def transposed(h):
                dve.wait_ge(fx_t, h + 1)
                if h:
                    dve.wait_ge(fx_pv, h)
                dve.tensor_copy(PT[:, 512:1024], ps[:, 4, :])
                dve.tensor_copy(PT[:, 1024:1280], ps[:, 5, 0:256]).then_inc(fx_pD, 1)

            def output(h):
                pr = h // 2
                dve.wait_ge(fx_hi, pr + 1)
                dve.tensor_tensor(MIXl1[:, pr, :], ps[:, 6 + pr % 2, :], MIXh1[:, pr, :].bitcast(F32),
                                  ALU.subtract).then_inc(fx_lo, 1)

            head(0)
            for h in range(H1):
                if h:
                    transposed(h - 1)
                if h + 1 < H1:
                    head(h + 1)
                if h and h % 2 == 0:
                    output(h - 1)
            transposed(H1 - 1)
            output(H1 - 1)

            def residual(name, s_, b):
                def make(t):
                    def piece():
                        dve.wait_ge(unit_used, FIRST[name] + UNITS[name])
                        dve.tensor_tensor(X[:, t, b * 512:(b + 1) * 512], X[:, t, b * 512:(b + 1) * 512],
                                          ps[:, 4 * s_ + t, :], ALU.add).then_inc(x_res, 1)
                    return piece
                return [make(t) for t in range(T)]

            w.upto(U["out0"] + 16)
            w.upto(U["out1"] + 8)
            w.beside(U["out1"] + 16, residual("out0", 0, 0))
            w.upto(U["up0"] + 8)
            for p in residual("out1", 1, 1):
                p()
            dve_norm(dve, 1, xnF, "nffn")
            w.upto(U["up1"] + 8)

            def split8(u0):
                for c in range(RING):
                    sl = (U["up0"] + c) % RING
                    dve.wait_ge(hi_ready, u0 + (c + 1))
                    dve.tensor_tensor(lo[:, sl, :], raw[:, sl, :], hi[:, sl, :].bitcast(F32), ALU.subtract
                                      ).then_inc(lo_ready, 1)
                    yield

            def post_f(b, s_, pump):
                for m in range(4):
                    f = b * 2 + (m if m < 2 else FF // P + m - 2)
                    dve.wait_ge(ffA, b * 4 + (m + 1))
                    for j in (1, 0):
                        sh = 2 - j
                        wcol = col("fw", 3 * f + j) if isinstance(f, int) else cst[:, bass.ds(COLS["fw"][0] + f * 3 + j, 1)]
                        ins = dve.scalar_tensor_tensor(facc[:, m, sh:], ps[:, 4 * s_ + m, 0:S - sh], wcol,
                                                       facc[:, m, sh:], ALU.mult, ALU.add)
                        if j:
                            ins.then_inc(ff_c, 1)
                            pump()
                            dve.wait_ge(ff_c, b * 4 + (m + 1))
                    ins.then_inc(ffD, 1)
                for m in range(2):
                    dve.wait_ge(ff_sg, b * 2 + (m + 1))
                    dve.wait_ge(ffD, b * 4 + 5)
                    dve.wait_ge(ff_lo, b * 2 + 1)
                    dve.tensor_tensor(fg[:, m, :], fsg[:, m, :], facc[:, 2 + m, :], ALU.mult).then_inc(ff_g, 1)
                    pump()
                for m in range(2):
                    dve.wait_ge(ff_hi, b * 2 + (m + 1))
                    if isinstance(b, int):
                        dve.tensor_tensor(gl[:, 2 * b + m, :], fg[:, m, :], gh[:, 2 * b + m, :].bitcast(F32),
                                          ALU.subtract).then_inc(ff_lo, 1)
                    else:
                        dve.tensor_tensor(gl[:, bass.ds(b * 2 + m, 1), :], fg[:, m:m + 1, :],
                                          ghF[:, bass.ds(b * 2 + m, 1), :], ALU.subtract).then_inc(ff_lo, 1)
                    pump()

            ghF = gh[:, :, :].bitcast(F32)
            dve.memset(small[:, 58:59], 0.0).then_inc(ff_lo, 1)
            with dve.Fori(0, 5) as i:
                for s_ in range(2):
                    gen = split8(i * 16 + (U["up2"] + 8 * s_))
                    post_f(i * 2 + s_, s_, lambda: next(gen, None))
                    for _ in gen:
                        pass
            w.n = U["up2"] + 80
            post_f(10, 0, lambda: None)
            w.upto(U["down1"] + 8)
            w.beside(U["down1"] + 16, residual("down0", 1, 0))
            w.upto(U["rq"] + 8)
            for p in residual("down1", 0, 1):
                p()
            DVE_B2(dve, w, ch)

        @block.gpsimd
        def _(pool):
            pool.memset(small[:, 12:16], -0.5).then_inc(pool_c, 1)
            pool.memset(small[:, 48:56], -0.5).then_inc(pool_c, 1)
            pool.wait_ge(pool_c, 2)
            pool_norm(pool, 0)
            pool.dma_start(selF[:, :, :], sel_d).then_inc(sel_loaded, 16)
            pool.wait_ge(ys_ms, 1)
            pool.tensor_tensor(small[:, 40:48], small[:, 32:40], small[:, 48:56], ALU.pow).then_inc(ys_rs, 1)
            pool.wait_ge(bc_mm, 16)
            pool.memset(sel[0:64, :, :].bitcast(F32), 0.0).then_inc(sel_z, 1)
            pool_norm(pool, 1)
            POOL_B2(pool)

        block_cm.__exit__(None, None, None)


def _columns(inputs):
    f = lambda n: np.asarray(inputs[n], np.float32)
    out = np.zeros((P, NCST), np.float32)

    def put(name, a):
        c0, n = COLS[name]
        out[:a.shape[0], c0:c0 + n] = a

    def chunks(a):
        return a.reshape(-1, P).T

    def twice(a):
        return np.concatenate([a, a])[:, None]

    put("nmix", chunks(f("norm_mix_w")[0]))
    put("nffn", chunks(f("norm_ffn_w")[0]))
    put("nmix2", chunks(f("mix_norm_g_2")[0]))
    put("nffn2", chunks(f("ffn_norm_g_2")[0]))
    put("nple", chunks(f("ple_gate_norm_g_2")[0]))
    put("nssd", chunks(f("ssd_norm_w")[0]))
    put("cw", f("ssd_conv_w")[0].reshape(4, 12, P).transpose(2, 1, 0).reshape(P, 48))
    put("cb", chunks(f("ssd_conv_b")[0]))
    put("fw", f("ffn_conv_w")[0].reshape(3, 44, P).transpose(2, 1, 0).reshape(P, 132))
    put("fb", chunks(f("ffn_conv_b")[0]))
    put("qw", twice(f("fox_q_norm_w")[0]))
    put("kw", twice(f("fox_k_norm_w")[0]))
    put("sqw", twice(f("q_norm_g_2")[0]))
    put("skw", twice(f("k_norm_g_2")[0]))
    c = {n: COLS[n][0] for n in COLS}
    for r in (0, 32):
        out[r:r + H1, c["dtb"]] = f("ssd_dt_bias")[0]
        out[r:r + H1, c["sgn"]] = 1
        out[r:r + H1, c["alog"]] = f("ssd_a_log")[0]
        out[r:r + H1, c["asg"]] = -1
        out[64 + r:64 + r + H1, c["dtb"]] = f("fox_f_bias")[0]
        out[64 + r:64 + r + H1, c["sgn"]] = -1
        out[64 + r:64 + r + H1, c["asg"]] = 1
    put("dskip", np.broadcast_to(f("ssd_d")[0], (P, H1)))
    put("gng", chunks(f("ret_gn_g_2")[0]))
    put("gnb", chunks(f("ret_gn_b_2")[0]))
    put("sink", np.broadcast_to(f("attn_sinks_2")[0], (P, SH)))
    j = np.arange(P)
    put("zeta", np.exp((P - 1.0 - j)[:, None] * LOG_GAMMA[None, :]) * P ** -0.5)
    return out


def _units(inputs):
    f = lambda n: np.asarray(inputs[n], np.float32)[0]
    w = np.zeros((NU - XU, P, 512), np.float32)

    def put(name, cols):
        kk = cols.shape[0] // P
        u = FIRST[name] - (XU if FIRST[name] > MOE_AT else 0)
        w[u:u + kk, :, :cols.shape[1]] = cols.reshape(kk, P, -1)

    w_in = f("w_in")
    z, xbc, dt, q, k, v, fg = np.split(w_in, [1024, 2560, 2576, 3600, 4624, 5648], axis=1)
    for n, a in (("z", z), ("xbc", xbc), ("q", q), ("k", k), ("v", v)):
        for b in range(a.shape[1] // 512):
            put(f"{n}{b}", a[:, b * 512:(b + 1) * 512])
    for u in range(2):
        for j in range(4):
            rows = slice((4 * u + j) * P, (4 * u + j + 1) * P)
            o = w[FIRST["dtf"] + u, :, j * P:(j + 1) * P]
            for c, a in ((0, dt), (32, dt), (64, fg), (96, fg)):
                o[:, c:c + H1] = a[rows]
    wo = f("w_out")
    up, down = f("w_up"), f("w_down")
    for b in range(2):
        put(f"out{b}", wo[:, b * 512:(b + 1) * 512])
        put(f"down{b}", down[:, b * 512:(b + 1) * 512])
    for b in range(FF // 256):
        put(f"up{b}", np.concatenate([up[:, b * 256:(b + 1) * 256], up[:, FF + b * 256:FF + (b + 1) * 256]], axis=1))
    w2 = f("w_in_2")
    for i, n in enumerate(("rq", "rk", "rv", "rg", "sq")):
        put(n, w2[:, i * 512:(i + 1) * 512])
    skv = w2[:, 2560:2816].reshape(4, 2, P, 256)
    w[FIRST["skv"]:FIRST["skv"] + 4] = skv.transpose(0, 2, 1, 3).reshape(4, P, 512)
    for i, n in enumerate(("gr0", "gr1", "gs0", "gs1")):
        put(n, w2[:, 2816 + i * 512:2816 + (i + 1) * 512])
    for b in range(2):
        for n, a in (("ro", "w_ret_o_2"), ("so", "w_swa_o_2"), ("mo", "w_out_2"), ("ple", "w_ple_2"), ("pg", "w_ple_gate_2")):
            put(f"{n}{b}", f(a)[:, b * 512:(b + 1) * 512])
    r = np.concatenate([f("w_router_group_2"), f("w_router_expert_2")], axis=1).reshape(DC, P, 36)
    w[FIRST["wr"], :, :DC * 36] = r.transpose(1, 0, 2).reshape(P, DC * 36)
    return w


def _experts(inputs):
    f = lambda n: np.asarray(inputs[n], np.float32)[0]
    w = np.empty((NE, 12, P, 512), np.float32)
    w[:, :8, :, :EF] = f("w_exp_gate_2").reshape(NE, 8, P, EF)
    w[:, :8, :, EF:] = f("w_exp_up_2").reshape(NE, 8, P, EF)
    w[:, 8:] = f("w_exp_down_2").reshape(NE, 2, P, 2, 512).transpose(0, 3, 1, 2, 4).reshape(NE, 4, P, 512)
    return w


def _arrays(inputs):
    bf16 = mybir.dt.np(BF16)

    f = lambda n: np.asarray(inputs[n], np.float32)
    j, i = np.arange(P)[:, None], np.arange(P)[None, :]
    diff = (i - j).astype(np.float64)
    dm = np.where((diff >= 0)[:, None, :], np.exp(np.maximum(diff, 0)[:, None, :] * LOG_GAMMA[None, :, None]), 0.0) * P ** -0.5
    xi = np.broadcast_to(np.exp((np.arange(P) + 1.0)[None, :] * LOG_GAMMA[:, None])[None], (P, RH, P))
    mats = np.stack([dm, xi], axis=1).astype(np.float32)
    rel = np.arange(P)[:, None] + P - np.arange(2 * P)[None, :]
    slopes = np.exp2(-8.0 * np.arange(1, SH + 1) / SH)
    bias = np.where(((rel >= 0) & (rel < P))[:, None, :], -slopes[None, :, None] * rel[:, None, :].astype(np.float64), NEG)
    rb = np.zeros((P, 76 + 2 * P), np.float32)
    rb[:, 76:] = np.arange(2 * P)
    rb[:, 0:4] = f("b_router_group_2")[0]
    rb[:, 4:36] = f("b_router_expert_2")[0]
    rb[:, 36:44] = 8 - np.arange(8)
    rb[:, 44:76] = np.arange(32)
    tri = np.stack([(j < i), np.ones((P, P), bool)], axis=1)
    return {
        "x": f("x")[0], "cst": _columns(inputs),
        "rows": np.stack([np.broadcast_to(f("ffn_norm_g_2")[0], (P, D)), np.broadcast_to(f("ple_norm_g_2")[0], (P, D))]),
        "mats": mats, "bias": bias.astype(np.float32), "ident": np.eye(P, dtype=np.float32),
        "identb": np.eye(P).astype(bf16),
        "maskT": np.where(j > i, NEG, 0.0).astype(bf16),
        "maskL": np.where(i > j, NEG, 0.0).astype(bf16),
        "sel": np.broadcast_to((np.arange(P) % 32)[:, None, None] == np.arange(H1)[None, :, None], (P, H1, P)).astype(np.float32),
        "rb": rb, "tri": tri.astype(bf16),
        "pT": np.ascontiguousarray(f("p_2")[0, 0].T).reshape(2, P, S).transpose(1, 0, 2),
        "wstream": _units(inputs), "wexp": _experts(inputs),
    }


def kernel(**inputs):
    import concourse.bacc as _bacc
    from concourse.bass_utils import run_bass_kernel_spmd as _run

    nc = _bacc.Bacc("TRN2", target_bir_lowering=False, num_devices=1)
    arrays, args = {}, []
    for name, a in _arrays(inputs).items():
        a = np.ascontiguousarray(a)
        arrays[f"in_{name}"] = a
        args.append(nc.dram_tensor(f"in_{name}", a.shape, mybir.dt.from_np(a.dtype), kind="ExternalInput").ap())
    args.append(nc.dram_tensor("out_dram", (S, D), F32, kind="ExternalOutput").ap())
    bass_two_blocks(nc, *args)
    r = _run(nc, [arrays], core_ids=[0])
    return r.results[0]["out_dram"].reshape(1, S, D)
```

```python
from contextlib import ExitStack

import numpy as np

import concourse.bass as bass
from concourse import mybir

F32 = mybir.dt.float32
F32R = mybir.dt.float32r
BF16 = mybir.dt.bfloat16
I32 = mybir.dt.int32
ALU = mybir.AluOpType
ACT = mybir.ActivationFunctionType
AX = mybir.AxisListType

P = 128
S = 512
T = S // P
D = 1024
DC = D // P
EPS = 1e-6
NEG = -1e30

HD = 64
H1 = 16
NS = 128
XBC = D + 4 * NS
FF = 2816
RH = 4
SH, SKV = 8, 2
NG, EG = 4, 8
NE = NG * EG
EF = 256
TILES = NE + 2 * S // P - 1
RING = 8

PLAN = (
    [("xbc0", 8), ("dtf", 2), ("z0", 8), ("xbc1", 8), ("xbc2", 8), ("z1", 8)]
    + [(f"{n}{b}", 8) for n in "qkv" for b in range(2)]
    + [(f"out{b}", 16) for b in range(2)]
    + [(f"up{b}", 8) for b in range(FF // 256)] + [(f"down{b}", FF // P) for b in range(2)]
    + [(n, 8) for n in ("rq", "rk", "rv", "rg", "sq")] + [("skv", 4)]
    + [(f"g{n}{b}", 8) for n in "rs" for b in range(2)]
    + [(f"{n}{b}", 4) for b in range(2) for n in ("ro", "so")]
    + [(f"mo{b}", 8) for b in range(2)] + [("wr", 1)]
    + [(f"ple{b}", 2) for b in range(2)] + [("moe", TILES * 8)] + [(f"pg{b}", 8) for b in range(2)]
)
FIRST, UNITS = {}, {}
_at = 0
for _name, _n in PLAN:
    FIRST[_name], UNITS[_name] = _at, _n
    _at += _n
NU = _at
MOE_AT = FIRST["moe"]
XU = TILES * 8

COLS = {}
_at = 0
for _name, _n in (("nmix", DC), ("nffn", DC), ("nmix2", DC), ("nffn2", DC), ("nple", DC), ("nssd", DC),
                  ("cw", 12 * 4), ("cb", 12), ("fw", 44 * 3), ("fb", 44), ("qw", 1), ("kw", 1),
                  ("sqw", 1), ("skw", 1), ("dtb", 1), ("sgn", 1), ("alog", 1), ("asg", 1),
                  ("dskip", H1), ("gng", RH), ("gnb", RH), ("sink", SH), ("zeta", RH)):
    COLS[_name] = (_at, _n)
    _at += _n
NCST = _at

LOG_GAMMA = np.log1p(-np.exp2(-5.0 - np.arange(RH)))


class Chain:

    def __init__(self, eng, sem):
        self.eng, self.sem, self.n = eng, sem, 0

    def mark(self, ins):
        self.n += 1
        ins.then_inc(self.sem, 1)
        return self.n

    def wait(self, n=None):
        self.eng.wait_ge(self.sem, self.n if n is None else n)

    def link(self, ins):
        self.mark(ins)
        self.wait()


def bass_two_blocks(nc, x, cst_d, rows_d, mats_d, bias_d, ident_d, identb_d, maskT_d, maskL_d, sel_d, rb_d, tri_d,
                    pT_d, wstream, wexp, out):
    ctx = ExitStack()
    with ctx:
        def sem(name):
            return ctx.enter_context(nc.semaphore(name))

        base = 16512

        def at(name, shape, dt, off):
            return nc.alloc_sbuf_tensor_at(name, shape, dt, offset=base + int(off * 1024))

        ctx.enter_context(nc.sbuf_tensor("slab", [P, (229344 - 16512) // 4 - 32], F32))

        X = at("X", [P, T, D], F32, 0)
        raw = at("raw", [P, RING, 512], F32, 16)
        hi = at("hi", [P, RING, 512], F32R, 32)
        lo = at("lo", [P, RING, 512], F32R, 48)
        cst = at("cst", [P, NCST], F32, 64)
        ident = at("ident", [P, P], F32, 65.375)
        identb = at("identb", [P, P], BF16, 65.875)
        maskT = at("maskT", [P, P], BF16, 66.125)
        maskL = at("maskL", [P, P], BF16, 66.375)
        small = at("small", [P, 128], F32, 66.625)
        assert NCST * 4 <= 1.375 * 1024
        A = 67.25
        HTh = at("HTh", [P, DC, S], F32R, A)
        HTl = at("HTl", [P, DC, S], F32R, A + 16)
        zs = at("zs", [P, T, D], F32, A + 32)
        xs = at("xs", [P, T, D], F32, A + 48)
        MIXh0 = at("MIXh0", [P, DC, S], F32R, A + 32)
        MIXl0 = at("MIXl0", [P, DC, S], F32R, A + 48)
        xbcT = at("xbcT", [P, 12, S], F32, A + 64)
        Y1 = at("Y1", [P, T, D], F32, A + 64)
        Btok = at("Btok", [P, T, 2 * NS], F32, A + 88)
        xn = at("xn", [P, T, D], F32, A + 92)
        rows = at("rows", [P, 7, S], F32, A + 92)
        xd = at("xd", [P, T, 512], F32, A + 92)
        xw = at("xw", [P, T, 512], F32, A + 100)
        st = at("st", [P, 3, 512], F32, A + 108)
        cbS = at("cbS", [P, 2, S], F32, A + 114)
        acc = at("acc", [P, 4, S], F32, A + 118)
        SC = at("SC", [P, 4, S], F32, A + 118)
        yt = at("yt", [P, 512], F32, A + 126)
        BR = at("BR", [P, S], F32R, A + 128)
        tok = at("tok", [P, 4, T, 32], F32, A + 130)
        decB = small[:, 64:128]
        sel = at("sel", [P, H1, P], F32R, A + 132)
        selF = at("selF", [P, H1, P], F32, A + 108)
        q = at("q", [P, T, D], F32, A + 64)
        k = at("k", [P, T, D], F32, A + 80)
        v = at("v", [P, T, D], F32, A + 96)
        qT = at("qT", [P, DC, S], F32, A)
        kT = at("kT", [P, DC, S], F32, A + 16)
        MIXh1 = at("MIXh1", [P, DC, S], F32R, A + 64)
        MIXl1 = at("MIXl1", [P, DC, S], F32R, A + 80)
        Pb = at("Pb", [P, 2, 1280], F32, A + 112)
        PT = at("PT", [P, 1280], F32, A + 122)
        sqr = at("sqr", [P, 2, 512], F32, A + 112)
        qst = at("qst", [P, 2, T, H1], F32, A + 130)
        qst2 = at("qst2", [P, 2, T, H1], F32, A + 130.5)
        fst = at("fst", [P, 3, 2, 4], F32, A + 131)
        qst3 = at("qst3", [P, 2, T, H1], F32, A + 131.25)
        gh = at("gh", [P, FF // P, S], F32R, A + 32)
        gl = at("gl", [P, FF // P, S], F32R, A + 76)
        xnF = at("xnF", [P, T, D], F32, A + 120)
        facc = at("facc", [P, 4, S], F32, A + 120)
        fsg = at("fsg", [P, 2, S], F32, A + 128)
        fg = at("fg", [P, 2, S], F32, A + 132)
        rqT = at("rqT", [P, RH, S], F32, A + 32)
        rqx = at("rqx", [P, RH, S], F32, A + 40)
        rkT = at("rkT", [P, RH, S], F32, A + 48)
        rv = at("rv", [P, T, 512], F32, A + 56)
        kz = at("kz", [P, T, 512], F32, A + 64)
        rg = at("rg", [P, RH, S], F32, A + 72)
        DM = at("DM", [P, 2, RH, P], F32, A + 80)
        sT = at("sT", [P, RH, S], F32, A + 84)
        xn2 = at("xn2", [P, T, D], F32, A + 84)
        yR = at("yR", [P, T, 512], F32, A + 92)
        yrh = at("yrh", [P, RH, S], F32R, A + 100)
        yrl = at("yrl", [P, RH, S], F32R, A + 108)
        rS = at("rS", [P, 3, 512], F32, A + 116)
        rbn = at("rbn", [P, T * RH, 6], F32, A + 122)
        rmv = at("rmv", [P, T * RH, 2], F32, A + 122.5)
        rrs = at("rrs", [P, T * RH], F32, A + 122.75)
        ryt = at("ryt", [P, RH, S], F32, A + 124)
        sq = at("sq", [P, T, 512], F32, A + 32)
        skv = at("skv", [P, T, 256], F32, A + 40)
        kd = at("kd", [P, T, 2, 128], F32, A + 44)
        sqT = at("sqT", [P, 4, S], F32, A + 48)
        skT = at("skT", [P, 2, S], F32, A + 56)
        sbias = at("sbias", [P, SH, 256], F32, A + 60)
        sPb = at("sPb", [P, 2, 896], F32, A + 68)
        sPT = at("sPT", [P, 896], F32, A + 76)
        ysh = at("ysh", [P, 4, S], F32R, A + 80)
        ysl = at("ysl", [P, 4, S], F32R, A + 88)
        sst = at("sst", [P, 3, T, 10], F32, A + 96)
        sfst = at("sfst", [P, 5, 2, 4], F32, A + 97)
        ssqr = at("ssqr", [P, 512], F32, A + 98)
        gr = at("gr", [P, DC, S], F32, A + 116)
        gs = at("gs", [P, DC, S], F32, A + 48)
        t1 = at("t1", [P, 4, S], F32, A + 64)
        t2 = at("t2", [P, 4, S], F32, A + 72)
        MTh = at("MTh", [P, DC, S], F32R, A)
        MTl = at("MTl", [P, DC, S], F32R, A + 16)
        xn3 = at("xn3", [P, T, D], F32, A + 32)
        XNh = at("XNh", [P, T, D], F32R, A + 48)
        XNl = at("XNl", [P, T, D], F32R, A + 64)
        rawd = at("rawd", [P, 4, 512], F32, A + 80)
        dh = at("dh", [P, 4, 512], F32R, A + 88)
        dl = at("dl", [P, 4, 512], F32R, A + 120)
        grow = at("grow", [P, D], F32, A + 96)
        XTh = [at(f"XTh{i}", [P, DC, 2 * P], F32R, A + o) for i, o in ((0, 8), (1, 24))]
        XTl = [at(f"XTl{i}", [P, DC, 2 * P], F32R, A + o) for i, o in ((0, 16), (1, 100))]
        Sel = at("Sel", [P, T, 2 * P], F32R, A + 108)
        Se1 = at("Se1", [P, T, 2 * P], F32, A + 133.1875)
        Se2 = at("Se2", [P, T, 2 * P], F32, A + 112)
        esg = at("esg", [P, EF], F32, A + 137.1875)
        hid = at("hid", [P, EF], F32, A + 138.1875)
        hTh = at("hTh", [P, EF], F32R, A + 139.1875)
        hTl = at("hTl", [P, EF], F32R, A + 128)
        R = at("R", [P, 24, T, 36], F32, A + 116)
        rb = at("rb", [P, 76 + 2 * P], F32, A + 129.5)
        ovw = at("ovw", [P, 5, NE], F32, A + 130.8125)
        eow = at("eow", [P, 8, NE], F32, A + 131.4375)
        Mb = at("Mb", [P, T, NE], BF16, A + 132.4375)
        tri = at("tri", [P, 2, P], BF16, A + 132.6875)
        yrow = at("yrow", [P, 2, T], F32, 66.875)
        yrel = at("yrel", [P, 2, T], F32, 66.90625)
        rq_w = at("rq_w", [P, 5, 2, T], F32, 66.9375)
        yidx = at("yidx", [P, 2, T], I32, 67.09375)
        eov = at("eov", [P, 8], I32, A + 129.25)
        Ye = at("Ye", [P, 2, D], F32, A)
        YG = at("YG", [P, 8, D], F32, A)
        pTf = at("pTf", [P, 2, S], F32, A + 133.1875)
        pTh = at("pTh", [P, 2, S], F32R, A + 108)
        pTl = at("pTl", [P, 2, S], F32R, A + 112)
        ple = at("ple", [P, T, D], F32, A + 32)
        psq = at("psq", [P, 2 * T, 512], F32, A + 8)
        prow = at("prow", [P, D], F32, A + 96)
        psg = at("psg", [P, T, 512], F32, A + 84)
        xn4 = at("xn4", [P, T, D], F32, A + 64)

        ye_d = nc.dram_tensor("ye_d", [TILES * P, D], F32, kind="Internal").ap()

        ps = ctx.enter_context(nc.psum_tensor("ps", [P, 8, 512], F32))

        def bset(s):
            return ps[:, 4 * s:4 * s + 4, :]

        x_loaded, misc_loaded = [sem(f"x_loaded{t}") for t in range(T)], sem("misc_loaded")
        raw_full = [sem(f"raw_full{i}") for i in range(RING)]
        hi_ready, lo_ready, unit_used = sem("hi_ready"), sem("lo_ready"), sem("unit_used")
        act_c, dve_c, pool_c = sem("act_c"), sem("dve_c"), sem("pool_c")
        n_ss, n_ms, n_rstd, n_xn, n_tr, n_hi, ht_lo = [sem(s) for s in "n_ss n_ms n_rstd n_xn n_tr n_hi ht_lo".split()]
        cvA, cvD, xbc_ready, z_done = [sem(s) for s in "cvA cvD xbc_ready z_done".split()]
        dtf_v, dtf_e, dtf_s, dtf_l, dtf_cs, br_hi, br_lo, dte_a, dte_d, tok_mm, tok_ready, ddg, dec_mm = [
            sem(s) for s in ("dtf_v dtf_e dtf_s dtf_l dtf_cs br_hi br_lo dte_a dte_d tok_mm tok_ready "
                             "ddg dec_mm").split()]
        xs_tr, xs_ready, cb_mm, cb_ready, xdw, st_mm, st_ready, bc_mm, ncum, dcy, sc_ready, yd_mm, yo_mm, y_done = [
            sem(s) for s in ("xs_tr xs_ready cb_mm cb_ready xdw st_mm st_ready bc_mm ncum dcy sc_ready yd_mm yo_mm "
                             "y_done").split()]
        mix_tr, mix_hi, mix_lo = [sem(s) for s in "mix_tr mix_hi mix_lo".split()]
        qkv_copied, qk_ss, qk_ln, qk_n, qk_tr = [
            sem(s) for s in "qkv_copied qk_ss qk_ln qk_n qk_tr".split()]
        fx_qk, fx_nm, fx_exp, fx_pn, fx_t, fx_pA, fx_pD, fx_pv, fx_hi, fx_lo = [
            sem(s) for s in "fx_qk fx_nm fx_exp fx_pn fx_t fx_pA fx_pD fx_pv fx_hi fx_lo".split()]
        x_res = sem("x_res")
        ys_ss, ys_ms, ys_rs, ys_n = [sem(s) for s in "ys_ss ys_ms ys_rs ys_n".split()]
        yo_done, dec_cp, qT_done, kT_done, etok, sel_loaded, sel_ready, sel_z, ff_c = [
            sem(s) for s in "yo_done dec_cp qT_done kT_done etok sel_loaded sel_ready sel_z ff_c".split()]
        ffA, ffD, ff_sg, ff_g, ff_hi, ff_lo = [sem(s) for s in "ffA ffD ff_sg ff_g ff_hi ff_lo".split()]
        b2c, mats_loaded, rq_x, rk_tr, kz_ready, ry_mm, yr_t, yr_hi, yr_lo = [
            sem(s) for s in ("b2c mats_loaded rq_x rk_tr kz_ready ry_mm yr_t "
                             "yr_hi yr_lo").split()]
        rvar, rpow, s_tr = [
            sem(s) for s in "rvar rpow s_tr".split()]
        sx_l = sem("sx_l")
        m_t, m_r, m_s, sbias_loaded = [
            sem(s) for s in "m_t m_r m_s sbias_loaded".split()]
        xg_f, xg_hi, xg_lo, mb_ready, rk_mm, yidx_ready, eov_ready, xsel, xt_h, xt_l, xg_mh, xg_ml = [
            sem(s) for s in ("xg_f xg_hi xg_lo mb_ready rk_mm yidx_ready eov_ready xsel xt_h xt_l xg_mh xg_ml "
                             "").split()]
        e_h, e_tr, e_hT, dn_mm, ye_a, ye_b = [sem(s) for s in "e_h e_tr e_hT dn_mm ye_a ye_b".split()]
        sel_c, y_add, skip, xw_ready = sem("sel_c"), sem("y_add"), sem("skip"), sem("xw_ready")
        ye_st = [sem("ye_st0"), sem("ye_st1")]
        dn_full, dn_hi, dn_lo, e_hL = sem("dn_full"), sem("dn_hi"), sem("dn_lo"), sem("e_hL")
        r_d, r_e, route_loaded, e_sg, p_loaded, p_hi, p_lo, ple_done, p_sg = [
            sem(s) for s in "r_d r_e route_loaded e_sg p_loaded p_hi p_lo ple_done p_sg".split()]
        prow_loaded, out_ready, out_stored = [sem(s) for s in "prow_loaded out_ready out_stored".split()]

        yg = [sel_loaded, mats_loaded, sbias_loaded, route_loaded]
        block_cm = nc.Block()
        block = block_cm.__enter__()

        def col(name, i=0, n=1):
            c0 = COLS[name][0] + i
            return cst[:, c0:c0 + n]

        def col_at(name, i):
            return col(name, i) if isinstance(i, int) else cst[:, bass.ds(COLS[name][0] + i, 1)]

        def act_split(act, u, n=1):
            for i in range(u, u + n):
                act.wait_ge(raw_full[i % RING], 16 * (i // RING + 1))
                if i >= RING:
                    act.wait_ge(unit_used, i - RING + 1)
                act.activation(hi[:, i % RING, :], raw[:, i % RING, :], ACT.Copy).then_inc(hi_ready, 1)

        def dve_split(dve, u, n=1):
            for i in range(u, u + n):
                dve.wait_ge(hi_ready, i + 1)
                dve.tensor_tensor(lo[:, i % RING, :], raw[:, i % RING, :], hi[:, i % RING, :].bitcast(F32),
                                  ALU.subtract).then_inc(lo_ready, 1)

        def mm3(pe, o, ah, al, bh, bl, start, stop):
            pe.matmul(o, al, bh, start=start, stop=False)
            pe.matmul(o, ah, bl, start=False, stop=False)
            return pe.matmul(o, ah, bh, start=False, stop=stop)

        def pe_tokens(pe, u, nk, s, Lh, Ll, k0=0, ready=None, first=True, last=True):
            for c in range(nk):
                if ready is not None:
                    pe.wait_ge(ready[0], ready[1] + c + 1)
                pe.wait_ge(lo_ready, u + c + 1)
                w = (u + c) % RING
                for t in range(T):
                    mm = mm3(pe, ps[:, 4 * s + t, :], Lh[:, k0 + c, t * P:(t + 1) * P], Ll[:, k0 + c, t * P:(t + 1) * P],
                             hi[:, w, :], lo[:, w, :], first and c == 0, last and c == nk - 1)
                mm.then_inc(unit_used, 1)

        def pe_features(pe, u, nk, s, Rh, Rl, ready=None, slot=None):
            for c in range(nk):
                if ready is not None:
                    pe.wait_ge(ready[0], ready[1] + c + 1)
                pe.wait_ge(lo_ready, u + (c + 1))
                w = ((u if slot is None else slot) + c) % RING
                for j in range(4):
                    mm = mm3(pe, ps[:, 4 * s + j, :], hi[:, w, j * P:(j + 1) * P], lo[:, w, j * P:(j + 1) * P],
                             Rh[:, c, :], Rl[:, c, :], c == 0, c == nk - 1)
                mm.then_inc(unit_used, 1)

        def act_norm(act, n, xnb, wname):
            for t in range(T):
                if n == 0:
                    act.wait_ge(x_loaded[t], 16)
                else:
                    act.wait_ge(x_res, XRES(n, t))
                act.activation(xnb[:, t, :], X[:, t, :], ACT.Square, accum_out=small[:, t:t + 1]).then_inc(n_ss, 1)
            if n == 0:
                act.wait_ge(misc_loaded, 80)
            for c in range(DC):
                act.wait_ge(n_tr, DC * n + c + 1)
                act.activation(HTh[:, c, :], ps[:, c, :], ACT.Identity,
                               scale=col(wname, c)).then_inc(n_hi, 1)

        def norm_mean(dve, n, t):
            dve.wait_ge(n_ss, T * n + t + 1)
            dve.tensor_scalar(small[:, 4 + t:5 + t], small[:, t:t + 1], 1.0 / D, EPS, ALU.mult, ALU.add).then_inc(n_ms, 1)

        def norm_scale(dve, n, t, xnb):
            dve.wait_ge(n_rstd, T * n + t + 1)
            dve.tensor_scalar(xnb[:, t, :], X[:, t, :], small[:, 8 + t:9 + t], None, ALU.mult).then_inc(n_xn, 1)

        def norm_rest(dve, n, wname):
            for c in range(DC):
                dve.wait_ge(n_hi, DC * n + c + 1)
                dve.scalar_tensor_tensor(HTl[:, c, :], ps[:, c, :], col(wname, c), HTh[:, c, :].bitcast(F32),
                                         ALU.mult, ALU.subtract).then_inc(ht_lo, 1)

        def dve_norm(dve, n, xnb, wname):
            norm_mean(dve, n, 0)
            for t in range(T):
                if t + 1 < T:
                    norm_mean(dve, n, t + 1)
                norm_scale(dve, n, t, xnb)
            norm_rest(dve, n, wname)

        def pool_norm(pool, n):
            for t in range(T):
                pool.wait_ge(n_ms, T * n + t + 1)
                pool.tensor_tensor(small[:, 8 + t:9 + t], small[:, 4 + t:5 + t], small[:, 12:13], ALU.pow).then_inc(n_rstd, 1)

        def pe_norm(pe, n, xnb, free):
            for s_, v_ in free:
                pe.wait_ge(s_, v_)
            for t in range(T):
                pe.wait_ge(n_xn, T * n + t + 1)
                for c in range(DC):
                    tr = pe.transpose(ps[:, c, t * P:(t + 1) * P], xnb[:, t, c * P:(c + 1) * P], ident[:, :])
                    if t == T - 1:
                        tr.then_inc(n_tr, 1)

        def XRES(n, t):
            return 8 * n - T + t + 1 if n < 4 else 8 * (n - 1) + 2 * (t + 1)

        FG = ((1, ((3, 0),)), (0, ((2, 0), (0, 384))), (2, ((1, 0),)))
        NG_ = len(FG)
        FOFF = (0, 128, 384, 768)
        PTB = ((3, 0), (4, 0), (5, 0), (4, 384))
        PTO = (0, 512, 1024, 896)
        SB = ((0, 256, P), (0, 0, 2 * P), (1, 0, 2 * P), (1, 256, 2 * P))
        SO = (0, 128, 384, 640)

        def PE_B2(pe):
            U = FIRST
            pe_norm(pe, 2, xn2, [(x_res, 16)])
            pe.wait_ge(ht_lo, 20)
            pe_features(pe, U["rq"], 8, 0, HTh, HTl, ready=(ht_lo, 16))
            pe_features(pe, U["rk"], 8, 1, HTh, HTl)
            pe.wait_ge(b2c, 4)
            pe_tokens(pe, U["rv"], 8, 0, HTh, HTl)
            pe.wait_ge(b2c, 8)
            pe_features(pe, U["rg"], 8, 1, HTh, HTl)
            pe.wait_ge(b2c, 12)
            for c in range(T - 1):
                for h in range(RH):
                    tr = pe.transpose(ps[:, c, h * P:(h + 1) * P], rkT[:, h, c * P:(c + 1) * P], ident[:, :])
                tr.then_inc(rk_tr, 1)
            pe.wait_ge(b2c, 16)
            for h in range(RH):
                for c in range(T):
                    mm = pe.matmul(ps[:, 4 + h, c * P:(c + 1) * P], rkT[:, h, c * P:(c + 1) * P],
                                   rqT[:, h, c * P:(c + 1) * P], start=True, stop=True)
                mm.then_inc(cb_mm, 1)
            for c in range(T - 1):
                pe.wait_ge(kz_ready, c + 1)
                for h in range(RH):
                    mm = pe.matmul(ps[:, c, h * P:(h + 1) * P], kz[:, c, h * P:(h + 1) * P], rv[:, c, h * P:(h + 1) * P],
                                   start=True, stop=True)
                mm.then_inc(st_mm, 1)
            pe.wait_ge(cb_ready, 2 + RH)
            pe.wait_ge(rq_x, RH)
            for c in range(T):
                if c:
                    pe.wait_ge(st_ready, 6 + c)
                for h in range(RH):
                    hc = slice(h * P, (h + 1) * P)
                    mm = pe.matmul(ps[:, 4 + c, hc], sT[:, h, c * P:(c + 1) * P], rv[:, c, hc], start=True, stop=c == 0)
                    if c:
                        mm = pe.matmul(ps[:, 4 + c, hc], rqx[:, h, c * P:(c + 1) * P], rS[:, c - 1, hc],
                                       start=False, stop=True)
                mm.then_inc(ry_mm, 1)
            pe_tokens(pe, U["sq"], 8, 0, HTh, HTl)
            pe.wait_ge(ys_n, 1 + T)
            for h in range(RH):
                for t in range(T):
                    tr = pe.transpose(ps[:, 4 + h, t * P:(t + 1) * P], yR[:, t, h * P:(h + 1) * P], ident[:, :])
                tr.then_inc(mix_tr, 1)
            pe.wait_ge(b2c, 20)
            for i in range(4):
                pe.wait_ge(lo_ready, U["skv"] + i + 1)
                w = (U["skv"] + i) % RING
                for t in range(T):
                    for k_ in range(2):
                        c = 2 * i + k_
                        cc = slice(256 * k_, 256 * k_ + 256)
                        mm = mm3(pe, ps[:, t, 0:256], HTh[:, c, t * P:(t + 1) * P], HTl[:, c, t * P:(t + 1) * P],
                                 hi[:, w, cc], lo[:, w, cc], c == 0, c == DC - 1)
                mm.then_inc(unit_used, 1)
            pe.wait_ge(b2c, 24)
            pe_features(pe, U["gr0"], 8, 0, HTh, HTl)
            pe.wait_ge(qk_n, 1 + 1)
            pe.wait_ge(yr_t, RH)
            for c in range(4):
                for t in range(T):
                    tr = pe.transpose(ps[:, 4 + c, t * P:(t + 1) * P], sq[:, t, c * P:(c + 1) * P], ident[:, :])
                tr.then_inc(s_tr, 1)
            for g in range(SKV):
                pe.wait_ge(qT_done, DC + g + 1)
                for t in range(T):
                    tr = pe.transpose(ps[:, 4 + g, t * P:(t + 1) * P], kd[:, t, g, :], ident[:, :])
                tr.then_inc(s_tr, 1)
            pe.wait_ge(b2c, 28)
            pe.wait_ge(qT_done, DC + 4)
            pe.wait_ge(kT_done, DC + SKV)

            def scores(h):
                r = slice(HD * (h % 2), HD * (h % 2) + HD)
                if h:
                    pe.wait_ge(sx_l, h)
                for i, (bank, o, n) in enumerate(SB):
                    mm = pe.matmul(ps[:, bank, o:o + n], sqT[r, h // 2, i * P:(i + 1) * P],
                                   skT[r, h // 4, (i + 1) * P - n:(i + 1) * P], start=True, stop=True)
                mm.then_inc(fx_qk, 1)

            def values(h):
                pe.wait_ge(fx_pA, H1 + h + 1)
                pe.wait_ge(fx_pD, H1 + h + 1)
                pr = h // 2
                if pr >= 2:
                    pe.wait_ge(fx_lo, H1 // 2 + pr - 1)
                vc = slice(128 + HD * (h // 4), 128 + HD * (h // 4) + HD)
                for i in range(T):
                    o = ps[HD * (h % 2):HD * (h % 2) + HD, 4 + pr % 2, i * P:(i + 1) * P]
                    if i:
                        pe.matmul(o, skv[:, i - 1, vc], sPT[:, SO[i]:SO[i] + P], start=True, stop=False)
                    c0 = SO[i] + (P if i else 0)
                    mm = pe.matmul(o, skv[:, i, vc], sPT[:, c0:c0 + P], start=i == 0, stop=True)
                mm.then_inc(fx_pv, 1)

            scores(0)
            for h in range(SH):
                if h + 1 < SH:
                    scores(h + 1)
                if h:
                    values(h - 1)
                pe.wait_ge(fx_pn, NG_ * H1 + h + 1)
                if h:
                    pe.wait_ge(fx_pA, H1 + h)
                    pe.wait_ge(fx_pD, H1 + h)
                for k_ in range(7):
                    tr = pe.transpose(ps[:, 2 + k_ // 4, (k_ % 4) * P:(k_ % 4 + 1) * P],
                                      sPb[:, h % 2, k_ * P:(k_ + 1) * P], ident[:, :])
                tr.then_inc(fx_t, 1)
            values(SH - 1)
            for b, n in ((1, "gr1"), (2, "gs0"), (3, "gs1")):
                if b == 1:
                    pe.wait_ge(fx_lo, H1 // 2 + 4)
                if b == 3:
                    pe.wait_ge(b2c, 32)
                pe_features(pe, U[n], 8, b % 2, HTh, HTl)
            pe.wait_ge(yr_lo, RH)
            for b in range(2):
                if b:
                    pe.wait_ge(m_r, 4)
                else:
                    pe.wait_ge(b2c, 36)
                pe_features(pe, U[f"ro{b}"], 4, 0, yrh, yrl)
                if b:
                    pe.wait_ge(m_s, 4)
                else:
                    pe.wait_ge(b2c, 40)
                pe_features(pe, U[f"so{b}"], 4, 1, ysh, ysl)
            for b in range(2):
                pe.wait_ge((m_r, m_s)[b], 8)
                pe_tokens(pe, U[f"mo{b}"], 8, b, MTh, MTl, ready=(mix_lo, DC) if b == 0 else None)
            PE_MOE(pe)

        def ACT_B2(act, w, ch):
            U = FIRST
            act_norm(act, 2, xn2, "nmix2")

            def copy(dst, src, name, func=ACT.Copy, after=()):
                def piece():
                    act.wait_ge(unit_used, FIRST[name] + UNITS[name])
                    for s_, v_ in after:
                        act.wait_ge(s_, v_)
                    act.activation(dst, src, func).then_inc(b2c, 1)
                return piece

            w.upto(U["rk"] + 8)
            w.beside(U["rv"] + 8, [copy(rqT[:, j, :], ps[:, j, :], "rq") for j in range(4)])
            w.beside(U["rg"] + 8, [copy(rkT[:, j, :], ps[:, 4 + j, :], "rk") for j in range(4)])
            w.beside(U["sq"] + 8, [copy(rv[:, j, :], ps[:, j, :], "rv") for j in range(4)])
            for j in range(4):
                copy(rg[:, j, :], ps[:, 4 + j, :], "rg", ACT.Silu)()
            w.beside(U["skv"] + 4, [copy(sq[:, j, :], ps[:, j, :], "sq", after=((ry_mm, 4),)) for j in range(4)])
            for h in range(RH):
                act.wait_ge(yr_t, h + 1)
                act.activation(yrh[:, h, :], ryt[:, h, :], ACT.Copy).then_inc(yr_hi, 1)
            w.beside(U["gr0"] + 8, [copy(skv[:, j, :], ps[:, j, 0:256], "skv") for j in range(4)])
            w.upto(U["gr1"] + 7)
            for c in range(4):
                act.wait_ge(s_tr, c + 1)
                act.activation(sqT[:, c, :], ps[:, 4 + c, :], ACT.Identity, scale=small[:, 19:20]).then_inc(qT_done, 1)

            def weights(h):
                act.wait_ge(fx_nm, NG_ * H1 + h + 1)
                for i in range(T):
                    n = P if i == 0 else 2 * P
                    act.activation(sPb[:, h % 2, SO[i]:SO[i] + n], sPb[:, h % 2, SO[i]:SO[i] + n], ACT.Exp,
                                   bias=sfst[:, 1, h % 2, i:i + 1], accum_out=sfst[:, 2, h % 2, i:i + 1])
                act.activation(sfst[:, 3, h % 2, :], sfst[:, 1, h % 2, :], ACT.Exp, bias=col("sink", h)).then_inc(fx_exp, 1)

            def transposed(h):
                act.wait_ge(fx_t, H1 + h + 1)
                if h:
                    act.wait_ge(fx_pv, H1 + h)
                act.activation(sPT[:, 0:512], ps[:, 2, :], ACT.Copy).then_inc(fx_pA, 1)

            def output(h):
                act.wait_ge(fx_pv, H1 + h + 1)
                act.activation(ysh[:, h // 2, :], ps[:, 4 + h // 2 % 2, :], ACT.Copy).then_inc(fx_hi, 1)

            for j in range(4):
                copy(gr[:, j, :], ps[:, j, :], "gr0", ACT.Sigmoid, after=((ys_n, 1 + T),))()
            weights(0)
            for h in range(SH):
                if h:
                    transposed(h - 1)
                if h + 1 < SH:
                    weights(h + 1)
                if h and h % 2 == 0:
                    output(h - 1)
            transposed(SH - 1)
            output(SH - 1)
            w.upto(U["gr1"] + 8)
            w.upto(U["gs0"] + 8)
            w.beside(U["gs1"] + 8, [copy(gr[:, 4 + j, :], ps[:, 4 + j, :], "gr1", ACT.Sigmoid) for j in range(4)])
            w.beside(U["ro0"] + 8, [copy(gs[:, j, :], ps[:, j, :], "gs0", ACT.Sigmoid) for j in range(4)])
            w.beside(U["ro1"] + 4, [copy(gs[:, 4 + j, :], ps[:, 4 + j, :], "gs1", ACT.Sigmoid) for j in range(4)])
            for b in range(2):
                w.upto((U["so1"], U["mo0"])[b] + 4)
                for j in range(4):
                    act.wait_ge(m_t, 4 * b + j + 1)
                    act.activation(MTh[:, 4 * b + j, :], t1[:, j, :], ACT.Copy).then_inc(mix_hi, 1)
            w.upto(U["mo1"] + 8)
            w.upto(U["wr"] + 1)
            ACT_MOE(act, w, ch)

        def DVE_B2(dve, w, ch):
            U = FIRST
            dve_norm(dve, 2, xn2, "nmix2")

            def heads(a):
                return a.rearrange("p (h e) -> p h e", e=HD)

            def per_chunk(a):
                return a.rearrange("p (c i) -> p c i", c=T)

            w.upto(U["rk"] + 8)
            w.upto(U["rv"] + 8)

            def rqx_h(h):
                def piece():
                    dve.wait_ge(b2c, h + 1)
                    dve.wait_ge(mats_loaded, 16)
                    dve.tensor_tensor(per_chunk(rqx[:, h, :]), per_chunk(rqT[:, h, :]),
                                      DM[:, 1, h:h + 1, :].broadcast_to([P, T, P]), ALU.mult).then_inc(rq_x, 1)
                return piece

            w.beside(U["rg"] + 8, [rqx_h(h) for h in range(RH)])
            w.upto(U["sq"] + 8)
            for c in range(T - 1):
                dve.wait_ge(rk_tr, c + 1)
                dve.tensor_tensor(per_chunk(kz[:, c, :]), per_chunk(ps[:, c, :]),
                                  col("zeta", 0, RH).unsqueeze(2).broadcast_to([P, RH, P]), ALU.mult).then_inc(kz_ready, 1)
            for h in range(RH):
                dve.wait_ge(cb_mm, 2 + h + 1)
                dve.tensor_tensor(per_chunk(sT[:, h, :]), per_chunk(ps[:, 4 + h, :]),
                                  DM[:, 0, h:h + 1, :].broadcast_to([P, T, P]), ALU.mult).then_inc(cb_ready, 1)
            for c in range(T - 1):
                dve.wait_ge(st_mm, 6 + c + 1)
                if c == 0:
                    dve.tensor_copy(rS[:, 0, :], ps[:, 0, :]).then_inc(st_ready, 1)
                    continue
                dve.wait_ge(st_ready, 6 + c)
                for h in range(RH):
                    hc = slice(h * P, (h + 1) * P)
                    ins = dve.scalar_tensor_tensor(rS[:, c, hc], rS[:, c - 1, hc], float(np.exp(P * LOG_GAMMA[h])),
                                                   ps[:, c, hc], ALU.mult, ALU.add)
                ins.then_inc(st_ready, 1)
            for c in range(T):
                dve.wait_ge(ry_mm, c + 1)
                for h in range(RH):
                    ins = dve.bn_stats(rbn[:, c * RH + h, :], ps[:, 4 + c, h * P:(h + 1) * P])
                ch.link(ins)
                for h in range(RH):
                    ins = dve.bn_aggr(rmv[:, c * RH + h, :], rbn[:, c * RH + h, :])
            ch.link(ins)
            dve.tensor_scalar(rrs[:, :].unsqueeze(2), rmv[:, :, 1:2], EPS, None, ALU.add).then_inc(rvar, 1)
            dve.wait_ge(rpow, 1)
            for c in range(T):
                for h in range(RH):
                    i = c * RH + h
                    ins = dve.tensor_scalar(yR[:, c, h * P:(h + 1) * P], ps[:, 4 + c, h * P:(h + 1) * P],
                                            rmv[:, i, 0:1], rrs[:, i:i + 1], ALU.subtract, ALU.mult)
                ins.then_inc(ys_n, 1)
            w.upto(U["skv"] + 4)
            for h in range(RH):
                dve.wait_ge(mix_tr, DC + h + 1)
                ch.link(dve.tensor_scalar(ryt[:, h, :], ps[:, 4 + h, :], col("gng", h), col("gnb", h), ALU.mult, ALU.add))
                dve.wait_ge(b2c, 13 + h)
                dve.tensor_tensor(ryt[:, h, :], ryt[:, h, :], rg[:, h, :], ALU.mult).then_inc(yr_t, 1)
            w.upto(U["gr0"] + 4)
            for t in range(T):
                dve.wait_ge(b2c, 17 + t)
                ch.wait()
                ch.link(dve.tensor_tensor(ssqr[:, :], sq[:, t, :], sq[:, t, :], ALU.mult))
                ch.mark(dve.tensor_reduce(sst[:, 0, t, 0:8], heads(ssqr[:, :]), AX.X, ALU.add))
            for t in range(T):
                dve.wait_ge(b2c, 21 + t)
                ch.wait()
                ch.link(dve.tensor_tensor(ssqr[:, 0:128], skv[:, t, 0:128], skv[:, t, 0:128], ALU.mult))
                ch.mark(dve.tensor_reduce(sst[:, 0, t, 8:10], heads(ssqr[:, 0:128]), AX.X, ALU.add))
            ch.wait()
            dve.tensor_scalar(sst[:, 1, :, :], sst[:, 0, :, :], 1.0 / HD, EPS, ALU.mult, ALU.add).then_inc(qk_ss, 1)
            w.upto(U["gr0"] + 8)
            dve.wait_ge(rpow, 1 + 1)
            for t in range(T):
                dve.tensor_tensor(heads(sq[:, t, :]), heads(sq[:, t, :]),
                                  sst[:, 2, t, 0:8].unsqueeze(2).broadcast_to([P, 8, HD]), ALU.mult)
                for r in range(2):
                    ins = dve.tensor_tensor(kd[:, t, :, r * HD:(r + 1) * HD], heads(skv[:, t, 0:128]),
                                            sst[:, 2, t, 8:10].unsqueeze(2).broadcast_to([P, SKV, HD]), ALU.mult)
            ins.then_inc(qk_n, 1)
            for h in range(RH):
                dve.wait_ge(yr_hi, h + 1)
                dve.tensor_tensor(yrl[:, h, :], ryt[:, h, :], yrh[:, h, :].bitcast(F32), ALU.subtract).then_inc(yr_lo, 1)
            w.upto(U["gr1"] + 7)
            for g in range(SKV):
                dve.wait_ge(s_tr, 5 + g)
                dve.tensor_scalar(skT[:, g, :], ps[:, 4 + g, :], col("skw"), None, ALU.mult).then_inc(kT_done, 1)

            def logits(h):
                dve.wait_ge(fx_qk, NG_ * H1 + h + 1)
                dve.wait_ge(sbias_loaded, 16)
                if h >= 2:
                    dve.wait_ge(fx_t, H1 + h - 1)
                b_ = h % 2
                i1 = dve.tensor_tensor(sPb[:, b_, 0:128], ps[:, 0, 256:384], sbias[:, h, 128:256], ALU.add)
                i1 = dve.tensor_tensor(sPb[:, b_, 128:384], ps[:, 0, 0:256], sbias[:, h, :], ALU.add)
                i1 = dve.tensor_tensor(sPb[:, b_, 384:896].rearrange("p (i n) -> p i n", i=2),
                                       ps[:, 1, :].rearrange("p (i n) -> p i n", i=2),
                                       sbias[:, h:h + 1, :].broadcast_to([P, 2, 256]), ALU.add)
                i1.then_inc(sx_l, 1)
                dve.wait_ge(sx_l, h + 1)
                dve.tensor_reduce(sfst[:, 0, b_, 0:1], sPb[:, b_, 0:128], AX.X, ALU.max)
                ch.link(dve.tensor_reduce(sfst[:, 0, b_, 1:4], sPb[:, b_, 128:896].rearrange("p (i n) -> p i n", i=3),
                                          AX.X, ALU.max))
                dve.tensor_scalar(sfst[:, 1, b_, :], sfst[:, 0, b_, :], col("sink", h), -1.0, ALU.max, ALU.mult
                                  ).then_inc(fx_nm, 1)

            def transposed(h):
                dve.wait_ge(fx_t, H1 + h + 1)
                if h:
                    dve.wait_ge(fx_pv, H1 + h)
                dve.tensor_copy(sPT[:, 512:896], ps[:, 3, 0:384]).then_inc(fx_pD, 1)

            def normalize(h):
                b_ = h % 2
                dve.wait_ge(fx_exp, NG_ * H1 + h + 1)
                ch.link(dve.tensor_tensor(sfst[:, 2, b_, :], sfst[:, 2, b_, :], sfst[:, 3, b_, :], ALU.add))
                ch.link(dve.reciprocal(sfst[:, 4, b_, :], sfst[:, 2, b_, :]))
                dve.tensor_scalar(sPb[:, b_, 0:128], sPb[:, b_, 0:128], sfst[:, 4, b_, 0:1], None, ALU.mult)
                v3 = sPb[:, b_, 128:896].rearrange("p (i n) -> p i n", i=3)
                dve.tensor_tensor(v3, v3, sfst[:, 4, b_, 1:4].unsqueeze(2).broadcast_to([P, 3, 256]), ALU.mult
                                  ).then_inc(fx_pn, 1)

            def output(h):
                pr = h // 2
                dve.wait_ge(fx_hi, H1 // 2 + pr + 1)
                dve.tensor_tensor(ysl[:, pr, :], ps[:, 4 + pr % 2, :], ysh[:, pr, :].bitcast(F32),
                                  ALU.subtract).then_inc(fx_lo, 1)

            logits(0)
            for h in range(SH):
                if h:
                    transposed(h - 1)
                normalize(h)
                if h + 1 < SH:
                    logits(h + 1)
                if h > 1 and h % 2:
                    output(h - 2)
            transposed(SH - 1)
            output(SH - 1)
            w.upto(U["so0"] + 4)

            def merge(b, then1, then2):
                for j in range(4):
                    dve.wait_ge(unit_used, U[f"ro{b}"] + 4)
                    if b:
                        dve.wait_ge(mix_lo, DC + 4)
                    dve.wait_ge(b2c, 36)
                    dve.tensor_tensor(t1[:, j, :], ps[:, j, :], gr[:, 4 * b + j, :], ALU.mult).then_inc(m_r, 1)
                w.upto(then1)
                for j in range(4):
                    dve.wait_ge(unit_used, U[f"so{b}"] + 4)
                    dve.wait_ge(b2c, 40)
                    if b:
                        dve.wait_ge(m_t, 4)
                    dve.tensor_tensor(t2[:, j, :], ps[:, 4 + j, :], gs[:, 4 * b + j, :], ALU.mult).then_inc(m_s, 1)
                    dve.wait_ge(m_r, 4 * b + j + 1)
                    dve.wait_ge(m_s, 4 * b + j + 1)
                    dve.tensor_tensor(t1[:, j, :], t1[:, j, :], t2[:, j, :], ALU.add).then_inc(m_t, 1)
                for j in range(4):
                    dve.wait_ge(mix_hi, DC + 4 * b + j + 1)
                    dve.tensor_tensor(MTl[:, 4 * b + j, :], t1[:, j, :], MTh[:, 4 * b + j, :].bitcast(F32),
                                      ALU.subtract).then_inc(mix_lo, 1)
                w.upto(then2)

            def residual2(name, s_, b):
                def make(t):
                    def piece():
                        dve.wait_ge(unit_used, FIRST[name] + UNITS[name])
                        dve.tensor_tensor(X[:, t, b * 512:(b + 1) * 512], X[:, t, b * 512:(b + 1) * 512],
                                          ps[:, 4 * s_ + t, :], ALU.add).then_inc(x_res, 1)
                    return piece
                return [make(t) for t in range(T)]

            merge(0, U["ro1"] + 4, U["so1"] + 4)
            merge(1, U["mo0"] + 4, U["mo0"] + 8)
            w.upto(U["mo1"] + 8)
            w.upto(U["wr"] + 1)
            for p in residual2("mo0", 0, 0) + residual2("mo1", 1, 1):
                p()
            DVE_MOE(dve, w, ch)

        def POOL_B2(pool):
            pool_norm(pool, 2)
            pool.wait_ge(x_res, 16)
            pool.dma_start(DM[:, :, :, :], mats_d).then_inc(mats_loaded, 16)
            pool.dma_start(pTf[:, :, :], pT_d).then_inc(p_loaded, 16)
            pool.wait_ge(rvar, 1)
            pool.tensor_tensor(rrs[:, :], rrs[:, :], small[:, 48:49].broadcast_to([P, T * RH]), ALU.pow).then_inc(rpow, 1)
            pool.wait_ge(ry_mm, T)
            pool.dma_start(sbias[:, :, :], bias_d).then_inc(sbias_loaded, 16)
            pool.wait_ge(qk_ss, 1 + 1)
            pool.tensor_tensor(sst[:, 2, :, :], sst[:, 1, :, :], small[:, 48:49].unsqueeze(2).broadcast_to([P, T, 10]),
                               ALU.pow).then_inc(rpow, 1)
            POOL_MOE(pool)

        def PE_MOE(pe):
            U = FIRST
            pe_norm(pe, 3, xn3, [(x_res, 24)])
            pe.wait_ge(ht_lo, 32)
            pe.wait_ge(lo_ready, U["wr"] + 1)
            w = U["wr"] % RING
            for t in range(T):
                for c in range(DC):
                    mm = mm3(pe, ps[:, 0, t * 36:(t + 1) * 36], HTh[:, c, t * P:(t + 1) * P], HTl[:, c, t * P:(t + 1) * P],
                             hi[:, w, c * 36:(c + 1) * 36], lo[:, w, c * 36:(c + 1) * 36], c == 0, c == DC - 1)
            mm.then_inc(unit_used, 1)
            pe.wait_ge(p_lo, 1)
            pe_tokens(pe, U["ple0"], 2, 1, pTh, pTl)
            pe.wait_ge(r_d, 1)
            pe_tokens(pe, U["ple1"], 2, 0, pTh, pTl)
            pe.wait_ge(b2c, 44)
            pe.wait_ge(mb_ready, 1)
            pe.wait_ge(route_loaded, 48)
            for t in range(T + 1):
                for t_ in range(min(t, T - 1) + 1):
                    mm = pe.matmul(ps[:, 4, t * NE:(t + 1) * NE], tri[:, 0 if t_ == t else 1, :], Mb[:, t_, :],
                                   start=t_ == 0, stop=t_ == min(t, T - 1))
            mm.then_inc(rk_mm, 1)

            def gather(g, src, bank0, done):
                for b in range(2):
                    for j in range(2):
                        c = 4 * g + 2 * b + j
                        for t in range(T):
                            mm = pe.matmul(ps[:, bank0 + b, j * 2 * P:(j + 1) * 2 * P], src[:, t, c * P:(c + 1) * P],
                                           Sel[:, t, :], start=t == 0, stop=t == T - 1)
                    mm.then_inc(done, 1)

            pe.wait_ge(xg_lo, T)
            pe.wait_ge(xsel, 1)
            pe.wait_ge(b2c, 48)
            for g in range(2):
                if g:
                    pe.wait_ge(xt_h, 2)
                    pe.wait_ge(xt_l, 2)
                gather(g, XNh, 0, xg_mh)
                gather(g, XNl, 2, xg_ml)

            def body(n, par, h, h1, pp):
                pe.wait_ge(xt_h, h * 4 + 4)
                pe.wait_ge(xt_l, h * 4 + 4)
                if not (isinstance(n, int) and n == 0):
                    pe.wait_ge(e_h, n)
                for c in range(DC):
                    pe.wait_ge(lo_ready, n * 8 + (MOE_AT + c + 1))
                    w = (MOE_AT + c) % RING
                    rows_ = slice(par * P, (par + 1) * P)
                    mm3(pe, ps[:, 4, :], XTh[pp][:, c, rows_], XTl[pp][:, c, rows_], hi[:, w, :], lo[:, w, :], c == 0, c == DC - 1
                        ).then_inc(unit_used, 1)
                last = isinstance(n, int) and n == TILES - 1
                if not last:
                    pe.wait_ge(xsel, h + 2)
                    pe.wait_ge(xt_h, n * 2 + 4)
                    pe.wait_ge(xt_l, n * 2 + 4)
                    gather(par, XNh, 0, xg_mh)
                pe.wait_ge(e_h, n + 1)
                if not (isinstance(n, int) and n == 0):
                    pe.wait_ge(e_hL, n)
                for j in range(2):
                    tr = pe.transpose(ps[:, 5, j * P:(j + 1) * P], hid[:, j * P:(j + 1) * P], ident[:, :])
                tr.then_inc(e_tr, 1)
                if not last:
                    gather(par, XNl, 2, xg_ml)
                pe.wait_ge(e_hL, n + 1)
                pe.wait_ge(dn_lo, n * 4 + 4)
                if not (isinstance(n, int) and n == 0):
                    pe.wait_ge(ye_a, n)
                    pe.wait_ge(ye_b, n)
                for hf in range(2):
                    for c in range(2):
                        cc = slice(c * P, (c + 1) * P)
                        mm = mm3(pe, ps[:, 6 + hf, :], hTh[:, cc], hTl[:, cc], dh[:, 2 * hf + c, :], dl[:, 2 * hf + c, :],
                                 c == 0, c == 1)
                    mm.then_inc(dn_mm, 1)

            tiles(pe, body)
            PE_PLE(pe)

        def tiles(eng, body):
            for n in range(3):
                body(n, n % 2, n // 2, (n - 1) // 2, n // 2 % 2)
            with eng.Fori(0, (TILES - 7) // 4) as i:
                body(i * 4 + 3, 1, i * 2 + 1, i * 2 + 1, 1)
                body(i * 4 + 4, 0, i * 2 + 2, i * 2 + 1, 0)
                body(i * 4 + 5, 1, i * 2 + 2, i * 2 + 2, 0)
                body(i * 4 + 6, 0, i * 2 + 3, i * 2 + 2, 1)
            for n in range(TILES - 4, TILES):
                body(n, n % 2, n // 2, (n - 1) // 2, n // 2 % 2)

        def PE_PLE(pe):
            U = FIRST
            pe_norm(pe, 4, xn4, [(x_res, 32), (ye_a, TILES), (ye_b, TILES)])
            pe.wait_ge(ht_lo, 36)
            pe_tokens(pe, U["pg0"], 8, 0, HTh, HTl, ready=(ht_lo, 32))
            pe_tokens(pe, U["pg1"], 8, 1, HTh, HTl)

        def ACT_MOE(act, w, ch):
            act.wait_ge(x_res, 17)
            act.wait_ge(p_loaded, 16)
            act.activation(pTh[:, :, :], pTf[:, :, :], ACT.Copy).then_inc(p_hi, 1)
            act_norm(act, 3, xn3, "nffn2")
            w.upto(MOE_AT + 3)
            for t in range(T):
                act.wait_ge(xg_f, t + 1)
                act.activation(XNh[:, t, :], xn3[:, t, :], ACT.Copy).then_inc(xg_hi, 1)
            act.wait_ge(r_d, 2)
            act.activation(R[:, 2, :, 0:4], R[:, 1, :, 0:4], ACT.Exp).then_inc(r_e, 1)
            act.wait_ge(r_d, 3)
            act.activation(R[:, 10, :, 0:1], R[:, 9, :, 0:1], ACT.Exp).then_inc(r_e, 1)
            act.wait_ge(xg_lo, T)
            for b in range(2):
                act.wait_ge(unit_used, FIRST[f"ple{b}"] + 2)
                for t in range(T):
                    act.activation(psq[:, b * T + t, :], ps[:, 4 * (1 - b) + t, :], ACT.Square,
                                   accum_out=small[:, 24 + 2 * t + b:25 + 2 * t + b])
                    act.activation(ple[:, t, b * 512:(b + 1) * 512], ps[:, 4 * (1 - b) + t, :], ACT.Copy).then_inc(b2c, 1)
            w.upto(MOE_AT + 8)

            def xt(k_, g, pp):
                for b in range(2):
                    act.wait_ge(xg_mh, k_ * 2 + (b + 1))
                    c = 4 * g + 2 * b
                    act.activation(XTh[pp][:, c:c + 2, :], ps[:, b, :].rearrange("p (c r) -> p c r", c=2), ACT.Copy
                                   ).then_inc(xt_h, 1)

            xt(0, 0, 0)
            xt(1, 1, 0)

            def body(n, par, h, h1, pp):
                last = isinstance(n, int) and n == TILES - 1
                if not (isinstance(n, int) and n == 0):
                    store(n, par, h1)
                act.wait_ge(dn_full, n * 16 + 16)
                if not (isinstance(n, int) and n == 0):
                    act.wait_ge(dn_mm, n * 2)
                for c in range(4):
                    act.activation(dh[:, c, :], rawd[:, c, :], ACT.Copy).then_inc(dn_hi, 1)
                if not last:
                    for c in range(6):
                        split1(act, n, c)
                act.wait_ge(unit_used, n * 8 + (MOE_AT + 8))
                if not (isinstance(n, int) and n == 0):
                    act.wait_ge(e_h, n)
                act.activation(esg[:, :], ps[:, 4, 0:EF], ACT.Silu).then_inc(e_sg, 1)
                if not last:
                    for c in range(6, 8):
                        split1(act, n, c)
                act.wait_ge(e_tr, n + 1)
                if not (isinstance(n, int) and n == 0):
                    act.wait_ge(dn_mm, n * 2)
                act.activation(hTh[:, :], ps[:, 5, 0:EF], ACT.Copy).then_inc(e_hT, 1)
                if not last:
                    xt(n + 2, par, 1 - pp)

            def store(n, par, h1):
                act.wait_ge(dn_mm, n * 2 - 1)
                if not isinstance(n, int) or n >= 3:
                    act.wait_ge(ye_st[1 - par], h1 * 16)
                act.activation(Ye[:, 1 - par, 0:512], ps[:, 6, :], ACT.Copy).then_inc(ye_a, 1)

            tiles(act, body)
            store(TILES, TILES % 2, TILES // 2)
            ACT_PLE(act, w)

        def split1(act, n, c):
            sl = (MOE_AT + c) % RING
            act.wait_ge(raw_full[sl], n * 16 + 16 * ((MOE_AT + c) // RING + 2))
            act.wait_ge(unit_used, n * 8 + (MOE_AT + c + 1))
            act.activation(hi[:, sl, :], raw[:, sl, :], ACT.Copy).then_inc(hi_ready, 1)

        def split2(dve, n, c):
            sl = (MOE_AT + c) % RING
            dve.wait_ge(hi_ready, n * 8 + (MOE_AT + 8 + c + 1))
            dve.tensor_tensor(lo[:, sl, :], raw[:, sl, :], hi[:, sl, :].bitcast(F32), ALU.subtract).then_inc(lo_ready, 1)

        def ACT_PLE(act, w):
            U = FIRST
            w.n = U["pg0"]
            act_norm(act, 4, xn4, "nple")
            w.upto(U["pg1"] + 8)
            for b in range(2):
                act.wait_ge(unit_used, U[f"pg{b}"] + 8)
                for t in range(T):
                    if b:
                        act.wait_ge(out_ready, t + 1)
                    act.activation(psg[:, t, :], ps[:, 4 * b + t, :], ACT.Sigmoid).then_inc(p_sg, 1)

        def DVE_MOE(dve, w, ch):
            U = FIRST
            dve_norm(dve, 3, xn3, "nffn2")
            w.upto(MOE_AT + 3)
            dve.wait_ge(p_hi, 1)
            dve.tensor_tensor(pTl[:, :, :], pTf[:, :, :], pTh[:, :, :].bitcast(F32), ALU.subtract).then_inc(p_lo, 1)
            dve.wait_ge(unit_used, U["wr"] + 1)
            dve.wait_ge(route_loaded, 48)
            L = R[:, 0, :, :]
            dve.tensor_tensor(L, ps[:, 0, 0:4 * 36].rearrange("p (t n) -> p t n", t=T),
                              rb[:, 0:36].unsqueeze(1).broadcast_to([P, T, 36]), ALU.add).then_inc(r_d, 1)
            dve.wait_ge(r_d, 1)

            def first_of(v, n, k0, idx0=36):
                m = R[:, k0, :, 0:1]
                oh = R[:, k0 + 1, :, 0:n]
                ch.link(dve.tensor_reduce(m, v, AX.X, ALU.max))
                ch.link(dve.tensor_tensor(oh, v, m.broadcast_to([P, T, n]), ALU.is_ge))
                ch.link(dve.tensor_tensor(oh, oh, rb[:, 36:36 + n].unsqueeze(1).broadcast_to([P, T, n]), ALU.mult))
                ch.link(dve.tensor_reduce(R[:, k0 + 2, :, 0:1], oh, AX.X, ALU.max))
                ch.link(dve.tensor_tensor(oh, oh, R[:, k0 + 2, :, 0:1].broadcast_to([P, T, n]), ALU.is_equal))
                return m, oh

            gmax, g1 = first_of(L[:, :, 0:4], 4, 11)
            dve.tensor_tensor(R[:, 1, :, 0:4], L[:, :, 0:4], gmax.broadcast_to([P, T, 4]), ALU.subtract).then_inc(r_d, 1)
            for t in range(T):
                dve.wait_ge(xg_hi, t + 1)
                dve.tensor_tensor(XNl[:, t, :], xn3[:, t, :], XNh[:, t, :].bitcast(F32), ALU.subtract).then_inc(xg_lo, 1)
            pg = R[:, 3, :, 0:32].rearrange("p t (g e) -> p t g e", g=NG)
            ch.link(dve.tensor_tensor(pg, L[:, :, 4:36].rearrange("p t (g e) -> p t g e", g=NG),
                                      g1.unsqueeze(3).broadcast_to([P, T, NG, EG]), ALU.mult))
            E = R[:, 4, :, 0:8]
            ch.link(dve.tensor_reduce(E, R[:, 3, :, 0:32].rearrange("p t (g e) -> p t e g", g=NG), AX.X, ALU.add))
            m1, o1 = first_of(E, 8, 14)
            E2 = R[:, 5, :, 0:8]
            ch.link(dve.scalar_tensor_tensor(E2, o1, NEG, E, ALU.mult, ALU.add))
            m2, o2 = first_of(E2, 8, 17)
            dve.tensor_tensor(R[:, 9, :, 0:1], m2, m1, ALU.subtract).then_inc(r_d, 1)
            dve.wait_ge(r_e, 1)
            ch.link(dve.tensor_reduce(R[:, 6, :, 0:1], R[:, 2, :, 0:4], AX.X, ALU.add))
            dve.wait_ge(r_e, 2)
            ch.link(dve.scalar_tensor_tensor(R[:, 6, :, 1:2], R[:, 10, :, 0:1], 1.0, R[:, 6, :, 0:1], ALU.add, ALU.mult))
            W1, W2 = R[:, 6, :, 2:3], R[:, 6, :, 3:4]
            ch.link(dve.reciprocal(W1, R[:, 6, :, 1:2]))
            ch.link(dve.tensor_tensor(W2, W1, R[:, 10, :, 0:1], ALU.mult))
            O = (R[:, 20, :, 0:NE], R[:, 21, :, 0:NE])
            for k_, o in enumerate((o1, o2)):
                for g in range(NG):
                    ins = dve.tensor_tensor(R[:, 20 + k_, :, 8 * g:8 * g + 8], o, g1[:, :, g:g + 1].broadcast_to([P, T, 8]),
                                            ALU.mult)
            ch.link(ins)
            dve.tensor_tensor(Mb[:, :, :], O[0], O[1], ALU.add).then_inc(mb_ready, 1)
            dve.wait_ge(rk_mm, 1)
            rank = R[:, 23, :, 0:NE]
            ch.mark(dve.tensor_copy(rank, ps[:, 4, 0:T * NE].rearrange("p (t e) -> p t e", t=T)))
            cnt, ov, inc, base, one = [ovw[:, i, :] for i in range(5)]
            ch.link(dve.tensor_copy(cnt, ps[:, 4, T * NE:(T + 1) * NE]))
            ch.mark(dve.memset(one, 1.0))
            ch.link(dve.tensor_scalar(ov, cnt, float(P + 1), None, ALU.is_ge))
            for q_ in (2, 3):
                ch.link(dve.scalar_tensor_tensor(ov, cnt, float(P * q_ + 1), ov, ALU.is_ge, ALU.add))
            ch.link(dve.tensor_tensor_scan(inc, one, ov, 0.0, ALU.mult, ALU.add))
            ch.link(dve.tensor_tensor(base, inc, ov, ALU.subtract))
            rk, bs, ex, qq, fl = [rq_w[:, i, :, :].unsqueeze(3) for i in range(5)]
            both = [P, 2, T, NE]
            for dst, v in ((rk, rank.unsqueeze(1)), (bs, base.unsqueeze(1).unsqueeze(1)),
                           (ex, rb[:, 44:76].unsqueeze(1).unsqueeze(1))):
                ch.link(dve.tensor_tensor(R[:, 17:19, :, 0:NE], R[:, 20:22, :, 0:NE], v.broadcast_to(both), ALU.mult))
                ch.link(dve.tensor_reduce(dst, R[:, 17:19, :, 0:NE], AX.X, ALU.add))
            ch.link(dve.tensor_scalar(fl, rk, float(P), None, ALU.is_ge))
            ch.link(dve.scalar_tensor_tensor(qq, rk, float(2 * P), fl, ALU.is_ge, ALU.add))
            ch.link(dve.scalar_tensor_tensor(qq, rk, float(3 * P), qq, ALU.is_ge, ALU.add))
            ch.link(dve.scalar_tensor_tensor(bs, bs, NE - 1.0, qq, ALU.add, ALU.add))
            ch.link(dve.tensor_tensor(bs, bs, ex, ALU.subtract))
            ch.link(dve.tensor_tensor(bs, bs, fl, ALU.mult))
            ch.link(dve.tensor_tensor(bs, bs, ex, ALU.add))
            ch.link(dve.tensor_tensor(bs, bs, qq, ALU.subtract))
            ch.link(dve.scalar_tensor_tensor(yrow[:, :, :].unsqueeze(3), bs, float(P), rk, ALU.mult, ALU.add))
            dve.tensor_copy(yidx[:, :, :], yrow[:, :, :]).then_inc(yidx_ready, 1)

            def select(p):
                k_ = [0]

                def link(ins):
                    k_[0] += 1
                    ins.then_inc(sel_c, 1)
                    dve.wait_ge(sel_c, p * 3 + k_[0])

                if isinstance(p, int) and p == 0:
                    link(dve.tensor_copy(yrel[:, :, :], yrow[:, :, :]))
                else:
                    dve.wait_ge(xg_ml, p * 4)
                    link(dve.tensor_scalar(yrel[:, :, :], yrel[:, :, :], -2.0 * P, None, ALU.add))
                io = rb[:, 76:76 + 2 * P].unsqueeze(1).broadcast_to([P, T, 2 * P])
                link(dve.tensor_tensor(Se1[:, :, :], io, yrel[:, 0, :].unsqueeze(2).broadcast_to([P, T, 2 * P]), ALU.is_equal))
                link(dve.tensor_tensor(Se2[:, :, :], io, yrel[:, 1, :].unsqueeze(2).broadcast_to([P, T, 2 * P]), ALU.is_equal))
                dve.tensor_tensor(Sel[:, :, :], Se1[:, :, :], Se2[:, :, :], ALU.add).then_inc(xsel, 1)

            dve.wait_ge(unit_used, U["ple1"] + 2)
            select(0)
            w.upto(MOE_AT + 8)
            ch.link(dve.tensor_tensor(eow[:, 0:7, :], rb[:, 44:51].unsqueeze(2).broadcast_to([P, 7, NE]),
                                      inc.unsqueeze(1).broadcast_to([P, 7, NE]), ALU.is_ge))
            ch.link(dve.tensor_reduce(eow[:, 7, 0:7].unsqueeze(2), eow[:, 0:7, :], AX.X, ALU.add))
            dve.tensor_scalar(eov[:, 0:7], eow[:, 7, 0:7], NE - 1.0, None, ALU.min).then_inc(eov_ready, 1)

            def xt(k_, g, pp):
                for b in range(2):
                    dve.wait_ge(xg_ml, k_ * 2 + (b + 1))
                    c = 4 * g + 2 * b
                    dve.tensor_copy(XTl[pp][:, c:c + 2, :], ps[:, 2 + b, :].rearrange("p (c r) -> p c r", c=2)
                                    ).then_inc(xt_l, 1)

            xt(0, 0, 0)
            xt(1, 1, 0)
            dve.wait_ge(b2c, 48)
            ch.link(dve.tensor_tensor(small[:, 32:36], small[:, 24:32:2], small[:, 25:32:2], ALU.add))
            dve.tensor_scalar(small[:, 36:40], small[:, 32:36], 1.0 / D, EPS, ALU.mult, ALU.add).then_inc(ys_ms, 1)

            def store(n, par, h1):
                dve.wait_ge(dn_mm, n * 2)
                if not isinstance(n, int) or n >= 3:
                    dve.wait_ge(ye_st[1 - par], h1 * 16)
                dve.tensor_copy(Ye[:, 1 - par, 512:1024], ps[:, 7, :]).then_inc(ye_b, 1)

            def body(n, par, h, h1, pp):
                last = isinstance(n, int) and n == TILES - 1
                first = isinstance(n, int) and n == 0
                if not last and par == 0:
                    select(h + 1)
                if not first:
                    store(n, par, h1)
                early = 5 if par else 4
                if not last:
                    for c in range(early):
                        split2(dve, n, c)
                dve.wait_ge(e_sg, n + 1)
                if not first:
                    dve.wait_ge(e_tr, n)
                dve.tensor_tensor(hid[:, :], esg[:, :], ps[:, 4, EF:2 * EF], ALU.mult).then_inc(e_h, 1)
                if not last:
                    for c in range(early, 7):
                        split2(dve, n, c)
                dve.wait_ge(e_hT, n + 1)
                if not first:
                    dve.wait_ge(dn_mm, n * 2)
                dve.tensor_tensor(hTl[:, :], ps[:, 5, 0:EF], hTh[:, :].bitcast(F32), ALU.subtract).then_inc(e_hL, 1)
                if not last:
                    split2(dve, n, 7)
                    xt(n + 2, par, 1 - pp)

            tiles(dve, body)
            store(TILES, TILES % 2, TILES // 2)
            dve.wait_ge(ys_rs, 1 + 1)
            dve.wait_ge(prow_loaded, 16)
            for t in range(T):
                dve.scalar_tensor_tensor(ple[:, t, :], ple[:, t, :], small[:, 40 + t:41 + t], prow[:, :],
                                         ALU.mult, ALU.mult).then_inc(ple_done, 1)
            for t in range(T):
                dve.wait_ge(yg[t], (48 if t == 3 else 16) + 32)
                for k_ in range(2):
                    if k_:
                        dve.wait_ge(x_res, 24 + 2 * t + 1)
                    dve.scalar_tensor_tensor(X[:, t, :], YG[:, k_ * T + t, :], R[:, 6, t, 2 + k_:3 + k_], X[:, t, :],
                                             ALU.mult, ALU.add).then_inc(x_res, 1)
                if t:
                    norm_mean(dve, 4, t - 1)
                    norm_scale(dve, 4, t - 1, xn4)
            norm_mean(dve, 4, T - 1)
            norm_scale(dve, 4, T - 1, xn4)
            norm_rest(dve, 4, "nple")
            DVE_PLE(dve, w, ch)

        def DVE_PLE(dve, w, ch):
            U = FIRST
            w.n = U["pg0"]
            w.upto(U["pg1"] + 8)
            for b in range(2):
                for t in range(T):
                    cc = slice(b * 512, (b + 1) * 512)
                    dve.wait_ge(p_sg, 4 * b + t + 1)
                    dve.wait_ge(ple_done, T)
                    ch.link(dve.tensor_tensor(ple[:, t, cc], ple[:, t, cc], psg[:, t, :], ALU.mult))
                    dve.tensor_tensor(X[:, t, cc], X[:, t, cc], ple[:, t, cc], ALU.add).then_inc(out_ready, 1)

        def POOL_MOE(pool):

            pool.wait_ge(x_res, 24)
            pool.dma_start(rb[:, :], rb_d).then_inc(route_loaded, 16)
            pool.dma_start(grow[:, :], rows_d[0]).then_inc(route_loaded, 16)
            pool.dma_start(tri[:, :, :], tri_d).then_inc(route_loaded, 16)
            pool_norm(pool, 3)
            pool.wait_ge(route_loaded, 48)
            pool.wait_ge(n_tr, 32)
            for t in range(T):
                pool.tensor_tensor(xn3[:, t, :], xn3[:, t, :], grow[:, :], ALU.mult).then_inc(xg_f, 1)
            pool.wait_ge(xg_f, T)
            pool.dma_start(prow[:, :], rows_d[1]).then_inc(prow_loaded, 16)
            pool.wait_ge(ys_ms, 1 + 1)
            pool.tensor_tensor(small[:, 40:44], small[:, 36:40], small[:, 48:52], ALU.pow).then_inc(ys_rs, 1)

            def store(n, par, dst):
                pool.wait_ge(ye_a, n + 1)
                pool.wait_ge(ye_b, n + 1)
                pool.dma_start(dst, Ye[:, par, :]).then_inc(ye_st[par], 16)

            def body(n, par, h, h1, pp):
                if not (isinstance(n, int) and n == 0):
                    pool.wait_ge(dn_mm, n * 2)
                for c in range(4):
                    pool.wait_ge(dn_hi, n * 4 + (c + 1))
                    pool.tensor_tensor(dl[:, c, :], rawd[:, c, :], dh[:, c, :].bitcast(F32), ALU.subtract).then_inc(dn_lo, 1)
                if isinstance(n, int):
                    if n:
                        store(n - 1, 1 - par, ye_d[(n - 1) * P:n * P, :])
                else:
                    store(n - 1, 1 - par, ye_d[bass.ds(n * P - P, P), :])

            tiles(pool, body)
            store(TILES - 1, 0, ye_d[(TILES - 1) * P:TILES * P, :])
            pool.wait_ge(yidx_ready, 1)
            pool.wait_ge(ye_st[0], 16 * (TILES // 2 + 1))
            pool.wait_ge(ye_st[1], 16 * (TILES // 2))
            for t in range(T):
                for k_ in range(2):
                    pool.indirect_dma_start(YG[:, k_ * T + t, :], None, ye_d,
                                            bass.IndirectOffsetOnAxis(ap=yidx[:, k_, t:t + 1], axis=0)
                                            ).then_inc(yg[t], 16)
            pool_norm(pool, 4)

        @block.sync
        def _(sp):
            for t in range(T):
                sp.dma_start(X[:, t, :], x[t * P:(t + 1) * P, :]).then_inc(x_loaded[t], 16)
            for c in range(RING):
                sp.dma_start(raw[:, c, :], wstream[c]).then_inc(raw_full[c], 16)

            def reload(u0, n=RING):
                for u in range(u0, u0 + n):
                    sp.wait_ge(lo_ready, u + 1 - RING)
                    sp.dma_start(raw[:, u % RING, :], wstream[u if u < MOE_AT else u - XU]).then_inc(raw_full[u % RING], 16)

            rounds = MOE_AT // RING
            with sp.Fori(1, rounds) as i:
                for c in range(RING):
                    sp.wait_ge(lo_ready, i * RING + (c + 1 - RING))
                    sp.dma_start(raw[:, c, :], wstream[bass.ds(i * RING + c, 1)].rearrange("a p n -> (a p) n")
                                 ).then_inc(raw_full[c], 16)
            reload(rounds * RING, MOE_AT - rounds * RING)
            def gate_up(n, src):
                for c in range(8):
                    u = MOE_AT + c
                    sp.wait_ge(lo_ready, n * 8 + (u + 1 - RING))
                    sp.dma_start(raw[:, u % RING, :], src[c]).then_inc(raw_full[u % RING], 16)

            def down(n, par, src):
                if not isinstance(n, int) or n >= 1:
                    sp.wait_ge(dn_lo, n * 4)
                sp.dma_start(rawd[:, :, :], src).then_inc(dn_full, 16)

            def expert(n, par, e):
                w_e = wexp[bass.ds(e, 1)].rearrange("a c p n -> (a c) p n")
                gate_up(n, w_e)
                down(n, par, w_e[8:12].rearrange("c p n -> p c n"))

            gate_up(0, wexp[0])
            sp.wait_ge(x_res, 24)
            down(0, 0, wexp[0, 8:12].rearrange("c p n -> p c n"))
            gate_up(1, wexp[1])
            down(1, 1, wexp[1, 8:12].rearrange("c p n -> p c n"))
            with sp.Fori(0, NE // 2 - 1) as i:
                for k_ in range(2):
                    expert(i * 2 + (2 + k_), k_, i * 2 + (2 + k_))
            sp.wait_ge(eov_ready, 1)
            for j in range(TILES - NE):
                e = sp.value_load(eov[0:1, j:j + 1], min_val=0, max_val=NE - 1)
                expert(NE + j, j % 2, e)
            reload(FIRST["pg0"], NU - FIRST["pg0"])
            for t in range(T):
                sp.wait_ge(out_ready, 4 + t + 1)
                sp.dma_start(out[t * P:(t + 1) * P, :], X[:, t, :]).then_inc(out_stored, 16)
            sp.wait_ge(out_stored, 16 * T)

        @block.tensor
        def _(pe):
            U = FIRST
            pe.wait_ge(misc_loaded, 80)
            pe_norm(pe, 0, xn, [])
            pe.wait_ge(ht_lo, 4)
            pe_features(pe, U["xbc0"], 8, 0, HTh, HTl, ready=(ht_lo, 0))
            pe.wait_ge(ht_lo, 8)
            for u in range(2):
                pe.wait_ge(lo_ready, U["dtf"] + u + 1)
                w = (U["dtf"] + u) % RING
                for j in range(4):
                    c = 4 * u + j
                    mm = mm3(pe, ps[:, 4, :], hi[:, w, j * P:(j + 1) * P], lo[:, w, j * P:(j + 1) * P],
                             HTh[:, c, :], HTl[:, c, :], c == 0, c == DC - 1)
                mm.then_inc(unit_used, 1)
            pe.wait_ge(dtf_v, 1)
            pe_tokens(pe, U["z0"], 8, 1, HTh, HTl)
            pe.wait_ge(cvD, 4)
            pe_features(pe, U["xbc1"], 8, 0, HTh, HTl)
            pe.wait_ge(z_done, 4)
            pe_features(pe, U["xbc2"], 8, 1, HTh, HTl)
            pe.wait_ge(cvD, 8)
            pe_tokens(pe, U["z1"], 8, 0, HTh, HTl)
            pe.wait_ge(z_done, 8)
            pe.wait_ge(xbc_ready, 12)
            for m in range(10):
                if m >= 4:
                    pe.wait_ge(xs_ready, m - 3)
                for i in range(4):
                    if m < 8:
                        t, kk = m // 2, 4 * (m % 2) + i
                    else:
                        t, kk = 2 * (m - 8) + i // 2, 8 + i % 2
                    tr = pe.transpose(ps[:, m % 4, i * P:(i + 1) * P], xbcT[:, kk, t * P:(t + 1) * P], ident[:, :])
                tr.then_inc(xs_tr, 1)
            for g in range(2):
                for c in range(T):
                    mm = pe.matmul(ps[:, 5 + g, c * P:(c + 1) * P], xbcT[:, 8 + g, c * P:(c + 1) * P],
                                   xbcT[:, 10 + g, c * P:(c + 1) * P], start=True, stop=True)
                mm.then_inc(cb_mm, 1)
            pe.wait_ge(dte_d, 1)
            for i, r in enumerate((3, 2, 5)):
                for t in range(T):
                    tr = pe.transpose(ps[:, 7, (i * T + t) * 32:(i * T + t + 1) * 32], rows[0:32, r, t * P:(t + 1) * P],
                                      ident[0:32, 0:32])
            tr.then_inc(tok_mm, 1)
            pe.wait_ge(ddg, 1)
            pe.matmul(ps[:, 4, 0:4 * H1], rows[0:H1, 6, 0:P], rows[0:H1, 4, 0:4 * H1],
                      start=True, stop=True).then_inc(dec_mm, 1)

            pe.wait_ge(br_lo, 2)
            pe.wait_ge(sel_ready, 1)
            for g in range(2):
                pe.wait_ge(xw_ready, g + 1)
                pe.wait_ge(xs_ready, 10)
                if g == 1:
                    pe.wait_ge(y_add, 4)
                    pe.wait_ge(dcy, 8)
                    pe.wait_ge(yo_done, 3)
                for c in range(3):
                    pe.matmul(ps[:, c, :], Btok[:, c, g * P:(g + 1) * P], xw[:, c, :],
                              start=True, stop=True).then_inc(st_mm, 1)
                for c in range(1, 4):
                    pe.wait_ge(st_ready, 3 * (g + 1))
                    pe.matmul(ps[:, c, :], xbcT[:, 10 + g, c * P:(c + 1) * P], st[:, c - 1, :],
                              start=True, stop=True).then_inc(yo_mm, 1)

                def bcast(i):
                    h = 8 * g + i
                    if i == 0:
                        pe.wait_ge(st_ready, 3 * (g + 1))
                    if i == 1:
                        pe.wait_ge(yo_done, 3 * g + 1)
                    if i >= 2:
                        pe.wait_ge(dcy, h - 1)
                    b = i % 2
                    pe.matmul(ps[:, b, :], sel[0:64, h, :], BR[0:64, :], start=True, stop=False)
                    for c in range(T):
                        mm = pe.matmul(ps[:, b, c * P:(c + 1) * P], identb[:, :], maskT[:, :],
                                       start=False, stop=(c == T - 1))
                    mm.then_inc(bc_mm, 1)

                bcast(0)
                bcast(1)
                for i in range(8):
                    h = 8 * g + i
                    if i + 2 < 8:
                        bcast(i + 2)
                    pe.wait_ge(sc_ready, h + 1)
                    if i == 0:
                        pe.wait_ge(xdw, g + 1)
                        pe.wait_ge(dec_cp, 1)
                        pe.wait_ge(tok_ready, 1)
                        pe.wait_ge(cb_ready, 2)
                    for c in range(T):
                        mm = pe.matmul(ps[:, 4 + c, i * HD:(i + 1) * HD], SC[:, h % 4, c * P:(c + 1) * P],
                                       xd[:, c, i * HD:(i + 1) * HD], start=True, stop=True)
                    mm.then_inc(yd_mm, 1)
            pe.wait_ge(yo_done, 6)
            pe.wait_ge(dcy, 16)
            pe_tokens(pe, U["q0"], 8, 0, HTh, HTl)
            pe.wait_ge(ys_n, 1)
            pe.wait_ge(y_add, 8)
            for c in range(DC):
                if c >= 4:
                    pe.wait_ge(mix_lo, c - 3)
                for t in range(T):
                    tr = pe.transpose(ps[:, 4 + c % 4, t * P:(t + 1) * P], Y1[:, t, c * P:(c + 1) * P], ident[:, :])
                tr.then_inc(mix_tr, 1)

            for b in range(1, 6):
                if b == 1:
                    pe.wait_ge(mix_lo, 8)
                else:
                    pe.wait_ge(qkv_copied, 4 * (b - 1))
                pe_tokens(pe, U["qqkkvv"[b] + str(b % 2)], 8, b % 2, HTh, HTl)
            for c in range(DC):
                for i, src in enumerate((q, k)):
                    if c >= 4:
                        pe.wait_ge((qT_done, kT_done)[i], c - 3)
                    elif c == 0:
                        pe.wait_ge(qk_n, 1)
                        pe.wait_ge(qkv_copied, 24)
                    for t in range(T):
                        tr = pe.transpose(ps[:, 4 * i + c % 4, t * P:(t + 1) * P], src[:, t, c * P:(c + 1) * P],
                                          ident[:, :])
                    tr.then_inc(qk_tr, 1)

            def scores(h, g):
                r = slice(HD * (h % 2), HD * (h % 2) + HD)
                if h == 0:
                    pe.wait_ge(sel_z, 1)
                    pe.wait_ge(qT_done, 8)
                    pe.wait_ge(kT_done, 8)
                else:
                    pe.wait_ge(fx_exp, NG_ * (h - 1) + g + 1)
                bank, parts = FG[g]
                for i, o in parts:
                    n = (i + 1) * P
                    pe.matmul(ps[:, bank, o:o + n], qT[r, h // 2, i * P:(i + 1) * P], kT[r, h // 2, 0:n],
                              start=True, stop=False)
                    pe.matmul(ps[:, bank, o:o + n], sel[:, h, :], BR[:, 0:n], start=False, stop=False)
                    mm = pe.matmul(ps[:, bank, o + n - P:o + n], identb[:, :], maskL[:, :], start=False, stop=True)
                mm.then_inc(fx_qk, 1)

            def values(h):
                pe.wait_ge(fx_pA, h + 1)
                pe.wait_ge(fx_pD, h + 1)
                pr = h // 2
                if pr >= 2:
                    pe.wait_ge(fx_lo, pr - 1)
                for j in range(T):
                    mm = pe.matmul(ps[HD * (h % 2):HD * (h % 2) + HD, 6 + pr % 2, j * P:S], v[:, j, h * HD:(h + 1) * HD],
                                   PT[:, PTO[j]:PTO[j] + S - j * P], start=(j == 0), stop=(j == T - 1))
                mm.then_inc(fx_pv, 1)

            for g in range(NG_):
                scores(0, g)
            for h in range(H1):
                if h + 1 < H1:
                    scores(h + 1, 0)
                    scores(h + 1, 1)
                if h:
                    values(h - 1)
                if h + 1 < H1:
                    scores(h + 1, 2)
                for g in range(NG_):
                    pe.wait_ge(fx_pn, NG_ * h + g + 1)
                    if g == 0 and h:
                        pe.wait_ge(fx_pA, h)
                        pe.wait_ge(fx_pD, h)
                    for i, _o in FG[g][1]:
                        for j in range(i + 1):
                            bank, o = PTB[j]
                            tr = pe.transpose(ps[:, bank, o + (i - j) * P:o + (i - j + 1) * P],
                                              Pb[:, h % 2, FOFF[i] + j * P:FOFF[i] + (j + 1) * P], ident[:, :])
                tr.then_inc(fx_t, 1)
            values(H1 - 1)

            pe.wait_ge(fx_lo, 8)
            for b in range(2):
                pe_tokens(pe, U[f"out{b}"], 8, b, MIXh0, MIXl0, last=False)
                pe_tokens(pe, U[f"out{b}"] + 8, 8, b, MIXh1, MIXl1, first=False)
            pe_norm(pe, 1, xnF, [(x_res, 8)])
            u = U["up0"]
            pe.wait_ge(ht_lo, 12)
            pe_features(pe, u, 8, 0, HTh, HTl, ready=(ht_lo, 8))
            with pe.Fori(0, 5) as i:
                for s_ in range(2):
                    st_ = (1 + s_) % 2
                    pe.wait_ge(ffD, i * 8 + (4 * s_ + 1))
                    pe_features(pe, i * 16 + (u + 8 + 8 * s_), 8, st_, HTh, HTl, slot=u + 8 + 8 * s_)
            for b in range(2):
                pe.wait_ge(ffD, 1 + 4 * (10 + b))
                pe_tokens(pe, U[f"down{b}"], FF // P, (1 + b) % 2, gh, gl, ready=(ff_lo, 1) if b == 0 else None)
            PE_B2(pe)

        class Splits:

            def __init__(self, eng, one):
                self.eng, self.one, self.n = eng, one, 0

            def upto(self, n):
                if n > self.n:
                    self.one(self.eng, self.n, n - self.n)
                    self.n = n

            def beside(self, n, pieces):
                pieces = list(pieces)
                total = max(1, n - self.n)
                each = -(-len(pieces) // total)
                for i in range(total):
                    self.upto(self.n + 1)
                    for _ in range(each):
                        if pieces:
                            pieces.pop(0)()
                for p in pieces:
                    p()

        @block.scalar
        def _(act):
            U = FIRST
            ch = Chain(act, act_c)
            w = Splits(act, act_split)
            for dst, src in ((ident, ident_d), (cst, cst_d), (identb, identb_d), (maskT, maskT_d), (maskL, maskL_d)):
                act.dma_start(dst[:, :], src).then_inc(misc_loaded, 16)
            act_norm(act, 0, xn, "nmix")
            w.upto(U["z0"] + 6)
            act.wait_ge(sel_loaded, 16)
            act.activation(sel[:, :, :], selF[:, :, :], ACT.Copy).then_inc(sel_ready, 1)
            ch.mark(act.activation(small[:, 18:19], col("qw"), ACT.Copy, scale=HD ** -0.5))
            ch.mark(act.activation(small[:, 19:20], col("sqw"), ACT.Copy, scale=HD ** -0.5))

            def silu_x(kk):
                act.wait_ge(cvD, kk + 1)
                act.activation(xbcT[:, kk, :], acc[:, kk % 4, :], ACT.Silu).then_inc(xbc_ready, 1)

            def conv_x(b, m):
                def piece():
                    kk = 4 * b + m
                    act.wait_ge(unit_used, U[f"xbc{b}"] + 8)
                    if kk >= 4:
                        act.wait_ge(xbc_ready, kk - 3)
                    act.activation(acc[:, m, :], ps[:, 4 * (b // 2) + m, :], ACT.Identity,
                                   scale=col("cw", 4 * kk + 3), bias=col("cb", kk)).then_inc(cvA, 1)
                    if kk:
                        silu_x(kk - 1)
                return piece

            def silu_z(b, t):
                def piece():
                    act.wait_ge(unit_used, U[f"z{b}"] + 8)
                    act.activation(zs[:, t, b * 512:(b + 1) * 512], ps[:, 4 * ((b + 1) % 2) + t, :],
                                   ACT.Silu).then_inc(z_done, 1)
                return piece

            def gates_exp():
                act.wait_ge(dtf_v, 2)
                act.activation(rows[:, 2, :], rows[:, 1, :], ACT.Exp).then_inc(dtf_e, 1)
                act.activation(small[:, 16:17], col("alog"), ACT.Exp).then_inc(dtf_e, 1)

            def gates_log():
                act.wait_ge(dtf_s, 1)
                act.activation(rows[:, 1, :], rows[:, 3, :], ACT.Ln).then_inc(dtf_l, 1)

            def gates_decay():
                act.wait_ge(dtf_cs, 5)
                act.activation(BR[:, :], rows[:, 2, :], ACT.Copy).then_inc(br_hi, 1)
                for c in range(T):
                    end = rows[0:32, 2, c * P + P - 1:c * P + P]
                    act.activation(rows[0:32, 5, c * P:(c + 1) * P], rows[0:32, 2, c * P:(c + 1) * P], ACT.Exp,
                                   bias=end, scale=-1.0).then_inc(dte_a, 1)
                act.activation(small[0:H1, 20:24], rows[0:H1, 2, P - 1:S:P], ACT.Exp).then_inc(dte_a, 1)

            w.beside(U["xbc1"] + 2, [gates_exp, conv_x(0, 0), conv_x(0, 1), gates_log, conv_x(0, 2), conv_x(0, 3)])
            w.upto(U["xbc2"])
            w.beside(U["z1"], [silu_z(0, t) for t in range(4)] + [gates_decay])
            w.beside(U["q0"], [conv_x(1, m) for m in range(4)])
            w.beside(U["q0"] + 8, [conv_x(2, m) for m in range(4)] + [lambda: silu_x(11)])
            for t in range(T):
                silu_z(1, t)()

            for m in range(10):
                act.wait_ge(xs_tr, m + 1)
                if m < 8:
                    dst = xs[:, m // 2, (m % 2) * 512:(m % 2 + 1) * 512]
                    src = ps[:, m % 4, :]
                else:
                    dst = Btok[:, 2 * (m - 8):2 * (m - 8) + 2, :]
                    src = ps[:, m % 4, :].rearrange("p (t n) -> p t n", t=2)
                act.activation(dst, src, ACT.Copy).then_inc(xs_ready, 1)
            act.wait_ge(tok_ready, 1)
            act.activation(tok[:, 3, :, :], tok[:, 1, :, :], ACT.Exp).then_inc(etok, 1)
            w.upto(U["q0"] + 8)
            act.wait_ge(ncum, 1)
            act.wait_ge(xbc_ready, 12)
            for h in range(H1):
                act.wait_ge(bc_mm, h + 1)
                if h >= 4:
                    act.wait_ge(yd_mm, h - 3)
                for c in range(T):
                    ins = act.activation(SC[:, h % 4, c * P:(c + 1) * P], ps[:, h % 2, c * P:(c + 1) * P], ACT.Exp,
                                         bias=tok[:, 1, c, h:h + 1])
                ins.then_inc(dcy, 1)
            act.wait_ge(y_done, 8)
            for g in range(2):
                for t in range(T):
                    ins = act.activation((xw, xd)[g][:, t, :], Y1[:, t, g * 512:(g + 1) * 512], ACT.Square,
                                         accum_out=small[:, 24 + 2 * t + g:25 + 2 * t + g])
            ins.then_inc(ys_ss, 1)
            for c in range(DC):
                act.wait_ge(mix_tr, c + 1)
                act.activation(MIXh0[:, c, :], ps[:, 4 + c % 4, :], ACT.Identity, scale=col("nssd", c)).then_inc(mix_hi, 1)

            def copy_qkv(b, t):
                def piece():
                    act.wait_ge(unit_used, U["qqkkvv"[b] + str(b % 2)] + 8)
                    if b == 0 and t == 0:
                        act.wait_ge(mix_tr, 8)
                    act.activation((q, k, v)[b // 2][:, t, (b % 2) * 512:(b % 2 + 1) * 512], ps[:, 4 * (b % 2) + t, :],
                                   ACT.Copy).then_inc(qkv_copied, 1)
                return piece

            w.upto(U["q1"] + 8)
            for b in range(4):
                w.beside(U["qqkkvv"[b + 2] + str(b % 2)] + 8, [copy_qkv(b, t) for t in range(T)])
            act.wait_ge(qk_ss, 1)
            act.activation(qst3[:, :, :, :], qst2[:, :, :, :], ACT.Ln).then_inc(qk_ln, 1)
            act.wait_ge(qk_ln, 1)
            act.activation(qst[:, :, :, :], qst3[:, :, :, :], ACT.Exp, scale=-0.5).then_inc(qk_ln, 1)
            w.beside(U["out0"], [copy_qkv(4, t) for t in range(T)])
            for t in range(T):
                copy_qkv(5, t)()
            w.upto(U["out0"] + 8)
            for c in range(DC):
                act.wait_ge(qk_tr, 2 * c + 1)
                act.activation(qT[:, c, :], ps[:, c % 4, :], ACT.Identity, scale=small[:, 18:19]).then_inc(qT_done, 1)

            def weights(h, g):
                act.wait_ge(fx_nm, NG_ * h + g + 1)
                if h >= 2:
                    act.wait_ge(fx_t, h - 1)
                bank, parts = FG[g]
                for i, o in parts:
                    n = (i + 1) * P
                    ins = act.activation(Pb[:, h % 2, FOFF[i]:FOFF[i] + n], ps[:, bank, o:o + n], ACT.Exp,
                                         bias=fst[:, 0, h % 2, i:i + 1], accum_out=fst[:, 1, h % 2, i:i + 1])
                ins.then_inc(fx_exp, 1)

            def transposed(h):
                act.wait_ge(fx_t, h + 1)
                if h:
                    act.wait_ge(fx_pv, h)
                act.activation(PT[:, 0:512], ps[:, 3, :], ACT.Copy).then_inc(fx_pA, 1)

            def output(h):
                act.wait_ge(fx_pv, h + 1)
                act.activation(MIXh1[:, h // 2, :], ps[:, 6 + h // 2 % 2, :], ACT.Copy).then_inc(fx_hi, 1)

            for g in range(NG_):
                weights(0, g)
            for h in range(H1):
                if h:
                    transposed(h - 1)
                if h + 1 < H1:
                    weights(h + 1, 0)
                    weights(h + 1, 1)
                if h + 1 < H1:
                    weights(h + 1, 2)
                if h and h % 2 == 0:
                    output(h - 1)
            transposed(H1 - 1)
            output(H1 - 1)
            w.upto(U["out0"] + 16)
            w.upto(U["out1"] + 16)
            w.upto(U["up0"] + 8)
            act_norm(act, 1, xnF, "nffn")
            w.upto(U["up1"] + 8)

            def split8(u0):
                for c in range(RING):
                    sl = (U["up0"] + c) % RING
                    act.wait_ge(raw_full[sl], (u0 + c - sl) * 2 + 16)
                    act.wait_ge(unit_used, u0 + (c - RING + 1))
                    act.activation(hi[:, sl, :], raw[:, sl, :], ACT.Copy).then_inc(hi_ready, 1)
                    yield

            def conv_f(b, s_, m):
                f = b * 2 + (m if m < 2 else FF // P + m - 2)
                act.activation(facc[:, m, :], ps[:, 4 * s_ + m, :], ACT.Identity, scale=col_at("fw", f * 3 + 2),
                               bias=col_at("fb", f)).then_inc(ffA, 1)

            def post_f(b, s_, pump):
                act.wait_ge(unit_used, b * 8 + (U["up0"] + 8))
                act.wait_ge(ff_g, b * 2 + 1)
                for m in range(4):
                    conv_f(b, s_, m)
                    pump()
                for m in range(2):
                    act.wait_ge(ffD, b * 4 + (m + 2))
                    act.activation(fsg[:, m, :], facc[:, m, :], ACT.Silu).then_inc(ff_sg, 1)
                    pump()
                for m in range(2):
                    act.wait_ge(ff_g, b * 2 + (m + 2))
                    if isinstance(b, int):
                        dst = gh[:, 2 * b + m, :]
                    else:
                        dst = gh[:, bass.ds(b * 2 + m, 1), :]
                    act.activation(dst, fg[:, m, :] if isinstance(b, int) else fg[:, m:m + 1, :], ACT.Copy).then_inc(ff_hi, 1)
                    pump()

            def steps(gen):
                def pump():
                    next(gen, None)
                return pump

            def drain(gen):
                for _ in gen:
                    pass

            with act.Fori(0, 5) as i:
                for s_ in range(2):
                    b = i * 2 + s_
                    gen = split8(i * 16 + (U["up2"] + 8 * s_))
                    post_f(b, s_, steps(gen))
                    drain(gen)
            w.n = U["up2"] + 80
            assert w.n == U["down0"] + 8
            post_f(10, 0, lambda: None)
            w.upto(U["rq"] + 8)
            ACT_B2(act, w, ch)

        @block.vector
        def _(dve):
            U = FIRST
            ch = Chain(dve, dve_c)
            w = Splits(dve, dve_split)
            dve.wait_ge(misc_loaded, 80)
            dve.memset(small[:, 56:57], 0.0).then_inc(ffD, 1)
            dve.memset(small[:, 57:58], 0.0).then_inc(ff_g, 1)
            dve_norm(dve, 0, xn, "nmix")

            def conv_x(b, m):
                def piece():
                    kk = 4 * b + m
                    dve.wait_ge(cvA, kk + 1)
                    for j in (2, 1, 0):
                        sh = 3 - j
                        ins = dve.scalar_tensor_tensor(acc[:, m, sh:], ps[:, 4 * (b // 2) + m, 0:S - sh],
                                                       col("cw", 4 * kk + j), acc[:, m, sh:], ALU.mult, ALU.add)
                        if j:
                            ch.link(ins)
                    ins.then_inc(cvD, 1)
                return piece

            V, E0, E, S1, Q, RC, ONE = range(7)

            def gates_rows():
                dve.wait_ge(n_tr, 8)
                ch.link(dve.memset(rows[:, ONE, :], 1.0))
                dve.wait_ge(unit_used, U["z0"])
                dve.tensor_scalar(rows[:, V, :], ps[:, 4, :], col("dtb"), col("sgn"), ALU.add, ALU.mult).then_inc(dtf_v, 1)
                dve.wait_ge(dtf_v, 1)
                dve.scalar_tensor_tensor(rows[:, E0, :], rows[:, V, :], -1.0, rows[:, V, :], ALU.mult, ALU.min
                                         ).then_inc(dtf_v, 1)

            def gates_rounding():
                dve.wait_ge(dtf_e, 2)
                dve.tensor_scalar(rows[:, S1, :], rows[:, E, :], 1.0, None, ALU.add).then_inc(dtf_s, 1)
                dve.wait_ge(dtf_s, 1)
                ch.mark(dve.scalar_tensor_tensor(rows[:, Q, :], rows[:, S1, :], 1.0, rows[:, E, :], ALU.subtract, ALU.subtract))
                ch.link(dve.reciprocal(rows[:, RC, :], rows[:, S1, :]))
                ch.link(dve.tensor_tensor(rows[:, Q, :], rows[:, Q, :], rows[:, RC, :], ALU.mult))

            def gates_sums():
                dve.wait_ge(dtf_l, 1)
                ch.link(dve.tensor_tensor(rows[:, E0, :], rows[:, E0, :], rows[:, Q, :], ALU.subtract))
                ch.link(dve.scalar_tensor_tensor(rows[:, S1, :], rows[:, V, :], 0.0, rows[:, E0, :], ALU.max, ALU.add))
                ch.link(dve.tensor_scalar(small[:, 17:18], small[:, 16:17], col("asg"), None, ALU.mult))
                ch.link(dve.tensor_scalar(rows[:, Q, :], rows[:, S1, :], small[:, 17:18], None, ALU.mult))
                for c in range(T):
                    cc = slice(c * P, (c + 1) * P)
                    dve.tensor_tensor_scan(rows[0:64, 2, cc], rows[0:64, ONE, cc], rows[0:64, Q, cc], 0.0,
                                           ALU.mult, ALU.add).then_inc(dtf_cs, 1)
                dve.tensor_tensor_scan(rows[64:128, 2, :], rows[64:128, ONE, :], rows[64:128, Q, :], 0.0,
                                       ALU.mult, ALU.add).then_inc(dtf_cs, 1)

            def gates_decay():
                dve.wait_ge(dtf_cs, 5)
                dve.wait_ge(br_hi, 1)
                for r in (slice(32, 64), slice(96, 128)):
                    dve.tensor_tensor(BR[r, :], rows[r, 2, :], BR[r, :].bitcast(F32), ALU.subtract).then_inc(br_lo, 1)
                dve.wait_ge(dte_a, 5)
                dve.tensor_tensor(rows[0:32, 5, :], rows[0:32, 5, :], rows[0:32, S1, :], ALU.mult).then_inc(dte_d, 1)
                for c in range(T):
                    ins = dve.tensor_scalar(rows[0:H1, Q, c * H1:(c + 1) * H1], ident[0:H1, 0:H1],
                                            small[0:H1, 20 + c:21 + c], None, ALU.mult)
                ins.then_inc(ddg, 1)

            w.upto(U["z0"] + 4)
            gates_rows()
            w.beside(U["xbc1"] + 2, [conv_x(0, 0), gates_rounding, conv_x(0, 1), conv_x(0, 2), gates_sums, conv_x(0, 3)])
            w.upto(U["z1"])
            gates_decay()
            w.beside(U["q0"], [conv_x(1, m) for m in range(4)])
            w.beside(U["q0"] + 8, [conv_x(2, m) for m in range(4)])
            for g in range(2):
                dve.wait_ge(cb_mm, g + 1)
                dve.wait_ge(sel_ready, 1)
                dve.tensor_copy(cbS[:, g, :], ps[:, 5 + g, :]).then_inc(cb_ready, 1)
            dve.wait_ge(tok_mm, 1)
            dve.tensor_copy(tok[:, 0:3, :, :].rearrange("p a t h -> p (a t h)"), ps[:, 7, 0:384]).then_inc(tok_ready, 1)
            dve.wait_ge(dec_mm, 1)
            dve.tensor_copy(decB, ps[:, 4, 0:4 * H1]).then_inc(dec_cp, 1)
            w.upto(U["q0"] + 8)
            dve.wait_ge(xs_ready, 10)
            dve.wait_ge(etok, 1)
            dve.tensor_scalar(tok[:, 1, :, :], tok[:, 1, :, :], -1.0, None, ALU.mult).then_inc(ncum, 1)
            dve.wait_ge(tok_ready, 1)
            dve.wait_ge(dec_cp, 1)

            def heads(a):
                return a.rearrange("p (h e) -> p h e", h=8)

            def per_head(a):
                return a.unsqueeze(2).broadcast_to([P, 8, HD])

            for g in range(2):
                G = slice(g * 512, (g + 1) * 512)
                hs = slice(8 * g, 8 * g + 8)
                if g:
                    dve.wait_ge(yd_mm, 8)
                    dve.wait_ge(yo_mm, 3)
                if g == 0:
                    for t in range(T):
                        i1 = dve.tensor_tensor(heads(xw[:, t, :]), heads(xs[:, t, G]), per_head(tok[:, 2, t, hs]), ALU.mult)
                    i1.then_inc(xw_ready, 1)
                for t in range(T):
                    i1 = dve.tensor_tensor(heads(xd[:, t, :]), heads(xs[:, t, G]), per_head(tok[:, 0, t, hs]), ALU.mult)
                i1.then_inc(xdw, 1)
                if g:
                    dve.wait_ge(yo_mm, 3)
                dve.wait_ge(st_mm, 3 * g + 1)
                dve.tensor_copy(st[:, 0, :], ps[:, 0, :]).then_inc(st_ready, 1)
                for c in (1, 2):
                    dve.wait_ge(st_ready, 3 * g + c)
                    ch.link(dve.tensor_tensor(heads(st[:, c, :]), heads(st[:, c - 1, :]),
                                              per_head(decB[:, c * H1 + 8 * g:c * H1 + 8 * g + 8]), ALU.mult))
                    dve.wait_ge(st_mm, 3 * g + c + 1)
                    dve.tensor_tensor(st[:, c, :], st[:, c, :], ps[:, c, :], ALU.add).then_inc(st_ready, 1)
                for c in range(1, T):
                    dve.wait_ge(yo_mm, 3 * g + c)
                    if c > 1:
                        ch.wait()
                    dve.tensor_tensor(heads(yt[:, :]), heads(ps[:, c, :]), per_head(tok[:, 3, c, hs]),
                                      ALU.mult).then_inc(yo_done, 1)
                    dve.wait_ge(yo_done, 3 * g + c)
                    dve.wait_ge(skip, T * g + c + 1)
                    ch.mark(dve.tensor_tensor(Y1[:, c, G], Y1[:, c, G], yt[:, :], ALU.add))
                def sc_h(h):
                    dve.wait_ge(dcy, h + 1)
                    dve.wait_ge(cb_ready, 2)
                    dve.tensor_tensor(SC[:, h % 4, :], SC[:, h % 4, :], cbS[:, g, :], ALU.mult).then_inc(sc_ready, 1)

                for h in range(8 * g, 8 * g + 8):
                    sc_h(h)
                dve.wait_ge(yd_mm, 8 * g + 8)
                ch.wait()
                for t in range(T):
                    dve.wait_ge(skip, T * g + t + 1)
                    dve.tensor_tensor(Y1[:, t, G], Y1[:, t, G], ps[:, 4 + t, :], ALU.add).then_inc(y_add, 1)
                if g:
                    for t in range(2):
                        dve.wait_ge(y_add, 4 + t + 1)
                        dve.tensor_tensor(Y1[:, t, G], Y1[:, t, G], zs[:, t, G], ALU.mult).then_inc(y_done, 1)
            dve.wait_ge(ys_ss, 1)
            dve.tensor_scalar(small[:, 32:40], small[:, 24:32], 1.0 / 512, EPS, ALU.mult, ALU.add).then_inc(ys_ms, 1)
            dve.wait_ge(ys_rs, 1)
            for t in range(T):
                for g in range(2):
                    ins = dve.tensor_scalar(Y1[:, t, g * 512:(g + 1) * 512], Y1[:, t, g * 512:(g + 1) * 512],
                                            small[:, 40 + 2 * t + g:41 + 2 * t + g], None, ALU.mult)
            ins.then_inc(ys_n, 1)
            for c in range(DC):
                dve.wait_ge(mix_hi, c + 1)
                dve.scalar_tensor_tensor(MIXl0[:, c, :], ps[:, 4 + c % 4, :], col("nssd", c), MIXh0[:, c, :].bitcast(F32),
                                         ALU.mult, ALU.subtract).then_inc(mix_lo, 1)

            def squares(b, t):
                def piece():
                    src = (q, k)[b // 2][:, t, (b % 2) * 512:(b % 2 + 1) * 512]
                    dve.wait_ge(qkv_copied, 4 * b + t + 1)
                    ch.wait()
                    ch.link(dve.tensor_tensor(sqr[:, t % 2, :], src, src, ALU.mult))
                    ch.mark(dve.tensor_reduce(qst[:, b // 2, t, 8 * (b % 2):8 * (b % 2) + 8],
                                              heads(sqr[:, t % 2, :]), AX.X, ALU.add))
                return piece

            w.upto(U["q1"] + 8)
            for b in range(4):
                w.beside(U["qqkkvv"[b + 2] + str(b % 2)] + 8, [squares(b, t) for t in range(T)])
            ch.wait()
            dve.tensor_scalar(qst2[:, :, :, :], qst[:, :, :, :], 1.0 / HD, EPS, ALU.mult, ALU.add).then_inc(qk_ss, 1)
            dve.wait_ge(qk_ln, 2)
            dve.wait_ge(qk_ss, 1)
            ch.link(dve.tensor_tensor(qst3[:, :, :, :], qst[:, :, :, :], qst[:, :, :, :], ALU.mult))
            ch.link(dve.tensor_tensor(qst3[:, :, :, :], qst3[:, :, :, :], qst2[:, :, :, :], ALU.mult))
            ch.link(dve.tensor_scalar(qst3[:, :, :, :], qst3[:, :, :, :], -0.5, 1.5, ALU.mult, ALU.add))
            ch.link(dve.tensor_tensor(qst3[:, :, :, :], qst3[:, :, :, :], qst[:, :, :, :], ALU.mult))

            def scale_qk(i, t):
                def piece():
                    src = (q, k)[i][:, t, :].rearrange("p (h e) -> p h e", h=H1)
                    ins = dve.tensor_tensor(src, src, qst3[:, i, t, :].unsqueeze(2).broadcast_to([P, H1, HD]), ALU.mult)
                    if (i, t) == (1, T - 1):
                        ins.then_inc(qk_n, 1)
                return piece

            w.beside(U["out0"], [scale_qk(i, t) for i in range(2) for t in range(T)])
            w.upto(U["out0"] + 8)
            for c in range(DC):
                dve.wait_ge(qk_tr, 2 * c + 2)
                dve.tensor_scalar(kT[:, c, :], ps[:, 4 + c % 4, :], col("kw"), None, ALU.mult).then_inc(kT_done, 1)

            def maxima(h, g):
                dve.wait_ge(fx_qk, NG_ * h + g + 1)
                if h >= 2:
                    dve.wait_ge(fx_exp, NG_ * (h - 1))
                bank, parts = FG[g]
                for i, o in parts:
                    ins = dve.tensor_reduce(fst[:, 0, h % 2, i:i + 1], ps[:, bank, o:o + (i + 1) * P], AX.X, ALU.max,
                                            negate=True)
                ins.then_inc(fx_nm, 1)

            def normalize(h, g):
                dve.wait_ge(fx_exp, NG_ * h + g + 1)
                parts = FG[g][1]
                for i, _o in parts:
                    ins = dve.reciprocal(fst[:, 2, h % 2, i:i + 1], fst[:, 1, h % 2, i:i + 1])
                ch.link(ins)
                for i, _o in parts:
                    ins = dve.tensor_scalar(Pb[:, h % 2, FOFF[i]:FOFF[i] + (i + 1) * P], Pb[:, h % 2, FOFF[i]:FOFF[i] + (i + 1) * P],
                                            fst[:, 2, h % 2, i:i + 1], None, ALU.mult)
                ins.then_inc(fx_pn, 1)

            def head(h):
                maxima(h, 0)
                maxima(h, 1)
                normalize(h, 0)
                normalize(h, 1)
                maxima(h, 2)
                normalize(h, 2)

            def transposed(h):
                dve.wait_ge(fx_t, h + 1)
                if h:
                    dve.wait_ge(fx_pv, h)
                dve.tensor_copy(PT[:, 512:1024], ps[:, 4, :])
                dve.tensor_copy(PT[:, 1024:1280], ps[:, 5, 0:256]).then_inc(fx_pD, 1)

            def output(h):
                pr = h // 2
                dve.wait_ge(fx_hi, pr + 1)
                dve.tensor_tensor(MIXl1[:, pr, :], ps[:, 6 + pr % 2, :], MIXh1[:, pr, :].bitcast(F32),
                                  ALU.subtract).then_inc(fx_lo, 1)

            head(0)
            for h in range(H1):
                if h:
                    transposed(h - 1)
                if h + 1 < H1:
                    head(h + 1)
                if h > 1 and h % 2:
                    output(h - 2)
            transposed(H1 - 1)
            output(H1 - 1)

            def residual(name, s_, b):
                def make(t):
                    def piece():
                        dve.wait_ge(unit_used, FIRST[name] + UNITS[name])
                        dve.tensor_tensor(X[:, t, b * 512:(b + 1) * 512], X[:, t, b * 512:(b + 1) * 512],
                                          ps[:, 4 * s_ + t, :], ALU.add).then_inc(x_res, 1)
                    return piece
                return [make(t) for t in range(T)]

            w.upto(U["out0"] + 16)
            w.upto(U["out1"] + 8)
            w.beside(U["out1"] + 16, residual("out0", 0, 0))
            w.upto(U["up0"] + 8)
            for p in residual("out1", 1, 1):
                p()
            dve_norm(dve, 1, xnF, "nffn")
            w.upto(U["up1"] + 8)

            def split8(u0):
                for c in range(RING):
                    sl = (U["up0"] + c) % RING
                    dve.wait_ge(hi_ready, u0 + (c + 1))
                    dve.tensor_tensor(lo[:, sl, :], raw[:, sl, :], hi[:, sl, :].bitcast(F32), ALU.subtract
                                      ).then_inc(lo_ready, 1)
                    yield

            def post_f(b, s_, pump):
                for m in range(4):
                    f = b * 2 + (m if m < 2 else FF // P + m - 2)
                    dve.wait_ge(ffA, b * 4 + (m + 1))
                    for j in (1, 0):
                        sh = 2 - j
                        wcol = col_at("fw", f * 3 + j)
                        ins = dve.scalar_tensor_tensor(facc[:, m, sh:], ps[:, 4 * s_ + m, 0:S - sh], wcol,
                                                       facc[:, m, sh:], ALU.mult, ALU.add)
                        if j:
                            ins.then_inc(ff_c, 1)
                            pump()
                            dve.wait_ge(ff_c, b * 4 + (m + 1))
                    ins.then_inc(ffD, 1)
                for m in range(2):
                    dve.wait_ge(ff_sg, b * 2 + (m + 1))
                    dve.wait_ge(ffD, b * 4 + 5)
                    dve.wait_ge(ff_lo, b * 2 + 1)
                    dve.tensor_tensor(fg[:, m, :], fsg[:, m, :], facc[:, 2 + m, :], ALU.mult).then_inc(ff_g, 1)
                    pump()
                for m in range(2):
                    dve.wait_ge(ff_hi, b * 2 + (m + 1))
                    if isinstance(b, int):
                        dve.tensor_tensor(gl[:, 2 * b + m, :], fg[:, m, :], gh[:, 2 * b + m, :].bitcast(F32),
                                          ALU.subtract).then_inc(ff_lo, 1)
                    else:
                        dve.tensor_tensor(gl[:, bass.ds(b * 2 + m, 1), :], fg[:, m:m + 1, :],
                                          ghF[:, bass.ds(b * 2 + m, 1), :], ALU.subtract).then_inc(ff_lo, 1)
                    pump()

            ghF = gh[:, :, :].bitcast(F32)
            dve.memset(small[:, 58:59], 0.0).then_inc(ff_lo, 1)
            with dve.Fori(0, 5) as i:
                for s_ in range(2):
                    gen = split8(i * 16 + (U["up2"] + 8 * s_))
                    post_f(i * 2 + s_, s_, lambda: next(gen, None))
                    for _ in gen:
                        pass
            w.n = U["up2"] + 80
            post_f(10, 0, lambda: None)
            w.upto(U["down1"] + 8)
            w.beside(U["down1"] + 16, residual("down0", 1, 0))
            w.upto(U["rq"] + 8)
            for p in residual("down1", 0, 1):
                p()
            DVE_B2(dve, w, ch)

        @block.gpsimd
        def _(pool):
            pool.memset(small[:, 12:16], -0.5).then_inc(pool_c, 1)
            pool.memset(small[:, 48:56], -0.5).then_inc(pool_c, 1)
            pool.wait_ge(pool_c, 2)
            pool_norm(pool, 0)
            pool.dma_start(selF[:, :, :], sel_d).then_inc(sel_loaded, 16)
            def heads(a):
                return a.rearrange("p (h e) -> p h e", h=8)

            def per_head(a):
                return a.unsqueeze(2).broadcast_to([P, 8, HD])

            pool.wait_ge(xs_ready, 8)
            pool.wait_ge(xs_tr, 8)
            for g in range(2):
                G = slice(g * 512, (g + 1) * 512)
                if g:
                    pool.wait_ge(st_mm, 3)
                    pool.wait_ge(etok, 1)
                    for t in range(T):
                        ins = pool.tensor_tensor(heads(xw[:, t, :]), heads(xs[:, t, G]), per_head(tok[:, 2, t, 8:16]),
                                                 ALU.mult)
                    ins.then_inc(xw_ready, 1)
                for t in range(T):
                    pool.tensor_tensor(heads(Y1[:, t, G]), heads(xs[:, t, G]), per_head(col("dskip", 8 * g, 8)),
                                       ALU.mult).then_inc(skip, 1)
            pool.wait_ge(z_done, 8)
            for g in range(2):
                G = slice(g * 512, (g + 1) * 512)
                for t in range(2 * g, T):
                    pool.wait_ge(y_add, T * g + t + 1)
                    pool.tensor_tensor(Y1[:, t, G], Y1[:, t, G], zs[:, t, G], ALU.mult).then_inc(y_done, 1)
            pool.wait_ge(ys_ms, 1)
            pool.tensor_tensor(small[:, 40:48], small[:, 32:40], small[:, 48:56], ALU.pow).then_inc(ys_rs, 1)
            pool.wait_ge(bc_mm, 16)
            pool.memset(sel[0:64, :, :].bitcast(F32), 0.0).then_inc(sel_z, 1)
            pool_norm(pool, 1)
            POOL_B2(pool)

        block_cm.__exit__(None, None, None)


def _columns(inputs):
    f = lambda n: np.asarray(inputs[n], np.float32)
    out = np.zeros((P, NCST), np.float32)

    def put(name, a):
        c0, n = COLS[name]
        out[:a.shape[0], c0:c0 + n] = a

    def chunks(a):
        return a.reshape(-1, P).T

    def twice(a):
        return np.concatenate([a, a])[:, None]

    put("nmix", chunks(f("norm_mix_w")[0]))
    put("nffn", chunks(f("norm_ffn_w")[0]))
    put("nmix2", chunks(f("mix_norm_g_2")[0]))
    put("nffn2", chunks(f("ffn_norm_g_2")[0]))
    put("nple", chunks(f("ple_gate_norm_g_2")[0]))
    put("nssd", chunks(f("ssd_norm_w")[0]))
    put("cw", f("ssd_conv_w")[0].reshape(4, 12, P).transpose(2, 1, 0).reshape(P, 48))
    put("cb", chunks(f("ssd_conv_b")[0]))
    put("fw", f("ffn_conv_w")[0].reshape(3, 44, P).transpose(2, 1, 0).reshape(P, 132))
    put("fb", chunks(f("ffn_conv_b")[0]))
    put("qw", twice(f("fox_q_norm_w")[0]))
    put("kw", twice(f("fox_k_norm_w")[0]))
    put("sqw", twice(f("q_norm_g_2")[0]))
    put("skw", twice(f("k_norm_g_2")[0]))
    c = {n: COLS[n][0] for n in COLS}
    for r in (0, 32):
        out[r:r + H1, c["dtb"]] = f("ssd_dt_bias")[0]
        out[r:r + H1, c["sgn"]] = 1
        out[r:r + H1, c["alog"]] = f("ssd_a_log")[0]
        out[r:r + H1, c["asg"]] = -1
        out[64 + r:64 + r + H1, c["dtb"]] = f("fox_f_bias")[0]
        out[64 + r:64 + r + H1, c["sgn"]] = -1
        out[64 + r:64 + r + H1, c["asg"]] = 1
    put("dskip", np.broadcast_to(f("ssd_d")[0], (P, H1)))
    put("gng", chunks(f("ret_gn_g_2")[0]))
    put("gnb", chunks(f("ret_gn_b_2")[0]))
    put("sink", np.broadcast_to(f("attn_sinks_2")[0], (P, SH)))
    j = np.arange(P)
    put("zeta", np.exp((P - 1.0 - j)[:, None] * LOG_GAMMA[None, :]) * P ** -0.5)
    return out


def _units(inputs):
    f = lambda n: np.asarray(inputs[n], np.float32)[0]
    w = np.zeros((NU - XU, P, 512), np.float32)

    def put(name, cols):
        kk = cols.shape[0] // P
        u = FIRST[name] - (XU if FIRST[name] > MOE_AT else 0)
        w[u:u + kk, :, :cols.shape[1]] = cols.reshape(kk, P, -1)

    w_in = f("w_in")
    z, xbc, dt, q, k, v, fg = np.split(w_in, [1024, 2560, 2576, 3600, 4624, 5648], axis=1)
    for n, a in (("z", z), ("xbc", xbc), ("q", q), ("k", k), ("v", v)):
        for b in range(a.shape[1] // 512):
            put(f"{n}{b}", a[:, b * 512:(b + 1) * 512])
    for u in range(2):
        for j in range(4):
            rows = slice((4 * u + j) * P, (4 * u + j + 1) * P)
            o = w[FIRST["dtf"] + u, :, j * P:(j + 1) * P]
            for c, a in ((0, dt), (32, dt), (64, fg), (96, fg)):
                o[:, c:c + H1] = a[rows]
    wo = f("w_out")
    up, down = f("w_up"), f("w_down")
    for b in range(2):
        put(f"out{b}", wo[:, b * 512:(b + 1) * 512])
        put(f"down{b}", down[:, b * 512:(b + 1) * 512])
    for b in range(FF // 256):
        put(f"up{b}", np.concatenate([up[:, b * 256:(b + 1) * 256], up[:, FF + b * 256:FF + (b + 1) * 256]], axis=1))
    w2 = f("w_in_2")
    for i, n in enumerate(("rq", "rk", "rv", "rg", "sq")):
        put(n, w2[:, i * 512:(i + 1) * 512])
    skv = w2[:, 2560:2816].reshape(4, 2, P, 256)
    w[FIRST["skv"]:FIRST["skv"] + 4] = skv.transpose(0, 2, 1, 3).reshape(4, P, 512)
    for i, n in enumerate(("gr0", "gr1", "gs0", "gs1")):
        put(n, w2[:, 2816 + i * 512:2816 + (i + 1) * 512])
    for b in range(2):
        for n, a in (("ro", "w_ret_o_2"), ("so", "w_swa_o_2"), ("mo", "w_out_2"), ("ple", "w_ple_2"), ("pg", "w_ple_gate_2")):
            put(f"{n}{b}", f(a)[:, b * 512:(b + 1) * 512])
    r = np.concatenate([f("w_router_group_2"), f("w_router_expert_2")], axis=1).reshape(DC, P, 36)
    w[FIRST["wr"], :, :DC * 36] = r.transpose(1, 0, 2).reshape(P, DC * 36)
    return w


def _experts(inputs):
    f = lambda n: np.asarray(inputs[n], np.float32)[0]
    w = np.empty((NE, 12, P, 512), np.float32)
    w[:, :8, :, :EF] = f("w_exp_gate_2").reshape(NE, 8, P, EF)
    w[:, :8, :, EF:] = f("w_exp_up_2").reshape(NE, 8, P, EF)
    w[:, 8:] = f("w_exp_down_2").reshape(NE, 2, P, 2, 512).transpose(0, 3, 1, 2, 4).reshape(NE, 4, P, 512)
    return w


def _arrays(inputs):
    bf16 = mybir.dt.np(BF16)

    f = lambda n: np.asarray(inputs[n], np.float32)
    j, i = np.arange(P)[:, None], np.arange(P)[None, :]
    diff = (i - j).astype(np.float64)
    dm = np.where((diff >= 0)[:, None, :], np.exp(np.maximum(diff, 0)[:, None, :] * LOG_GAMMA[None, :, None]), 0.0) * P ** -0.5
    xi = np.broadcast_to(np.exp((np.arange(P) + 1.0)[None, :] * LOG_GAMMA[:, None])[None], (P, RH, P))
    mats = np.stack([dm, xi], axis=1).astype(np.float32)
    rel = np.arange(P)[:, None] + P - np.arange(2 * P)[None, :]
    slopes = np.exp2(-8.0 * np.arange(1, SH + 1) / SH)
    bias = np.where(((rel >= 0) & (rel < P))[:, None, :], -slopes[None, :, None] * rel[:, None, :].astype(np.float64), NEG)
    rb = np.zeros((P, 76 + 2 * P), np.float32)
    rb[:, 76:] = np.arange(2 * P)
    rb[:, 0:4] = f("b_router_group_2")[0]
    rb[:, 4:36] = f("b_router_expert_2")[0]
    rb[:, 36:44] = 8 - np.arange(8)
    rb[:, 44:76] = np.arange(32)
    tri = np.stack([(j < i), np.ones((P, P), bool)], axis=1)
    return {
        "x": f("x")[0], "cst": _columns(inputs),
        "rows": np.stack([np.broadcast_to(f("ffn_norm_g_2")[0], (P, D)), np.broadcast_to(f("ple_norm_g_2")[0], (P, D))]),
        "mats": mats, "bias": bias.astype(np.float32), "ident": np.eye(P, dtype=np.float32),
        "identb": np.eye(P).astype(bf16),
        "maskT": np.where(j > i, NEG, 0.0).astype(bf16),
        "maskL": np.where(i > j, NEG, 0.0).astype(bf16),
        "sel": np.broadcast_to((np.arange(P) % 32)[:, None, None] == np.arange(H1)[None, :, None], (P, H1, P)).astype(np.float32),
        "rb": rb, "tri": tri.astype(bf16),
        "pT": np.ascontiguousarray(f("p_2")[0, 0].T).reshape(2, P, S).transpose(1, 0, 2),
        "wstream": _units(inputs), "wexp": _experts(inputs),
    }


def kernel(**inputs):
    import concourse.bacc as _bacc
    from concourse.bass_utils import run_bass_kernel_spmd as _run

    nc = _bacc.Bacc("TRN2", target_bir_lowering=False, num_devices=1)
    arrays, args = {}, []
    for name, a in _arrays(inputs).items():
        a = np.ascontiguousarray(a)
        arrays[f"in_{name}"] = a
        args.append(nc.dram_tensor(f"in_{name}", a.shape, mybir.dt.from_np(a.dtype), kind="ExternalInput").ap())
    args.append(nc.dram_tensor("out_dram", (S, D), F32, kind="ExternalOutput").ap())
    bass_two_blocks(nc, *args)
    r = _run(nc, [arrays], core_ids=[0])
    return r.results[0]["out_dram"].reshape(1, S, D)
```
